# Optimizing a Trainium2 kernel written in Bass

```python
import math
import jax, jax.numpy as jnp
from jax import lax
import numpy as np

D_MODEL = 1024
BATCH = 1
SEQ = 256
DEPTH = 2

CTX_LEN = 256
GRID_W = 64
HEAD_DIM = 64
ROPE_BASE = 10000.0
EPS = 1e-6
CHUNK = 128
D_RET = D_MODEL // 2
D_MLSTM = D_MODEL // 2
H_RET = D_RET // HEAD_DIM
H_MLSTM = D_MLSTM // HEAD_DIM
CONV_W = 3
AB_IN = 4 * D_RET + 4 * D_MLSTM + 4 * H_MLSTM
AB_SPLITS = tuple(int(s) for s in np.cumsum([D_RET] * 4 + [D_MLSTM] * 4))
H_ATTN = D_MODEL // HEAD_DIM
H_KV = 4
GQA_G = H_ATTN // H_KV
WINDOW = 128
BLK = 128
ATTN_IN = D_MODEL + 2 * H_KV * HEAD_DIM
D_FF = ((8 * D_MODEL // 3 + 255) // 256) * 256


def _rmsnorm(x, w):
    xf = x.astype(jnp.float32)
    y = xf * lax.rsqrt(jnp.mean(xf * xf, axis=-1, keepdims=True) + EPS)
    return (y * w.astype(jnp.float32)).astype(x.dtype)

def _heads(x, h):
    return x.reshape(x.shape[0], x.shape[1], h, -1)

def _head_major(a):
    return jnp.transpose(a, (0, 2, 1, 3)).astype(jnp.float32)

def _axial_rope(L, dtype):
    rows = L // GRID_W
    row = jnp.repeat(jnp.arange(rows, dtype=jnp.float32), GRID_W)
    col = jnp.tile(jnp.arange(GRID_W, dtype=jnp.float32), rows)
    n = HEAD_DIM // 4
    inv = ROPE_BASE ** (-jnp.arange(n, dtype=jnp.float32) / n)
    ang = jnp.concatenate([row[:, None] * inv, col[:, None] * inv], axis=-1)
    return jnp.cos(ang).astype(dtype), jnp.sin(ang).astype(dtype)

def _apply_rope(x, cos, sin):
    half = x.shape[-1] // 2
    x1, x2 = x[..., :half], x[..., half:]
    c = cos[None, :, None, :]
    s = sin[None, :, None, :]
    return jnp.concatenate([x1 * c - x2 * s, x2 * c + x1 * s], axis=-1)

def _short_conv(x, w, b):
    L = x.shape[1]
    p = CONV_W // 2
    xp = jnp.pad(x, ((0, 0), (p, p), (0, 0)))
    y = b
    for j in range(CONV_W):
        y = y + w[j] * xp[:, j:j + L]
    return y

def _swiglu(h, w_in, w_out):
    g, u = jnp.split(h @ w_in, 2, axis=-1)
    return (jax.nn.silu(g) * u) @ w_out

def _retention_chunked(q, k, v, log_g, s0):
    B, H, L, dk = q.shape
    n = L // CHUNK
    k = k * dk ** -0.5
    qc = q.reshape(B, H, n, CHUNK, dk)
    kc = k.reshape(B, H, n, CHUNK, dk)
    vc = v.reshape(B, H, n, CHUNK, -1)
    pos = jnp.arange(CHUNK, dtype=jnp.float32)
    diff = pos[:, None] - pos[None, :]
    decay = jnp.where(diff >= 0, jnp.exp(log_g[:, None, None] * jnp.maximum(diff, 0.0)), 0.0)
    scores = jnp.einsum('bhnid,bhnjd->bhnij', qc, kc) * decay[None, :, None]
    intra = jnp.einsum('bhnij,bhnje->bhnie', scores, vc)
    k_dec = jnp.exp(log_g[:, None] * (CHUNK - 1.0 - pos))
    kv_local = jnp.einsum('bhnjd,hj,bhnje->nbhde', kc, k_dec, vc)
    chunk_decay = jnp.exp(log_g * CHUNK)[None, :, None, None]

    def step(s, kv):
        return chunk_decay * s + kv, s

    s_fin, s_prev = lax.scan(step, s0, kv_local)
    q_dec = jnp.exp(log_g[:, None] * (pos + 1.0))
    inter = jnp.einsum('bhnid,hi,nbhde->bhnie', qc, q_dec, s_prev)
    return (intra + inter).reshape(B, H, L, -1), s_fin

def _mlstm_chunked(q, k, v, i_pre, f_pre, state):
    B, H, L, d = q.shape
    n = L // CHUNK
    k = k * d ** -0.5
    qc = q.reshape(B, H, n, CHUNK, d)
    kc = k.reshape(B, H, n, CHUNK, d)
    vc = v.reshape(B, H, n, CHUNK, d)
    ic = i_pre.reshape(B, H, n, CHUNK)
    b = jnp.cumsum(jax.nn.log_sigmoid(f_pre).reshape(B, H, n, CHUNK), axis=-1)
    b_end = b[..., -1]
    causal = jnp.tril(jnp.ones((CHUNK, CHUNK), dtype=bool))
    d_log = jnp.where(causal, b[..., :, None] - b[..., None, :] + ic[..., None, :], -jnp.inf)
    g_end = b_end[..., None] - b + ic
    g_max = jnp.max(g_end, axis=-1)
    w_end = jnp.exp(g_end - g_max[..., None])
    kv_local = jnp.einsum('bhns,bhnsd,bhnse->nbhde', w_end, kc, vc)
    n_local = jnp.einsum('bhns,bhnsd->nbhd', w_end, kc)

    def step(carry, xs):
        c_mat, n_vec, m = carry
        kv, nl, gm, be = xs
        m_new = jnp.maximum(be + m, gm)
        a = jnp.exp(be + m - m_new)
        bb = jnp.exp(gm - m_new)
        c_new = a[..., None, None] * c_mat + bb[..., None, None] * kv
        n_new = a[..., None] * n_vec + bb[..., None] * nl
        return (c_new, n_new, m_new), (c_mat, n_vec, m)

    xs = (kv_local, n_local, jnp.moveaxis(g_max, 2, 0), jnp.moveaxis(b_end, 2, 0))
    final, (c_prev, n_prev, m_prev) = lax.scan(step, state, xs)
    m_prev = jnp.moveaxis(m_prev, 0, 2)
    a_log = b + m_prev[..., None]
    m_t = jnp.maximum(a_log, jnp.max(d_log, axis=-1))
    w = jnp.exp(d_log - m_t[..., None])
    a = jnp.exp(a_log - m_t)
    s = jnp.einsum('bhntd,bhnsd->bhnts', qc, kc) * w
    num = jnp.einsum('bhnts,bhnse->bhnte', s, vc) + a[..., None] * jnp.einsum('bhntd,nbhde->bhnte', qc, c_prev)
    den = jnp.sum(s, axis=-1) + a * jnp.einsum('bhntd,nbhd->bhnt', qc, n_prev)
    h = num / jnp.maximum(jnp.abs(den), jnp.exp(-m_t))[..., None]
    return h.reshape(B, H, L, d), final

def _sink_softmax(scores, sink):
    snk = sink[:, :, None]
    m = snk
    for s in scores:
        m = jnp.maximum(m, jnp.max(s, axis=-1))
    ex = [jnp.exp(s - m[..., None]) for s in scores]
    denom = jnp.exp(snk - m)
    for e in ex:
        denom = denom + jnp.sum(e, axis=-1)
    return [e / denom[..., None] for e in ex]

def _ret_mlstm_mixer(h, hc, rope, w_in, w_out, ret_log_gamma, ret_norm_w,
                     conv_w, conv_b, gate_b, mlstm_norm_w):
    f32 = jnp.float32
    B = h.shape[0]

    def prep(t, use_rope):
        rq, rk, rv, rg, mq, mk, mv, mo, mg = jnp.split(t @ w_in, AB_SPLITS, axis=-1)
        rq, rk, rv = _heads(rq, H_RET), _heads(rk, H_RET), _heads(rv, H_RET)
        if use_rope:
            rq, rk = rope(rq), rope(rk)
        mqk = jax.nn.silu(_short_conv(jnp.concatenate([mq, mk], axis=-1), conv_w, conv_b))
        mq, mk = jnp.split(mqk, 2, axis=-1)
        gates = (mg.astype(f32).reshape(t.shape[0], t.shape[1], 4, H_MLSTM)
                 + gate_b.astype(f32)).transpose(2, 0, 3, 1)
        ret = tuple(_head_major(a) for a in (rq, rk, rv))
        mls = tuple(_head_major(_heads(a, H_MLSTM)) for a in (mq, mk, mv))
        return ret, mls, gates, rg, mo

    ret_l, mls_l, gates_l, rg_l, mo_l = prep(h, True)
    ret_c, mls_c, gates_c, rg_c, mo_c = prep(hc, False)
    flip = lambda t: jnp.flip(t, axis=2)
    lg = ret_log_gamma.astype(f32)
    s0_r = jnp.zeros((B, H_RET, HEAD_DIM, HEAD_DIM), f32)
    s0_m = (jnp.zeros((B, H_MLSTM, HEAD_DIM, HEAD_DIM), f32),
            jnp.zeros((B, H_MLSTM, HEAD_DIM), f32),
            jnp.zeros((B, H_MLSTM), f32))

    def ret_dir(direction, ctx_args, lat_args):
        yc, s = _retention_chunked(*ctx_args, lg[direction], s0_r)
        yl, _ = _retention_chunked(*lat_args, lg[direction], s)
        return yc, yl

    def mls_dir(ctx_args, lat_args):
        yc, s = _mlstm_chunked(*ctx_args, s0_m)
        yl, _ = _mlstm_chunked(*lat_args, s)
        return yc, yl

    rc_f, rl_f = ret_dir(0, ret_c, ret_l)
    rc_b, rl_b = ret_dir(1, tuple(map(flip, ret_c)), tuple(map(flip, ret_l)))
    mc_f, ml_f = mls_dir((*mls_c, gates_c[0], gates_c[1]), (*mls_l, gates_l[0], gates_l[1]))
    mc_b, ml_b = mls_dir(tuple(map(flip, (*mls_c, gates_c[2], gates_c[3]))),
                         tuple(map(flip, (*mls_l, gates_l[2], gates_l[3]))))

    def merge(r, m, rg, mo, dtype):
        r = _rmsnorm(jnp.transpose(r, (0, 2, 1, 3)), ret_norm_w.reshape(H_RET, HEAD_DIM)).astype(dtype)
        r = r.reshape(r.shape[0], r.shape[1], D_RET) * jax.nn.silu(rg)
        m = _rmsnorm(jnp.transpose(m, (0, 2, 1, 3)), mlstm_norm_w.reshape(H_MLSTM, HEAD_DIM)).astype(dtype)
        m = m.reshape(m.shape[0], m.shape[1], D_MLSTM) * jax.nn.sigmoid(mo)
        return jnp.concatenate([r, m], axis=-1) @ w_out

    y_lat = merge(rl_f + flip(rl_b), ml_f + flip(ml_b), rg_l, mo_l, h.dtype)
    y_ctx = merge(rc_f + flip(rc_b), mc_f + flip(mc_b), rg_c, mo_c, hc.dtype)
    return y_lat, y_ctx

def _window_attn_mixer(h, hc, rope, w_in, w_out, q_norm_w, k_norm_w, sink, need_ctx_out):
    f32 = jnp.float32
    B, L, _ = h.shape
    nb = L // BLK
    scale = HEAD_DIM ** -0.5

    def prep(t):
        q, k, v = jnp.split(t @ w_in, [D_MODEL, D_MODEL + H_KV * HEAD_DIM], axis=-1)
        return (_rmsnorm(_heads(q, H_ATTN), q_norm_w), _rmsnorm(_heads(k, H_KV), k_norm_w), _heads(v, H_KV))

    q, k, v = prep(h)
    q, k = rope(q), rope(k)
    qc, kc, vc = prep(hc)
    snk = sink.astype(f32).reshape(H_KV, GQA_G)

    qb = q.reshape(B, nb, BLK, H_KV, GQA_G, HEAD_DIM)

    def band(t):
        tp = jnp.pad(t, ((0, 0), (BLK, BLK), (0, 0), (0, 0))).reshape(B, nb + 2, BLK, H_KV, HEAD_DIM)
        return jnp.concatenate([tp[:, :-2], tp[:, 1:-1], tp[:, 2:]], axis=2)

    kw, vw = band(k), band(v)
    s_win = jnp.einsum('bnqhgd,bnkhd->bnhgqk', qb, kw).astype(f32) * scale
    blk = jnp.arange(nb)[:, None, None]
    qpos = blk * BLK + jnp.arange(BLK)[None, :, None]
    kpos = (blk - 1) * BLK + jnp.arange(3 * BLK)[None, None, :]
    valid = (jnp.abs(qpos - kpos) <= WINDOW) & (kpos >= 0) & (kpos < L)
    s_win = jnp.where(valid[None, :, None, None], s_win, -jnp.inf)
    s_ctx = jnp.einsum('bnqhgd,bkhd->bnhgqk', qb, kc).astype(f32) * scale
    p_win, p_ctx = _sink_softmax([s_win, s_ctx], snk)
    o = (jnp.einsum('bnhgqk,bnkhd->bnqhgd', p_win.astype(v.dtype), vw)
         + jnp.einsum('bnhgqk,bkhd->bnqhgd', p_ctx.astype(vc.dtype), vc))
    y = o.reshape(B, L, D_MODEL) @ w_out
    if not need_ctx_out:
        return y, None
    Lc = hc.shape[1]
    qcg = qc.reshape(B, Lc, H_KV, GQA_G, HEAD_DIM)
    s_cc = jnp.einsum('bqhgd,bkhd->bhgqk', qcg, kc).astype(f32) * scale
    (p_cc,) = _sink_softmax([s_cc], snk)
    oc = jnp.einsum('bhgqk,bkhd->bqhgd', p_cc.astype(vc.dtype), vc).reshape(B, Lc, D_MODEL) @ w_out
    return y, oc

def first_inputs(seed: int = 0) -> dict:
    key = jax.random.key(seed)
    ks = jax.random.split(key, 24)
    f32 = jnp.float32
    n_even = (DEPTH + 1) // 2
    n_odd = DEPTH // 2
    D = D_MODEL

    def nrm(k, shape, scale):
        return jax.random.normal(k, shape, f32) * scale

    base_lg = jnp.log1p(-jnp.exp2(-5.0 - jnp.arange(H_RET, dtype=f32)))
    fb = jnp.linspace(3.0, 6.0, H_MLSTM, dtype=f32)
    zb = jnp.zeros((H_MLSTM,), f32)
    gate_base = jnp.stack([zb, fb, zb, fb])
    return {
        'x': nrm(ks[0], (BATCH, SEQ, D), 1.0),
        'c': nrm(ks[1], (BATCH, D), 1.0),
        'ctx': nrm(ks[2], (BATCH, CTX_LEN, D), 1.0),
        'c_ctx': nrm(ks[3], (D,), 1.0),
        'ada_w': nrm(ks[4], (DEPTH, D, 6 * D), 0.5 * D ** -0.5),
        'ada_b': nrm(ks[5], (DEPTH, 6 * D), 0.02),
        'norm_w': 1.0 + nrm(ks[6], (DEPTH, 2, D), 0.02),
        'ffn_w_in': nrm(ks[7], (DEPTH, D, 2 * D_FF), D ** -0.5),
        'ffn_w_out': nrm(ks[8], (DEPTH, D_FF, D), D_FF ** -0.5),
        'ab_w_in': nrm(ks[9], (n_even, D, AB_IN), D ** -0.5),
        'ab_w_out': nrm(ks[10], (n_even, D_RET + D_MLSTM, D), (D_RET + D_MLSTM) ** -0.5),
        'ret_log_gamma': base_lg * (1.0 + nrm(ks[11], (n_even, 2, H_RET), 0.05)),
        'ret_norm_w': 1.0 + nrm(ks[12], (n_even, D_RET), 0.02),
        'mlstm_conv_w': nrm(ks[13], (n_even, CONV_W, 2 * D_MLSTM), CONV_W ** -0.5),
        'mlstm_conv_b': nrm(ks[14], (n_even, 2 * D_MLSTM), 0.02),
        'mlstm_gate_b': gate_base + nrm(ks[15], (n_even, 4, H_MLSTM), 0.1),
        'mlstm_norm_w': 1.0 + nrm(ks[16], (n_even, D_MLSTM), 0.02),
        'attn_w_in': nrm(ks[17], (n_odd, D, ATTN_IN), D ** -0.5),
        'attn_w_out': nrm(ks[18], (n_odd, D, D), D ** -0.5),
        'attn_q_norm_w': 1.0 + nrm(ks[19], (n_odd, HEAD_DIM), 0.02),
        'attn_k_norm_w': 1.0 + nrm(ks[20], (n_odd, HEAD_DIM), 0.02),
        'attn_sink': nrm(ks[21], (n_odd, H_ATTN), 0.5),
    }

def first_block(x, c, ctx, c_ctx, ada_w, ada_b, norm_w, ffn_w_in, ffn_w_out, ab_w_in, ab_w_out,
              ret_log_gamma, ret_norm_w, mlstm_conv_w, mlstm_conv_b, mlstm_gate_b, mlstm_norm_w,
              attn_w_in, attn_w_out, attn_q_norm_w, attn_k_norm_w, attn_sink):
    L = x.shape[1]
    cos, sin = _axial_rope(L, x.dtype)
    rope = lambda t: _apply_rope(t, cos, sin)
    silu_c = jax.nn.silu(c)
    silu_cc = jax.nn.silu(c_ctx)
    for layer in range(DEPTH):
        last = layer == DEPTH - 1
        mod = (silu_c @ ada_w[layer] + ada_b[layer])[:, None, :]
        mod_c = (silu_cc @ ada_w[layer] + ada_b[layer])[None, None, :]
        sh1, sc1, g1, sh2, sc2, g2 = jnp.split(mod, 6, axis=-1)
        csh1, csc1, cg1, csh2, csc2, cg2 = jnp.split(mod_c, 6, axis=-1)
        h = _rmsnorm(x, norm_w[layer, 0]) * (1.0 + sc1) + sh1
        hc = _rmsnorm(ctx, norm_w[layer, 0]) * (1.0 + csc1) + csh1
        if layer % 2 == 0:
            e = layer // 2
            y, yc = _ret_mlstm_mixer(h, hc, rope, ab_w_in[e], ab_w_out[e], ret_log_gamma[e], ret_norm_w[e],
                                     mlstm_conv_w[e], mlstm_conv_b[e], mlstm_gate_b[e], mlstm_norm_w[e])
        else:
            o = layer // 2
            y, yc = _window_attn_mixer(h, hc, rope, attn_w_in[o], attn_w_out[o], attn_q_norm_w[o],
                                       attn_k_norm_w[o], attn_sink[o], not last)
        x = x + g1 * y
        x = x + g2 * _swiglu(_rmsnorm(x, norm_w[layer, 1]) * (1.0 + sc2) + sh2, ffn_w_in[layer], ffn_w_out[layer])
        if not last:
            ctx = ctx + cg1 * yc
            ctx = ctx + cg2 * _swiglu(_rmsnorm(ctx, norm_w[layer, 1]) * (1.0 + csc2) + csh2,
                                      ffn_w_in[layer], ffn_w_out[layer])
    return x


N_MIXERS = 2
N_LAYERS_A = (DEPTH + 1) // 2
N_LAYERS_B = DEPTH // 2
N_MOD = 6

MLA_HEADS = 16
Q_LORA = 512
KV_LORA = 256
QK_NOPE = 64
QK_ROPE = 32
V_HEAD = 64
ROPE_THETA = 10000.0
Q_BLOCK = 128
MASK_VALUE = -1e30

GDN_HEADS = 8
GDN_DK = 128
GDN_DV = 128
CONV_K = 4
CHUNK_2 = 64

D_FF_2 = 2816
N_EXPERTS = 8
TOP_K = 2
D_FF_EXPERT = 1408

MLA_IN = Q_LORA + KV_LORA + QK_ROPE
GDN_QKV = 2 * GDN_HEADS * GDN_DK + GDN_HEADS * GDN_DV
GDN_IN = GDN_QKV + GDN_HEADS * GDN_DV + 2 * GDN_HEADS


def rms_norm(x, g):
    xf = x.astype(jnp.float32)
    y = xf * lax.rsqrt(jnp.mean(xf * xf, axis=-1, keepdims=True) + EPS)
    return (y * g.astype(jnp.float32)).astype(x.dtype)

def l2_norm(x):
    xf = x.astype(jnp.float32)
    return xf * lax.rsqrt(jnp.sum(xf * xf, axis=-1, keepdims=True) + EPS)

def apply_rope(x, pos):
    half = QK_ROPE // 2
    inv_freq = ROPE_THETA ** (-jnp.arange(half, dtype=jnp.float32) / half)
    ang = pos.astype(jnp.float32)[:, :, None, None] * inv_freq
    cos, sin = jnp.cos(ang), jnp.sin(ang)
    xf = x.astype(jnp.float32)
    x1, x2 = xf[..., :half], xf[..., half:]
    out = jnp.concatenate([x1 * cos - x2 * sin, x2 * cos + x1 * sin], axis=-1)
    return out.astype(x.dtype)

def mla_mixer(h, pos, w_in, q_norm, w_qb, kv_norm, w_kvb, w_out):
    B, S, _ = h.shape
    H = MLA_HEADS
    proj = h @ w_in
    q_lat, kv_lat, k_rope = jnp.split(proj, [Q_LORA, Q_LORA + KV_LORA], axis=-1)
    q = (rms_norm(q_lat, q_norm) @ w_qb).reshape(B, S, H, QK_NOPE + QK_ROPE)
    q_nope = q[..., :QK_NOPE]
    q_rope = apply_rope(q[..., QK_NOPE:], pos)
    kv = (rms_norm(kv_lat, kv_norm) @ w_kvb).reshape(B, S, H, QK_NOPE + V_HEAD)
    k_nope, v = kv[..., :QK_NOPE], kv[..., QK_NOPE:]
    k_rope = apply_rope(k_rope[:, :, None, :], pos)[:, :, 0, :]
    scale = (QK_NOPE + QK_ROPE) ** -0.5
    n_blk = S // Q_BLOCK
    qn_b = q_nope.reshape(B, n_blk, Q_BLOCK, H, QK_NOPE).transpose(1, 0, 2, 3, 4)
    qr_b = q_rope.reshape(B, n_blk, Q_BLOCK, H, QK_ROPE).transpose(1, 0, 2, 3, 4)
    key_idx = jnp.arange(S)

    def attend(args):
        blk, qn, qr = args
        s = (jnp.einsum('bqhd,bkhd->bhqk', qn, k_nope)
             + jnp.einsum('bqhr,bkr->bhqk', qr, k_rope)).astype(jnp.float32) * scale
        q_idx = blk * Q_BLOCK + jnp.arange(Q_BLOCK)
        causal = key_idx[None, :] <= q_idx[:, None]
        s = jnp.where(causal, s, MASK_VALUE)
        p = jax.nn.softmax(s, axis=-1).astype(v.dtype)
        return jnp.einsum('bhqk,bkhd->bqhd', p, v)

    o = lax.map(attend, (jnp.arange(n_blk), qn_b, qr_b))
    o = o.transpose(1, 0, 2, 3, 4).reshape(B, S, H * V_HEAD)
    return o @ w_out

def causal_conv(x, w):
    C = x.shape[-1]
    return lax.conv_general_dilated(
        x, w[:, None, :].astype(x.dtype), window_strides=(1,),
        padding=[(CONV_K - 1, 0)], dimension_numbers=('NWC', 'WIO', 'NWC'),
        feature_group_count=C)

def chunk_gated_delta(q, k, v, g, beta):
    B, S, H, DK = q.shape
    DV = v.shape[-1]
    N = S // CHUNK_2

    def to_chunks(t):
        return t.astype(jnp.float32).reshape(B, N, CHUNK_2, H, -1).transpose(0, 3, 1, 2, 4)

    q, k, v = to_chunks(q), to_chunks(k), to_chunks(v)
    beta = beta.astype(jnp.float32).reshape(B, N, CHUNK_2, H).transpose(0, 3, 1, 2)
    g = g.astype(jnp.float32).reshape(B, N, CHUNK_2, H).transpose(0, 3, 1, 2)
    gc = jnp.cumsum(g, axis=-1)
    causal = jnp.tril(jnp.ones((CHUNK_2, CHUNK_2), dtype=bool))
    strict = jnp.tril(jnp.ones((CHUNK_2, CHUNK_2), dtype=bool), -1)
    diff = gc[..., :, None] - gc[..., None, :]
    decay = jnp.where(causal, jnp.exp(jnp.where(causal, diff, 0.0)), 0.0)
    k_beta = k * beta[..., None]
    a_mat = jnp.where(strict, jnp.einsum('bhnid,bhnjd->bhnij', k_beta, k) * decay, 0.0)
    t_mat = a_mat + jnp.eye(CHUNK_2, dtype=jnp.float32)
    rhs = jnp.concatenate([v * beta[..., None], k_beta * jnp.exp(gc)[..., None]], axis=-1)
    sol = lax.linalg.triangular_solve(t_mat, rhs, left_side=True, lower=True,
                                      unit_diagonal=True)
    u, w = sol[..., :DV], sol[..., DV:]
    attn_intra = jnp.where(causal, jnp.einsum('bhnid,bhnjd->bhnij', q, k) * decay, 0.0)
    q_dec = q * jnp.exp(gc)[..., None]
    g_last = gc[..., -1]
    k_state = k * jnp.exp(g_last[..., None] - gc)[..., None]
    chunk_decay = jnp.exp(g_last)

    def step(state, xs):
        u_c, w_c, qd_c, at_c, ks_c, dec_c = xs
        v_new = u_c - w_c @ state
        o_c = qd_c @ state + at_c @ v_new
        state = state * dec_c[..., None, None] + jnp.einsum('bhcd,bhce->bhde', ks_c, v_new)
        return state, o_c

    xs = (jnp.moveaxis(u, 2, 0), jnp.moveaxis(w, 2, 0), jnp.moveaxis(q_dec, 2, 0),
          jnp.moveaxis(attn_intra, 2, 0), jnp.moveaxis(k_state, 2, 0),
          jnp.moveaxis(chunk_decay, 2, 0))
    s0 = jnp.zeros((B, H, DK, DV), jnp.float32)
    _, o = lax.scan(step, s0, xs)
    return o.transpose(1, 0, 3, 2, 4).reshape(B, S, H, DV)

def gdn_mixer(h, w_in, conv_w, a_log, dt_bias, out_norm, w_out):
    B, S, _ = h.shape
    H = GDN_HEADS
    proj = h @ w_in
    qkv, z, b, a = jnp.split(proj, [GDN_QKV, GDN_QKV + H * GDN_DV, GDN_QKV + H * GDN_DV + H],
                             axis=-1)
    qkv = jax.nn.silu(causal_conv(qkv, conv_w))
    q, k, v = jnp.split(qkv, [H * GDN_DK, 2 * H * GDN_DK], axis=-1)
    q = l2_norm(q.reshape(B, S, H, GDN_DK)) * (GDN_DK ** -0.5)
    k = l2_norm(k.reshape(B, S, H, GDN_DK))
    v = v.reshape(B, S, H, GDN_DV)
    beta = jax.nn.sigmoid(b.astype(jnp.float32))
    g = -jnp.exp(a_log.astype(jnp.float32)) * jax.nn.softplus(
        a.astype(jnp.float32) + dt_bias.astype(jnp.float32))
    o = chunk_gated_delta(q, k, v, g, beta).astype(h.dtype)
    o = rms_norm(o, out_norm) * jax.nn.silu(z.reshape(B, S, H, GDN_DV))
    return o.reshape(B, S, H * GDN_DV) @ w_out

def swiglu_ffn(h, w_gate_up, w_down):
    gt, up = jnp.split(h @ w_gate_up, 2, axis=-1)
    return (jax.nn.silu(gt) * up) @ w_down

def moe_ffn(h, w_router, w_gate_up, w_down):
    B, S, D = h.shape
    t = h.reshape(B * S, D)
    logits = (t @ w_router).astype(jnp.float32)
    top_val, top_idx = lax.top_k(logits, TOP_K)
    top_w = jax.nn.softmax(top_val, axis=-1)
    combine = jnp.sum(jax.nn.one_hot(top_idx, N_EXPERTS, dtype=jnp.float32)
                      * top_w[..., None], axis=1)
    out = jnp.zeros((B * S, D), jnp.float32)
    for e in range(N_EXPERTS):
        y_e = swiglu_ffn(t, w_gate_up[e], w_down[e])
        out = out + combine[:, e:e + 1] * y_e
    return out.reshape(B, S, D).astype(h.dtype)

def second_inputs(seed: int = 0) -> dict:
    key = jax.random.key(seed)
    ks = iter(jax.random.split(key, 40))
    f32 = jnp.float32

    def nrm(shape, fan_in, scale=1.0):
        return jax.random.normal(next(ks), shape, f32) * (scale * fan_in ** -0.5)

    def gain(shape):
        return 1.0 + 0.05 * jax.random.normal(next(ks), shape, f32)

    D = D_MODEL
    A, Bn = N_LAYERS_A, N_LAYERS_B
    x = jax.random.normal(next(ks), (BATCH, SEQ, D), f32)
    c = jax.random.normal(next(ks), (BATCH, D), f32)
    positions = jnp.broadcast_to(jnp.arange(SEQ, dtype=jnp.int32)[None, :], (BATCH, SEQ))
    dt = jnp.exp(jax.random.uniform(next(ks), (Bn, GDN_HEADS), f32,
                                    minval=jnp.log(0.001), maxval=jnp.log(0.1)))
    return {
        'x': x,
        'c': c,
        'positions': positions,
        'ada_w': nrm((DEPTH, D, N_MOD * D), D, 0.5),
        'ada_b': 0.02 * jax.random.normal(next(ks), (DEPTH, N_MOD * D), f32),
        'norm_mix': gain((DEPTH, D)),
        'norm_ffn': gain((DEPTH, D)),
        'mla_w_in': nrm((A, D, MLA_IN), D),
        'mla_q_norm': gain((A, Q_LORA)),
        'mla_w_qb': nrm((A, Q_LORA, MLA_HEADS * (QK_NOPE + QK_ROPE)), Q_LORA),
        'mla_kv_norm': gain((A, KV_LORA)),
        'mla_w_kvb': nrm((A, KV_LORA, MLA_HEADS * (QK_NOPE + V_HEAD)), KV_LORA),
        'mla_w_out': nrm((A, MLA_HEADS * V_HEAD, D), MLA_HEADS * V_HEAD),
        'ffn_w_gate_up': nrm((A, D, 2 * D_FF_2), D),
        'ffn_w_down': nrm((A, D_FF_2, D), D_FF_2),
        'gdn_w_in': nrm((Bn, D, GDN_IN), D),
        'gdn_conv_w': nrm((Bn, CONV_K, GDN_QKV), CONV_K),
        'gdn_a_log': jnp.log(jax.random.uniform(next(ks), (Bn, GDN_HEADS), f32,
                                                minval=1.0, maxval=16.0)),
        'gdn_dt_bias': dt + jnp.log(-jnp.expm1(-dt)),
        'gdn_out_norm': gain((Bn, GDN_DV)),
        'gdn_w_out': nrm((Bn, GDN_HEADS * GDN_DV, D), GDN_HEADS * GDN_DV),
        'moe_w_router': nrm((Bn, D, N_EXPERTS), D),
        'moe_w_gate_up': nrm((Bn, N_EXPERTS, D, 2 * D_FF_EXPERT), D),
        'moe_w_down': nrm((Bn, N_EXPERTS, D_FF_EXPERT, D), D_FF_EXPERT),
        'final_norm': gain((D,)),
    }

def second_block(x, c, positions, ada_w, ada_b, norm_mix, norm_ffn,
              mla_w_in, mla_q_norm, mla_w_qb, mla_kv_norm, mla_w_kvb, mla_w_out,
              ffn_w_gate_up, ffn_w_down,
              gdn_w_in, gdn_conv_w, gdn_a_log, gdn_dt_bias, gdn_out_norm, gdn_w_out,
              moe_w_router, moe_w_gate_up, moe_w_down, final_norm):
    cond = jax.nn.silu(c)
    for i in range(DEPTH):
        j = i // N_MIXERS
        mod = cond @ ada_w[i] + ada_b[i]
        sh1, sc1, g1, sh2, sc2, g2 = [m[:, None, :] for m in jnp.split(mod, N_MOD, axis=-1)]
        h = rms_norm(x, norm_mix[i]) * (1.0 + sc1) + sh1
        if i % N_MIXERS == 0:
            y = mla_mixer(h, positions, mla_w_in[j], mla_q_norm[j], mla_w_qb[j],
                          mla_kv_norm[j], mla_w_kvb[j], mla_w_out[j])
        else:
            y = gdn_mixer(h, gdn_w_in[j], gdn_conv_w[j], gdn_a_log[j], gdn_dt_bias[j],
                          gdn_out_norm[j], gdn_w_out[j])
        x = x + g1 * y
        h = rms_norm(x, norm_ffn[i]) * (1.0 + sc2) + sh2
        if i % 2 == 0:
            y = swiglu_ffn(h, ffn_w_gate_up[j], ffn_w_down[j])
        else:
            y = moe_ffn(h, moe_w_router[j], moe_w_gate_up[j], moe_w_down[j])
        x = x + g2 * y
    return rms_norm(x, final_norm)


def setup_inputs(seed=0):
    out = dict(first_inputs(seed))
    for name, value in second_inputs(seed + 1).items():
        if name != "x":
            out[name + "_2"] = value
    return out


def reference(
    x, c, ctx, c_ctx, ada_w, ada_b, norm_w, ffn_w_in, ffn_w_out, ab_w_in, ab_w_out,
    ret_log_gamma, ret_norm_w, mlstm_conv_w, mlstm_conv_b, mlstm_gate_b, mlstm_norm_w,
    attn_w_in, attn_w_out, attn_q_norm_w, attn_k_norm_w, attn_sink, c_2, positions_2, ada_w_2,
    ada_b_2, norm_mix_2, norm_ffn_2, mla_w_in_2, mla_q_norm_2, mla_w_qb_2, mla_kv_norm_2,
    mla_w_kvb_2, mla_w_out_2, ffn_w_gate_up_2, ffn_w_down_2, gdn_w_in_2, gdn_conv_w_2,
    gdn_a_log_2, gdn_dt_bias_2, gdn_out_norm_2, gdn_w_out_2, moe_w_router_2, moe_w_gate_up_2,
    moe_w_down_2, final_norm_2,
):
    x = first_block(
        x, c, ctx, c_ctx, ada_w, ada_b, norm_w, ffn_w_in, ffn_w_out, ab_w_in, ab_w_out,
        ret_log_gamma, ret_norm_w, mlstm_conv_w, mlstm_conv_b, mlstm_gate_b, mlstm_norm_w,
        attn_w_in, attn_w_out, attn_q_norm_w, attn_k_norm_w, attn_sink,
    )
    return second_block(
        x, c_2, positions_2, ada_w_2, ada_b_2, norm_mix_2, norm_ffn_2, mla_w_in_2, mla_q_norm_2,
        mla_w_qb_2, mla_kv_norm_2, mla_w_kvb_2, mla_w_out_2, ffn_w_gate_up_2, ffn_w_down_2,
        gdn_w_in_2, gdn_conv_w_2, gdn_a_log_2, gdn_dt_bias_2, gdn_out_norm_2, gdn_w_out_2,
        moe_w_router_2, moe_w_gate_up_2, moe_w_down_2, final_norm_2,
    )


_drawn_inputs = setup_inputs


def setup_inputs(seed=0):
    import zlib

    import numpy as np

    out = dict(_drawn_inputs(seed))
    spreads = {}
    factors = {'norm_w': 3.653,
     'ret_norm_w': 6.27,
     'mlstm_conv_b': 8.0,
     'mlstm_norm_w': 8.0,
     'attn_q_norm_w': 8.0,
     'attn_k_norm_w': 8.0,
     'attn_sink': 8.0,
     'norm_mix_2': 2.932,
     'mla_q_norm_2': 7.936,
     'mla_kv_norm_2': 3.218,
     'gdn_out_norm_2': 10.787,
     'norm_ffn_2': 8.0}
    for name, (base, spread) in spreads.items():
        noise = np.random.default_rng([zlib.crc32(name.encode()), seed]).standard_normal(out[name].shape)
        drawn = base * np.exp(spread * noise) if base else spread * noise
        out[name] = __import__('jax').numpy.asarray(drawn.astype(out[name].dtype))
    for name, factor in factors.items():
        out[name] = (out[name] * factor).astype(out[name].dtype)
    return out
```

```python
from contextlib import ExitStack, contextmanager

import concourse.bass as bass
from concourse import mybir

F32 = mybir.dt.float32
I32 = mybir.dt.int32
ALU = mybir.AluOpType
ACT = mybir.ActivationFunctionType
X = mybir.AxisListType.X

P = 128
D = 1024
KD = D // P
L = 256
T2 = 512
EPS = 1e-6
HD = 64
FF = 2816
KF = FF // P
FE = 1408
KE = FE // P
NE = 8
NSLOT = 4
SLOT = 4096
NEG = -1e30

CONST, _at = {}, 0
for _name, _width in (("ident", P), ("ones", P), ("halves", P), ("rot", P), ("upto", P), ("from", P),
                      ("before", P), ("cos", L), ("sin", L), ("rot32", 32), ("invf", 1), ("earlier", 64)):
    CONST[_name] = (_at, _width)
    _at += _width
NCONST = _at
STRIP = 3 * P
PHASE_A = {n: (i * STRIP, STRIP) for i, n in enumerate(("dist", "ahead", "behind", "is_ahead", "is_behind"))}
NPHASE_A = 5 * STRIP
NPHASE_B = 2 * T2
NPHASE_G = 8 * P
NPHASE = NPHASE_A

PACKS = (
    (("c", 8), ("c_ctx", 8), ("c_2", 8), ("norm_w", 32), ("norm_mix_2", 16), ("norm_ffn_2", 16), ("final_norm_2", 8),
     ("ret_norm_w", 4), ("mlstm_norm_w", 4), ("gdn_out_norm_2", 1), ("mla_q_norm_2", 4), ("mla_kv_norm_2", 2),
     ("attn_q_norm_w", 1), ("attn_k_norm_w", 1)),
    (("ada_b", 96), ("mlstm_conv_w", 24), ("mlstm_conv_b", 8)),
    (("ada_b_2", 96),),
    (("gdn_conv_w_2", 96),),
)


NVEC = sum(len(p) for p in PACKS) + 2
NROW = 6
Q_LORA, KV_LORA = 512, 256
PI = 3.1415925
HALF_PI = 1.5707964
TWO_PI = 6.2831855
TWO_PI_PARTS = (6.28125, 0.0019350051879882812, 3.019916050561733e-07)
NPROJ = {"gdn": 153}


class Count:

    def __init__(self):
        self.n, self.i, self.per = 0, None, 0

    def next(self):
        self.n += 1
        return self.n if self.i is None else self.i * self.per + self.n

    def ahead(self, k):
        return self.n - k if self.i is None else self.i * self.per + (self.n - k)

    def place(self, places):
        assert self.i is None or self.per % places == 0
        return (self.n - 1) % places


@contextmanager
def turns(engine, times, **counts):
    with engine.Fori(0, times) as i:
        before = {}
        for name, (count, per) in counts.items():
            before[name] = count.n
            count.i, count.per = i, per
        yield i
        for name, (count, per) in counts.items():
            assert count.n - before[name] == per, (name, count.n - before[name], per)
            count.n, count.i = before[name] + per * times, None


def build(nc, A, out, stop=99):
    ctx = ExitStack()
    with ctx:
        free = [0]
        total = 53200
        mem = ctx.enter_context(nc.sbuf_tensor("mem", [P, total], F32))

        def room(width):
            free[0] += width
            assert free[0] <= total, free[0]
            return free[0] - width

        def at(start, *shape, rows=(0, P)):
            width = 1
            for s in shape:
                width *= s
            v = mem[rows[0]:rows[1], start:start + width]
            if len(shape) == 2:
                return v.rearrange("p (a b) -> p a b", a=shape[0])
            if len(shape) == 3:
                return v.rearrange("p (a b c) -> p a b c", a=shape[0], b=shape[1])
            if len(shape) == 4:
                return v.rearrange("p (a b c d) -> p a b c d", a=shape[0], b=shape[1], c=shape[2])
            return v

        ring0 = room(NSLOT * SLOT)
        xT = at(room(KD * T2), KD, T2)
        h0 = room(KD * T2 + 64)
        hT = at(h0, KD, T2)
        const0 = room(NCONST)
        phase0 = room(NPHASE)
        pack_cols = at(room(4 * P), 4, P)
        mod = at(room(2 * 48 * 2), 2, 48, 2)
        gain = at(room(16), KD, 2)
        conds = at(room(4 * KD), 4, KD)
        rw = at(room(KD * NE), KD, NE)
        rowvec = at(room(64), 64)
        small = at(room(256), 256)
        lgam = at(room(48), 3, 16)
        rstd = at(room(T2), T2)
        work0 = room(0)
        nwork = total - work0

        def work(start, *shape, rows=(0, P)):
            width = 1
            for s in shape:
                width *= s
            assert start + width <= nwork, (start + width, nwork)
            return at(work0 + start, *shape, rows=rows)

        def const(name, rows=(0, P)):
            a, w = CONST[name]
            return at(const0 + a, w, rows=rows)

        ident = const("ident")

        def pconst(name):
            a, w = PHASE_A[name]
            return at(phase0 + a, w)

        def imask(lev):
            return at(phase0 + lev * P, P)

        def vector_rows():
            for g, pack in enumerate(PACKS):
                r = 0
                for name, n in pack:
                    v = A[name].flatten()
                    yield g, r, (v.rearrange("(r p) -> r p", p=P) if v.shape[0] % P == 0 else
                                 v.rearrange("(r p) -> r p", r=1))
                    r += n

        PS = [ctx.enter_context(nc.psum_tensor(f"bank{i}", [P, 512], F32)) for i in range(8)]

        def slot(s, k, n):
            return at(ring0 + s * SLOT, k, n)

        col_at = {}
        for g, pack in enumerate(PACKS):
            r = 0
            for name, n in pack:
                col_at[name] = (g, r, n)
                r += n

        def col(name, first=0, n=None):
            g, r, m = col_at[name]
            n = m - first if n is None else n
            return pack_cols[:, g, r + first:r + first + n]

        s = {}
        for name in (
            "const_loaded", "vectors_loaded", "x_loaded", "phase_loaded", "rows_loaded", "packs_turned", "packs_copied",
            "cond_ready", "x_turned", "x_copied", "panel_used", "ada_ready", "ada_taken", "gain_ready",
            "square_ready", "sum_ready", "mean_ready", "rstd_ready", "scaled", "h_ready",
            "gu_ready", "silu_ready", "gu_taken", "out_ready", "out_taken", "proj_ready", "proj_taken",
            "dve_step", "act_step", "pool_step",
            "act_for_dve", "dve_for_act", "act_for_pe", "dve_for_pe", "pe_for_dve",
            "score_ready", "score_taken", "max_ready", "exp_ready", "turn_ready", "turn_copied", "o_ready", "o_taken",
            "gates_split", "moved_ready", "moved_taken", "picks_ready", "most_ready", "acc_ready", "acc_step", "rows_ready", "out_stored", "retain_ready", "retain_taken",
            "weight_ready", "pair_ready", "masked_ready", "blocks_masked", "inv_ready", "inv_copied", "final_copied",
        ):
            s[name] = ctx.enter_context(nc.semaphore(name))
        panel_loaded = [ctx.enter_context(nc.semaphore(f"panel_loaded{i}")) for i in range(NSLOT)]
        block = ctx.enter_context(nc.Block())

        def cols_panel(w, c, n):
            v = w.rearrange("(k p) n -> p k n", p=P)
            k = v.shape[1]
            h = (k + 1) // 2
            return k, n, [(slice(0, h), slice(0, n), v[:, 0:h, c:c + n]), (slice(h, k), slice(0, n), v[:, h:k, c:c + n])]


        xin = work(0, 4, D)
        pack_rows = work(4096, 4, P)
        qk = work(0, 16, T2)
        tok = work(8192, 4, 4, T2)
        vext = work(16384, 4, 8, HD + 1)
        rrow = work(18464, 2, T2, rows=(0, 8))
        prob = work(19488, 3, 4, P)
        expo = work(21024, 2, 4, P)
        strip_same = work(22048, STRIP)
        strip_from = work(22432, STRIP)
        strip_tmp = [work(21024, STRIP), work(21024 + STRIP, STRIP), work(22816, STRIP)]
        rprob = work(19488, 1536)
        rowb = work(0, 4, 2, T2)
        y_sq = work(4096, 4, D)
        rope_tmp = work(21024, 2, L)
        gate = at(h0, 4, T2, rows=(0, 8))
        mrow = at(h0 + 2048, 2, T2, rows=(0, 8))
        arow = work(19488, 12, P, rows=(0, 8))
        graw = work(21024, T2, rows=(0, 32))
        hout = at(h0, 2, 4, 8, HD + 1)
        acol = small[:, 0:160].rearrange("p (a h) -> p a h", h=8)
        mcol = small[:, 160:224]
        ORDER = ((2, 3, 0, 1), (3, 2, 1, 0))

        def held(t, key, q, base=None):
            a = key * L + q * P if key < 2 else T2 + (key - 2) * T2 + q * P
            return t[:, a:a + P] if t is not None else PS[a // T2][:, a % T2:a % T2 + P]

        CROSS = {}
        for d in range(2):
            for ki in range(4):
                for qi in range(ki + 1, 4):
                    CROSS[d, ki, qi] = len(CROSS)
        y_tok = work(0, 4, D)
        y_tmp = work(4096, 4, T2)
        a_q = work(0, 16, L)
        a_k = work(4096, 16, L)
        a_kdup = work(4096, 4, T2)
        a_k2 = work(6144, 2, T2)
        a_v = work(8192, 4, L)
        m_v = work(8192, 2, D)
        a_sq = work(10240, 12, L)
        a_prob = work(12288, 3, T2)
        a_turn = work(13824, 3, 4, P)
        a_y = work(15360, 2, D)
        a_mx = work(17408, 6, 32)
        a_rs = work(17600, 8, L)
        m_lat = work(19648, 6, L)
        m_kr = work(21184, L)
        m_cs = work(21440, 4, L)
        pos = work(22464, L)
        g_x = work(0, 24, L)
        g_z = work(6144, 2, D)
        g_at = work(8192, 8, L)
        g_t = work(10240, 8, L)
        g_tt = work(12288, 8, L)
        g_u = work(14336, 8, L)
        g_att = work(16384, 8, L)
        g_qd = work(18432, 8, P)
        g_tmp = work(20736, 2, 3, L)
        g_mask = work(20224, 2, L)
        g_tok = work(20736, 2, 7, P)
        g_s = work(22528, P)
        g_acc = work(14336, 4, L)
        g_sq = work(8192, 16, L)
        g_rows = work(22656, 2, L, rows=(0, 8))
        g_row2 = work(19456, 3, L, rows=(0, 8))
        g_o = at(h0, 2, D)
        acc_t = work(19488, 2, T2)
        act_t = work(0, KF, T2)
        silu_t = work(11264, 2, T2)
        e_act = work(0, KE, L)
        e_own = e_act[:, :, 0:P]
        e_silu = work(2816, 2, T2)
        e_row = work(3840, NE, L)
        r_tmp = work(5888, 640)
        r_comb = work(6528, 2, NE)
        r_crow = work(6544, L, rows=(0, 8))
        h_tok = work(7168, 2, D)
        h_own = work(9216, 2, KD, P)
        pick = work(11264, 4, P)
        back = work(11776, 2, L)
        y_own = work(12288, D)
        slots = work(13312, NE + 2, 2)
        weights = work(13332, NE + 2, 2)
        r_row = work(13376, 3, L, rows=(0, 8))
        most_i = work(14144, 1, rows=(0, 1)).bitcast(I32)
        most_f = work(14145, 9, rows=(0, 1))

        @block.sync
        def _(sp):
            panels = Count()

            def load(k, n, halves):
                m = panels.next()
                place = panels.place(NSLOT)
                if panels.i is not None or panels.n > NSLOT:
                    sp.wait_ge(s["panel_used"], panels.ahead(NSLOT))
                dst = slot(place, k, n)
                for ks, ns, src in halves:
                    sp.dma_start(dst[:, ks, ns], src).then_inc(panel_loaded[place], 16)

            def ada_panel(w, i):
                v = w.rearrange("(k p) n -> p k n", p=P)
                load(8, 512, [(slice(0, 4), slice(0, 512), v[:, 0:4, bass.ds(i * 512, 512)]),
                              (slice(4, 8), slice(0, 512), v[:, 4:8, bass.ds(i * 512, 512)])])

            def gu_panel(w, i, half, width=256):
                v = w.rearrange("(k p) n -> p k n", p=P)
                load(8, 2 * width, [(slice(0, 8), slice(0, width), v[:, :, bass.ds(i * 256, width)]),
                                    (slice(0, 8), slice(width, 2 * width), v[:, :, bass.ds(i * 256 + half, width)])])

            def plain(w, parts):
                for c, n in parts:
                    load(*cols_panel(w, c, n))

            def ffn(w_in, w_out, ada):
                ada_panel(ada, 0)
                with turns(sp, 5, panels=(panels, 4)) as i:
                    for j in range(2):
                        gu_panel(w_in, i * 2 + j, FF)
                        ada_panel(ada, i * 2 + (j + 1))
                gu_panel(w_in, 10, FF)
                ada_panel(ada, 11)
                v = w_out.rearrange("(k p) n -> p k n", p=P)
                with turns(sp, 2, panels=(panels, 4)) as i:
                    for j in range(4):
                        c = (i * 4 + j) * P
                        load(KF, P, [(slice(0, 11), slice(0, P), v[:, 0:11, bass.ds(c, P)]),
                                     (slice(11, 22), slice(0, P), v[:, 11:22, bass.ds(c, P)])])

            for i in range(4):
                ada_panel(A["ada_w"][0], i)
            if stop >= 1:
                plain(A["ab_w_in"][0], [(4096, 32)])
                for i, cc in enumerate((0, 512, 1024, 2048, 2560, 3072, 1536, 3584)):
                    plain(A["ab_w_in"][0], [(cc, 512)])
                    ada_panel(A["ada_w"][0], 4 + i)
                plain(A["ab_w_out"][0], [(0, 512), (512, 512)])
            if stop >= 2:
                ffn(A["ffn_w_in"][0], A["ffn_w_out"][0], A["ada_w"][1])
            if stop >= 3:
                plain(A["attn_w_in"][0], [(0, 512), (512, 512), (1024, 512)])
                plain(A["attn_w_out"][0], [(0, 512), (512, 512)])
            if stop >= 4:
                ffn(A["ffn_w_in"][1], A["ffn_w_out"][1], A["ada_w_2"][0])
            if stop >= 5:
                plain(A["mla_w_in_2"][0], [(0, 512), (512, 288)])
                plain(A["mla_w_qb_2"][0], [(0, 768), (768, 768)])
                plain(A["mla_w_kvb_2"][0], [(0, 2048)])
                plain(A["mla_w_out_2"][0], [(0, 512), (512, 512)])
            if stop >= 6:
                ffn(A["ffn_w_gate_up_2"][0], A["ffn_w_down_2"][0], A["ada_w_2"][1])
            if stop >= 7:
                plain(A["gdn_w_in_2"][0], [(4096, 16)] + [(512 * i, 512) for i in range(8)])
                plain(A["gdn_w_out_2"][0], [(0, 512), (512, 512)])
            if stop >= 8:
                gu = A["moe_w_gate_up_2"][0].rearrange("e (k p) n -> p (e k) n", p=P)
                dn = A["moe_w_down_2"][0].rearrange("e (k p) n -> p (e k) n", p=P)
                with turns(sp, NE // 2, panels=(panels, 20)) as i:
                    for j in range(2):
                        e = i * 2 + j
                        for q in range(6):
                            w = 256 if q < 5 else 128
                            load(8, 2 * w, [(slice(0, 8), slice(0, w), gu[:, bass.ds(e * KD, KD), q * 256:q * 256 + w]),
                                            (slice(0, 8), slice(w, 2 * w),
                                             gu[:, bass.ds(e * KD, KD), FE + q * 256:FE + q * 256 + w])])
                        for q in range(4):
                            load(KE, 256, [(slice(0, 6), slice(0, 256), dn[:, bass.ds(e * KE, 6), q * 256:q * 256 + 256]),
                                           (slice(6, 11), slice(0, 256),
                                            dn[:, bass.ds(e * KE + 6, 5), q * 256:q * 256 + 256])])
            fin = work(0, 2, D)
            sp.wait_ge(s["final_copied"], 4)
            sp.dma_start(out.rearrange("a (t p) n -> p (a t) n", p=P), fin).then_inc(s["out_stored"], 16)
            sp.wait_ge(s["out_stored"], 16)

        @block.tensor
        def _(pe):
            c = {n: Count() for n in ("panels", "ada", "gu", "out", "proj", "sq", "h", "sum", "dve", "act", "pool",
                                      "score", "exp", "turn", "o", "ret", "inv", "acc", "moved", "picks")}
            fresh = [False]
            last_panel = [0]

            def mm(o, lhsT, rhs, start=True, stop=True):
                ins = nc.tensor.matmul(o, lhsT, rhs, start=start, stop=stop)
                if fresh[0]:
                    ins.then_inc(s["panel_used"], 1)
                    fresh[0] = False
                return ins

            def turn(o, i):
                n = i.partition_size()
                return nc.tensor.transpose(o, i, ident[0:n, 0:n])

            def panel(k, n):
                m = c["panels"]
                m.next()
                place = m.place(NSLOT)
                fills = (m.n - 1) // NSLOT + 1
                if m.i is not None:
                    fills = m.i * (m.per // NSLOT) + fills
                pe.wait_ge(panel_loaded[place], fills * 32)
                fresh[0] = not (m.i is None and m.n == 1)
                return slot(place, k, n)

            def await_(name, stream):
                pe.wait_ge(s[name], c[stream].next())

            def ada(cond):
                w = panel(8, 512)
                n = c["ada"].next()
                if c["ada"].i is not None or n > 2:
                    pe.wait_ge(s["ada_taken"], c["ada"].ahead(2))
                bank = PS[4 + c["ada"].place(2)]
                for b in range(4):
                    for k in range(8):
                        last = mm(bank[:, 2 * b:2 * b + 2], w[:, k, b * P:(b + 1) * P], conds[:, cond:cond + 2, k],
                                  k == 0, k == 7)
                last.then_inc(s["ada_ready"], 1)

            def ada_sum(nconds):
                m = c["panels"]
                m.next()
                fresh[0] = True
                await_("acc_ready", "acc")
                c["ada"].next()
                pe.wait_ge(s["ada_taken"], c["ada"].ahead(2))
                bank = PS[4 + c["ada"].place(2)]
                for b in range(4):
                    for j in range(nconds):
                        last = mm(bank[:, 2 * b + j:2 * b + j + 1], acc_t[:, j, b * P:(b + 1) * P], const("ones")[:, 0:1])
                last.then_inc(s["ada_ready"], 1)

            def norm_sum(blocks, width, lhsT, bank=6):
                for k in range(blocks):
                    await_("square_ready", "sq")
                    last = nc.tensor.matmul(PS[bank][:, 0:width], lhsT, hT[:, k, 0:width], start=k == 0, stop=k == blocks - 1)
                last.then_inc(s["sum_ready"], 1)

            def await_h(parts):
                c["h"].n += 8 * parts
                pe.wait_ge(s["h_ready"], c["h"].n)

            def out_item():
                n = c["out"].next()
                if c["out"].i is not None or n > 2:
                    pe.wait_ge(s["out_taken"], c["out"].ahead(2))
                return PS[6 + c["out"].place(2)]

            def project_out(width):
                for _ in range(2):
                    w = panel(8, 512)
                    for b in range(4):
                        bank = out_item()
                        for k in range(8):
                            last = mm(bank[:, 0:width], w[:, k, b * P:(b + 1) * P], hT[:, k, 0:width], k == 0, k == 7)
                        last.then_inc(s["out_ready"], 1)

            def proj_item():
                n = c["proj"].next()
                if n > 4:
                    pe.wait_ge(s["proj_taken"], n - 4)
                return PS[c["proj"].place(4)]

            def project(w, lhs_cols, width, kb=8, src=None, rows=(0, P)):
                src = hT if src is None else src
                bank = proj_item()
                for k in range(kb):
                    last = mm(bank[rows[0]:rows[1], 0:width], w[:, k, lhs_cols], src[:, k, 0:width], k == 0, k == kb - 1)
                last.then_inc(s["proj_ready"], 1)

            def project_tok(w, tile, cols, width, kb=8, src=None):
                src = hT if src is None else src
                bank = proj_item()
                for k in range(kb):
                    last = mm(bank[:, 0:width], src[:, k, tile * P:(tile + 1) * P], w[:, k, cols], k == 0, k == kb - 1)
                last.then_inc(s["proj_ready"], 1)

            def ffn(width, nconds):
                ada_sum(nconds)
                await_h(2 if width == T2 else 1)
                nb = T2 // width

                def chunk():
                    w = panel(8, 512)
                    for item in range(2 // nb):
                        c["gu"].next()
                        pe.wait_ge(s["gu_taken"], c["gu"].ahead(0))
                        pl = c["gu"].place(2)
                        for bank, off in ((PS[pl], 0), (PS[2 + pl], 256)):
                            for b in range(nb):
                                f = off + (item * nb + b) * P
                                for k in range(8):
                                    last = mm(bank[:, b * width:(b + 1) * width], w[:, k, f:f + P], hT[:, k, 0:width],
                                              k == 0, k == 7)
                        last.then_inc(s["gu_ready"], 1)

                with turns(pe, 5, panels=(c["panels"], 4), ada=(c["ada"], 2), acc=(c["acc"], 2), gu=(c["gu"], 4 // nb)):
                    for _ in range(2):
                        chunk()
                        ada_sum(nconds)
                chunk()
                ada_sum(nconds)
                pe.wait_ge(s["gu_taken"], c["gu"].n + 2)
                with turns(pe, 2, panels=(c["panels"], 4), out=(c["out"], 4)):
                    for _ in range(4):
                        w = panel(KF, P)
                        bank = out_item()
                        for k in range(KF):
                            last = mm(bank[:, 0:width], w[:, k, :], act_t[:, k, 0:width], k == 0, k == KF - 1)
                        last.then_inc(s["out_ready"], 1)

            pe.wait_ge(s["const_loaded"], 16)
            pe.wait_ge(s["vectors_loaded"], NVEC * 16)
            for g, pack in enumerate(PACKS):
                n = sum(x for _, x in pack)
                last = turn(PS[6][:, g * P:g * P + n], pack_rows[0:n, g, :])
            last.then_inc(s["packs_turned"], 1)
            pe.wait_ge(s["x_loaded"], 32)
            for k in range(8):
                if k >= 4:
                    pe.wait_ge(s["x_copied"], k - 3)
                for t in range(4):
                    last = turn(PS[k % 4][:, t * P:(t + 1) * P], xin[:, t, k * P:(k + 1) * P])
                last.then_inc(s["x_turned"], 1)
            pe.wait_ge(s["cond_ready"], 4)
            for _ in range(4):
                ada(0)

            if stop >= 1:
                norm_sum(8, T2, const("ones"))
                await_h(2)
                w = panel(8, 32)
                project(w, slice(0, 32), T2, rows=(0, 32))
                for kind in "fftffttt":
                    w = panel(8, 512)
                    for b in range(4):
                        if kind == "f":
                            project(w, slice(b * P, (b + 1) * P), T2)
                        else:
                            project_tok(w, b, slice(0, 512), 512)
                    ada_sum(2)
                for b in range(8):
                    bank = proj_item()
                    if b == 0:
                        pe.wait_ge(s["proj_taken"], 33)
                    nc.tensor.matmul(bank[:, 0:L], const("rot"), qk[:, b, 0:L], start=True, stop=True)\
                        .then_inc(s["proj_ready"], 1)
                await_("dve_for_pe", "dve")
                for d in range(2):
                    for a in range(4):
                        last = turn(PS[5][:, (d * 4 + a) * 8:(d * 4 + a) * 8 + 8], gate[:, 2 * d, a * P:(a + 1) * P])
                for a in range(12):
                    last = turn(PS[5][:, (8 + a) * 8:(9 + a) * 8], arow[:, a, :])
                for d in range(2):
                    for a in range(4):
                        last = turn(PS[5][:, 160 + (d * 4 + a) * 8:168 + (d * 4 + a) * 8], mrow[:, d, a * P:(a + 1) * P])
                last.then_inc(s["pe_for_dve"], 1)

                def scores(h, q0, k0):
                    r = (h % 2) * HD
                    for t in range(4):
                        qn = L if t < 2 else T2
                        o = PS[0][:, t * L:(t + 1) * L] if t < 2 else PS[t - 1][:, :]
                        last = nc.tensor.matmul(o, qk[r:r + HD, k0 + h // 2, t * P:(t + 1) * P],
                                                qk[r:r + HD, q0 + h // 2, 0:qn], start=True, stop=True)
                    last.then_inc(s["score_ready"], 1)

                pe.wait_ge(s["proj_taken"], c["proj"].n)
                for h in range(8):
                    if h:
                        pe.wait_ge(s["weight_ready"], h)
                    scores(h, 0, 4)
                    pe.wait_ge(s["weight_ready"], h + 1)
                    if h:
                        pe.wait_ge(s["retain_taken"], h)
                    for q in range(4):
                        keys = (0, 1, 2, 3) if q < 2 else (2, 3)
                        for t in keys:
                            last = nc.tensor.matmul(PS[5][:, q * HD:(q + 1) * HD], held(rprob, t, q), tok[:, 0, t, h * HD:(h + 1) * HD],
                                                    start=t == keys[0], stop=t == keys[-1])
                    last.then_inc(s["retain_ready"], 1)
                await_("act_for_pe", "act")
                group = 0

                def rows(h):
                    if h:
                        pe.wait_ge(s["masked_ready"], 2 * h)
                    sel = ident[0:8, h:h + 1].to_broadcast([8, P])
                    for d in range(2):
                        last = nc.tensor.matmul(PS[3 + d][:, :], sel, rrow[:, d, :], start=True, stop=True)
                    last.then_inc(s["rows_ready"], 1)

                pe.wait_ge(s["retain_taken"], 8)
                rows(0)
                for h in range(8):
                    scores(h, 8, 12)
                    if h < 7:
                        rows(h + 1)
                    for d in range(2):
                        if h:
                            pe.wait_ge(s["o_taken"], 2 * (h - 1) + d + 1)
                        for qi, q in enumerate(ORDER[d]):
                            pe.wait_ge(s["pair_ready"], group + 1)
                            for ki in range(qi + 1):
                                last = nc.tensor.matmul(PS[5 + d][:, q * (HD + 1):(q + 1) * (HD + 1)],
                                                        prob[:, group % 3, ki, :], vext[:, ORDER[d][ki], h, :],
                                                        start=ki == 0, stop=ki == qi)
                            last.then_inc(s["o_ready"], 1)
                            group += 1
                    if h < 7:
                        pe.wait_ge(s["pair_ready"], 8 * (h + 1))
                await_("dve_for_pe", "dve")
                for b in range(8):
                    bank = proj_item()
                    for t in range(4):
                        last = turn(bank[:, t * P:(t + 1) * P], y_tok[:, t, b * P:(b + 1) * P])
                    last.then_inc(s["proj_ready"], 1)
                pe.wait_ge(s["proj_taken"], c["proj"].n)
                project_out(T2)

            if stop >= 2:
                norm_sum(8, T2, const("ones"))
                ffn(T2, 2)

            def attention(items, qv, kv, keys, vv, sm):
                n0, t0, o0 = c["score"].n, c["turn"].n, c["o"].n
                N = len(items)
                for step in range(N + 2):
                    if step < N:
                        if step >= 2:
                            pe.wait_ge(s["score_taken"], SC[0] + step - 1)
                        last = nc.tensor.matmul(PS[step % 2][:, 0:keys(items[step])], qv(items[step]), kv(items[step]),
                                                start=True, stop=True)
                        last.then_inc(s["score_ready"], 1)
                    if 0 <= step - 1 < N:
                        n = step - 1
                        await_("exp_ready", "exp")
                        if n >= 2:
                            pe.wait_ge(s["turn_copied"], TC[0] + n - 1)
                        for t in range(keys(items[n]) // P):
                            last = turn(PS[2 + n % 2][:, t * P:(t + 1) * P], a_prob[:, n % 3, t * P:(t + 1) * P])
                        last.then_inc(s["turn_ready"], 1)
                    if step - 2 >= 0:
                        n = step - 2
                        pe.wait_ge(s["turn_copied"], TC[0] + n + 1)
                        if n >= 2:
                            pe.wait_ge(s["o_taken"], OT[0] + n - 1)
                        nk = keys(items[n]) // P
                        for t in range(nk):
                            last = nc.tensor.matmul(PS[4 + n % 2][:, 0:HD], a_turn[:, n % 3, t, :], vv(items[n], t),
                                                    start=t == 0, stop=t == nk - 1)
                        last.then_inc(s["o_ready"], 1)
                SC[0] += N
                TC[0] += N
                OT[0] += N

            SC, TC, OT = [0], [0], [16]
            c["exp"].n = 64
            if stop >= 3:
                norm_sum(8, T2, const("ones"))
                await_h(2)
                for _ in range(2):
                    w = panel(8, 512)
                    for b in range(4):
                        project(w, slice(b * P, (b + 1) * P), L)
                w = panel(8, 512)
                for b in range(2):
                    project(w, slice(b * P, (b + 1) * P), T2)
                for t in range(4):
                    project_tok(w, t, slice(256, 512), 256)
                for b in range(10):
                    await_("square_ready", "sq")
                    bank = proj_item()
                    if b < 8:
                        o, i = bank[:, 0:L], a_sq[:, b, :]
                    else:
                        o, i = bank[:, :], a_sq[:, 8 + 2 * (b - 8):10 + 2 * (b - 8), :].rearrange("p a b -> p (a b)")
                    nc.tensor.matmul(o, const("halves"), i, start=True, stop=True).then_inc(s["proj_ready"], 1)
                await_("dve_for_pe", "dve")
                for b in range(10):
                    bank = proj_item()
                    i = a_q[:, b, :] if b < 8 else a_k2[:, b - 8, 0:L]
                    nc.tensor.matmul(bank[:, 0:L], const("rot"), i, start=True, stop=True).then_inc(s["proj_ready"], 1)
                await_("dve_for_pe", "dve")
                items = [(h, q) for h in range(16) for q in range(2)]
                attention(items, lambda it: a_q[(it[0] % 2) * HD:(it[0] % 2) * HD + HD, it[0] // 2, it[1] * P:(it[1] + 1) * P],
                          lambda it: a_kdup[(it[0] % 2) * HD:(it[0] % 2) * HD + HD, it[0] // 4, :], lambda it: T2,
                          lambda it, t: a_v[:, t, (it[0] // 4) * HD:(it[0] // 4 + 1) * HD], None)
                await_("dve_for_pe", "dve")
                for b in range(8):
                    bank = proj_item()
                    for t in range(2):
                        last = turn(bank[:, t * P:(t + 1) * P], a_y[:, t, b * P:(b + 1) * P])
                    last.then_inc(s["proj_ready"], 1)
                pe.wait_ge(s["proj_taken"], c["proj"].n)
                project_out(L)

            if stop >= 4:
                norm_sum(8, L, const("ones"))
                ffn(L, 1)

            if stop >= 5:
                norm_sum(8, L, const("ones"))
                await_h(1)
                w = panel(8, 512)
                for b in range(4):
                    project(w, slice(b * P, (b + 1) * P), L)
                w = panel(8, 288)
                for b in range(2):
                    project(w, slice(b * P, (b + 1) * P), L)
                project(w, slice(256, 288), L, rows=(64, 96))
                for first, blocks in ((0, 4), (4, 2)):
                    bank = proj_item()
                    for k in range(blocks):
                        await_("square_ready", "sq")
                        last = nc.tensor.matmul(bank[:, 0:L], const("ones"), a_sq[:, first + k, :], start=k == 0, stop=k == blocks - 1)
                    last.then_inc(s["proj_ready"], 1)
                bank = proj_item()
                pe.wait_ge(s["proj_taken"], c["proj"].n - 3)
                nc.tensor.matmul(bank[64:96, 0:L], const("rot32", (64, 96)), m_kr[64:96, :], start=True, stop=True)\
                    .then_inc(s["proj_ready"], 1)
                await_("dve_for_pe", "dve")
                for q in range(2):
                    w = panel(4, 768)
                    for h in range(8):
                        project(w, slice(96 * h, 96 * h + 96), L, kb=4, src=m_lat, rows=(0, 96))
                w = panel(2, 2048)
                for h in range(16):
                    project(w, slice(P * h, P * h + HD), L, kb=2, src=m_lat[:, 4:6, :], rows=(0, HD))
                wv = w.rearrange("p k (h n) -> p k h n", h=16)
                for t in range(2):
                    for half in range(2):
                        bank = proj_item()
                        for k in range(2):
                            last = mm(bank[:, :].rearrange("p (h n) -> p h n", h=8), m_lat[:, 4 + k, t * P:(t + 1) * P],
                                      wv[:, k, half * 8:(half + 1) * 8, HD:P], k == 0, k == 1)
                        last.then_inc(s["proj_ready"], 1)
                pe.wait_ge(s["proj_taken"], c["proj"].n - 20)
                for b in range(8):
                    bank = proj_item()
                    nc.tensor.matmul(bank[64:96, :], const("rot32", (64, 96)), a_q[64:96, 2 * b:2 * b + 2, :],
                                     start=True, stop=True).then_inc(s["proj_ready"], 1)
                await_("dve_for_pe", "dve")
                items = [(h, q) for h in range(16) for q in range(2)]
                attention(items, lambda it: a_q[0:96, it[0], it[1] * P:(it[1] + 1) * P],
                          lambda it: a_k[0:96, it[0], 0:(it[1] + 1) * P], lambda it: (it[1] + 1) * P,
                          lambda it, t: m_v[:, t, it[0] * HD:(it[0] + 1) * HD], None)
                await_("dve_for_pe", "dve")
                for b in range(8):
                    bank = proj_item()
                    for t in range(2):
                        last = turn(bank[:, t * P:(t + 1) * P], a_y[:, t, b * P:(b + 1) * P])
                    last.then_inc(s["proj_ready"], 1)
                pe.wait_ge(s["proj_taken"], c["proj"].n)
                project_out(L)

            if stop >= 6:
                norm_sum(8, L, const("ones"))
                ffn(L, 1)

            if stop >= 7:
                norm_sum(8, L, const("ones"))
                await_h(1)
                w = panel(8, 16)
                bank = proj_item()
                for j in range(2):
                    for k in range(8):
                        last = mm(bank[0:8, j * L:(j + 1) * L], w[:, k, 8 * j:8 * j + 8], hT[:, k, 0:L], k == 0, k == 7)
                last.then_inc(s["proj_ready"], 1)
                for _ in range(6):
                    w = panel(8, 512)
                    for b in range(4):
                        project(w, slice(b * P, (b + 1) * P), L)
                for _ in range(2):
                    w = panel(8, 512)
                    for t in range(2):
                        project_tok(w, t, slice(0, 512), 512)
                for b in range(16):
                    await_("square_ready", "sq")
                    bank = proj_item()
                    nc.tensor.matmul(bank[:, 0:L], const("ones"), g_sq[:, b, :], start=True, stop=True)\
                        .then_inc(s["proj_ready"], 1)
                await_("dve_for_pe", "dve")
                for j in range(2):
                    for t in range(2):
                        last = turn(PS[7][:, (2 * j + t) * 8:(2 * j + t + 1) * 8], g_rows[:, j, t * P:(t + 1) * P])
                last.then_inc(s["pe_for_dve"], 1)
                await_("dve_for_pe", "dve")
                for h in range(8):
                    if h >= 2:
                        pe.wait_ge(s["pair_ready"], 64 + h - 1)
                    sel = ident[0:8, h:h + 1].to_broadcast([8, P])
                    nc.tensor.matmul(PS[h % 2][:, :], sel, g_rows[:, :, :], start=True, stop=True)
                    for t in range(2):
                        nc.tensor.matmul(PS[2 + h % 2][:, t * P:(t + 1) * P], g_x[:, 8 + h, t * P:(t + 1) * P],
                                         g_x[:, 8 + h, t * P:(t + 1) * P], start=True, stop=True)
                    for t in range(2):
                        last = nc.tensor.matmul(PS[2 + h % 2][:, L + t * P:L + (t + 1) * P], g_x[:, 8 + h, t * P:(t + 1) * P],
                                                g_x[:, h, t * P:(t + 1) * P], start=True, stop=True)
                    last.then_inc(s["score_ready"], 1)
                for h in range(8):
                    pe.wait_ge(s["inv_copied"], h + 1)
                    if h >= 2:
                        pe.wait_ge(s["inv_copied"], 8 + h - 1)
                    for t in range(2):
                        last = turn(PS[4 + h % 2][:, t * P:(t + 1) * P], g_tt[:, h, t * P:(t + 1) * P])
                    last.then_inc(s["inv_ready"], 1)
                CI = 16
                for lev in range(6):
                    for h in range(8):
                        n = lev * 8 + h
                        pe.wait_ge(s["blocks_masked"], n + 1)
                        pe.wait_ge(s["inv_copied"], CI + (lev - 1) * 16 + 8 + h + 1 if lev else 8 + h + 1)
                        if h >= 2:
                            pe.wait_ge(s["inv_copied"], CI + lev * 16 + h - 1)
                        elif lev == 0:
                            pe.wait_ge(s["inv_copied"], 16)
                        for t in range(2):
                            last = nc.tensor.matmul(PS[4 + h % 2][:, t * P:(t + 1) * P], g_mask[:, n % 2, t * P:(t + 1) * P],
                                                    g_t[:, h, t * P:(t + 1) * P], start=True, stop=True)
                        last.then_inc(s["inv_ready"], 1)
                    for h in range(8):
                        pe.wait_ge(s["inv_copied"], CI + lev * 16 + h + 1)
                        if h >= 2:
                            pe.wait_ge(s["inv_copied"], CI + lev * 16 + 8 + h - 1)
                        for t in range(2):
                            o = t * P
                            nc.tensor.matmul(PS[6 + h % 2][:, o:o + P], g_tt[:, h, o:o + P], g_u[:, h, o:o + P],
                                             start=True, stop=True)
                        for t in range(2):
                            o = t * P
                            last = nc.tensor.matmul(PS[6 + h % 2][:, L + o:L + o + P], g_u[:, h, o:o + P], g_tt[:, h, o:o + P],
                                                    start=True, stop=True)
                        last.then_inc(s["inv_ready"], 1)
                pe.wait_ge(s["inv_copied"], CI + 96)
                for h in range(8):
                    if h >= 2:
                        pe.wait_ge(s["turn_copied"], TC[0] + h - 1)
                    for t in range(2):
                        turn(PS[h % 2][:, t * P:(t + 1) * P], g_x[:, 8 + h, t * P:(t + 1) * P])
                    for t in range(2):
                        last = turn(PS[h % 2][:, L + t * P:L + (t + 1) * P], g_x[:, 16 + h, t * P:(t + 1) * P])
                    last.then_inc(s["turn_ready"], 1)
                    g = h % 2
                    pe.wait_ge(s["turn_copied"], TC[0] + h + 1)
                    if h:
                        pe.wait_ge(s["o_taken"], OT[0] + h)
                    nc.tensor.matmul(PS[2][:, 0:P], g_tt[:, h, 0:P], g_tok[:, g, 0, :], start=True, stop=True)
                    nc.tensor.matmul(PS[2][:, P:L], g_tok[:, g, 2, :], g_tt[:, h, P:L], start=True, stop=True)\
                        .then_inc(s["pe_for_dve"], 1)
                    await_("dve_for_pe", "dve")
                    nc.tensor.matmul(PS[3][:, 0:P], g_tok[:, g, 3, :], g_tok[:, g, 5, :], start=True, stop=True)\
                        .then_inc(s["pe_for_dve"], 1)
                    await_("dve_for_pe", "dve")
                    nc.tensor.matmul(PS[2][:, L:L + P], g_tt[:, h, P:L], g_tok[:, g, 1, :], start=True, stop=False)
                    nc.tensor.matmul(PS[2][:, L:L + P], g_tok[:, g, 4, :], g_s, start=False, stop=True)\
                        .then_inc(s["pe_for_dve"], 1)
                    nc.tensor.matmul(PS[4][:, 0:P], g_att[:, h, 0:P], g_tok[:, g, 5, :], start=True, stop=True)
                    nc.tensor.matmul(PS[4][:, P:L], g_qd[:, h, :], g_s, start=True, stop=False)
                    await_("dve_for_pe", "dve")
                    nc.tensor.matmul(PS[4][:, P:L], g_att[:, h, P:L], g_tok[:, g, 6, :], start=False, stop=True)\
                        .then_inc(s["o_ready"], 1)
                TC[0] += 8
                OT[0] += 8
                await_("dve_for_pe", "dve")
                for b in range(8):
                    bank = proj_item()
                    for t in range(2):
                        last = turn(bank[:, t * P:(t + 1) * P], g_z[:, t, b * P:(b + 1) * P])
                    last.then_inc(s["proj_ready"], 1)
                pe.wait_ge(s["proj_taken"], c["proj"].n)
                project_out(L)

            if stop >= 8:
                norm_sum(8, L, const("ones"))
                await_h(1)
                for t in range(2):
                    for k in range(8):
                        last = nc.tensor.matmul(PS[7][:, t * NE:(t + 1) * NE], hT[:, k, t * P:(t + 1) * P], rw[:, k, :],
                                                start=k == 0, stop=k == 7)
                last.then_inc(s["pe_for_dve"], 1)
                await_("dve_for_pe", "dve")
                for t in range(2):
                    last = turn(PS[7][0:8, 128 + t * P:128 + (t + 1) * P], r_comb[:, t, :])
                last.then_inc(s["pe_for_dve"], 1)
                for n in range(4):
                    for b in range(4):
                        k = (n % 2) * 4 + b
                        last = turn(PS[n][:, b * P:(b + 1) * P], hT[:, k, (n // 2) * P:(n // 2 + 1) * P])
                last.then_inc(s["pe_for_dve"], 1)
                await_("dve_for_pe", "dve")
                for t in range(2):
                    turn(PS[7][:, 8 * t:8 * t + 8], r_row[:, 2, t * P:(t + 1) * P])
                turn(PS[7][0:1, 16:24], r_row[:, 1, L - 1:L]).then_inc(s["pe_for_dve"], 1)
                pe.wait_ge(s["most_ready"], 1)
                most = pe.value_load(most_i, min_val=0, max_val=L)
                at_start = {n: (x.n, x.i, x.per) for n, x in c.items()}

                def moved_item():
                    n = c["moved"].next()
                    if c["moved"].i is not None or n > 2:
                        pe.wait_ge(s["moved_taken"], c["moved"].ahead(2))
                    return PS[4 + c["moved"].place(2)]

                def gather(j):
                    await_("picks_ready", "picks")
                    for half in range(2):
                        bank = moved_item()
                        for b in range(4):
                            k = half * 4 + b
                            for t in range(2):
                                last = nc.tensor.matmul(bank[:, b * P:(b + 1) * P], h_tok[:, t, k * P:(k + 1) * P],
                                                        pick[:, t, :], start=t == 0, stop=t == 1)
                        last.then_inc(s["moved_ready"], 1)
                    bank = moved_item()
                    for t in range(2):
                        last = turn(bank[:, t * P:(t + 1) * P], pick[:, 2 + t, :])
                    last.then_inc(s["moved_ready"], 1)

                with pe.If(most <= P):
                    gather(0)
                    with turns(pe, NE // 2, panels=(c["panels"], 20), gu=(c["gu"], 12), out=(c["out"], 16),
                               moved=(c["moved"], 14), picks=(c["picks"], 2)):
                        for j in range(2):
                            for q in range(6):
                                nb = 2 if q < 5 else 1
                                w = panel(8, 2 * nb * P)
                                c["gu"].next()
                                pe.wait_ge(s["gu_taken"], c["gu"].ahead(0))
                                if q == 0:
                                    pe.wait_ge(s["moved_taken"], c["moved"].ahead(0))
                                pl = c["gu"].place(2)
                                for bank, off in ((PS[pl], 0), (PS[2 + pl], nb * P)):
                                    for b in range(nb):
                                        for k in range(8):
                                            last = mm(bank[:, b * P:(b + 1) * P], w[:, k, off + b * P:off + (b + 1) * P],
                                                      h_own[:, j, k, :], k == 0, k == 7)
                                last.then_inc(s["gu_ready"], 1)
                            gather(1 - j)
                            pe.wait_ge(s["gu_taken"], c["gu"].ahead(-2))
                            for q in range(4):
                                w = panel(KE, 256)
                                bank = moved_item()
                                for k in range(KE):
                                    last = mm(bank[:, 0:L], e_own[:, k, :], w[:, k, :], k == 0, k == KE - 1)
                                last.then_inc(s["moved_ready"], 1)
                            pe.wait_ge(s["moved_taken"], c["moved"].ahead(0))
                            for m in range(8):
                                bank = out_item()
                                nc.tensor.matmul(bank[:, 0:L], y_own[:, m * P:(m + 1) * P], back[:, j, :],
                                                 start=True, stop=True).then_inc(s["out_ready"], 1)
                for n, x in c.items():
                    x.n, x.i, x.per = at_start[n]
                with pe.Else():
                    for e in range(NE):
                        bank = PS[e // 2]
                        last = nc.tensor.matmul(bank[:, (e % 2) * L:(e % 2) * L + L], ident[0:8, e:e + 1].to_broadcast([8, P]),
                                                r_crow, start=True, stop=True)
                    last.then_inc(s["moved_ready"], 1)
                    pe.wait_ge(s["picks_ready"], 1)
                    with turns(pe, NE // 2, panels=(c["panels"], 20), gu=(c["gu"], 12), out=(c["out"], 16)):
                        for _ in range(2):
                            for q in range(6):
                                nb = 2 if q < 5 else 1
                                w = panel(8, 2 * nb * P)
                                c["gu"].next()
                                pe.wait_ge(s["gu_taken"], c["gu"].ahead(0))
                                pl = c["gu"].place(2)
                                for bank, off in ((PS[pl], 0), (PS[2 + pl], nb * P)):
                                    for b in range(nb):
                                        for k in range(8):
                                            last = mm(bank[:, b * L:(b + 1) * L], w[:, k, off + b * P:off + (b + 1) * P],
                                                      hT[:, k, 0:L], k == 0, k == 7)
                                last.then_inc(s["gu_ready"], 1)
                            pe.wait_ge(s["gu_taken"], c["gu"].ahead(-2))
                            for q in range(4):
                                w = panel(KE, 256)
                                for b in range(2):
                                    bank = out_item()
                                    for k in range(KE):
                                        last = mm(bank[:, 0:L], w[:, k, b * P:(b + 1) * P], e_act[:, k, :], k == 0, k == KE - 1)
                                    last.then_inc(s["out_ready"], 1)
            norm_sum(8, L, const("ones"))
            await_("dve_for_pe", "dve")
            for t in range(2):
                for half in range(2):
                    n = 2 * t + half
                    for b in range(4):
                        last = turn(PS[n][:, b * P:(b + 1) * P], hT[:, half * 4 + b, t * P:(t + 1) * P])
                    last.then_inc(s["x_turned"], 1)

        @block.vector
        def _(dve):
            c = {n: Count() for n in ("ada", "gu", "out", "proj", "sum", "rstd", "scaled", "dve", "act", "pe", "score", "exp",
                                      "turn", "o", "fa", "inv", "step", "st", "ot", "silu", "masked", "pair", "panels", "astep")}
            V = nc.vector

            def link(ins):
                ins.then_inc(s["dve_step"], 1)
                dve.wait_ge(s["dve_step"], c["step"].next())

            def await_(name, stream):
                dve.wait_ge(s[name], c[stream].next())

            def post(ins, name, stream):
                ins.then_inc(s[name], 1)
                dve.wait_ge(s[name], c[stream].next())

            def scale(o, i, by, plus=None, op1=ALU.add):
                if plus is None:
                    return V.tensor_scalar(o, i, by, None, ALU.mult)
                return V.tensor_scalar(o, i, by, plus, ALU.mult, op1)

            def stt(o, a, sc, b, op0=ALU.mult, op1=ALU.add):
                return V.scalar_tensor_tensor(out=o, in0=a, scalar=sc, in1=b, op0=op0, op1=op1)

            def tt(o, a, b, op=ALU.mult):
                return V.tensor_tensor(o, a, b, op)

            def ada_acc(cond, nconds):
                m = c["panels"]
                m.next()
                place = m.place(NSLOT)
                fills = (m.n - 1) // NSLOT + 1
                if m.i is not None:
                    fills = m.i * (m.per // NSLOT) + fills
                dve.wait_ge(panel_loaded[place], fills * 32)
                w = slot(place, 8, 512)
                for k in range(8):
                    for j in range(nconds):
                        cc = conds[:, cond + j, k:k + 1]
                        if k == 0:
                            last = V.tensor_scalar(acc_t[:, j, :], w[:, 0, :], cc, None, ALU.mult)
                        else:
                            last = stt(acc_t[:, j, :], w[:, k, :], cc, acc_t[:, j, :])
                        if k < 7:
                            last.then_inc(s["acc_step"], 1)
                            c["astep"].next()
                    if k < 7:
                        dve.wait_ge(s["acc_step"], c["astep"].ahead(0))
                last.then_inc(s["acc_ready"], 1)

            def ada(bias, par, i, nconds=2):
                n = c["ada"]
                await_("ada_ready", "ada")
                bank = PS[4 + n.place(2)][:, 0:8].rearrange("p (a b) -> p a b", a=4)
                cols = mod[:, par, bass.ds(i * 4, 4), 0:nconds] if not isinstance(i, int) else \
                    mod[:, par, i * 4:i * 4 + 4, 0:nconds]
                bc = bias[:, bass.ds(i * 4, 4)] if not isinstance(i, int) else bias[:, i * 4:i * 4 + 4]
                tt(cols, bank[:, :, 0:nconds], bc.unsqueeze(2).to_broadcast([P, 4, nconds]), ALU.add).then_inc(s["ada_taken"], 1)

            def mean(bank, width, n, where=None, add=EPS):
                where = rstd if where is None else where
                link(scale(where[:, 0:width], bank[:, 0:width], 1.0 / n, add))
                V.reciprocal(where[:, 0:width], where[:, 0:width]).then_inc(s["mean_ready"], 1)

            def norm(par, which, weight, parts, final=False):
                dve.wait_ge(s["ada_taken"], c["ada"].n)
                if not final:
                    nw = weight.unsqueeze(2).to_broadcast([P, KD, parts])
                    link(stt(gain[:, :, 0:parts], mod[:, par, 24 * which + 8:24 * which + 16, 0:parts], 1.0, nw,
                             ALU.add, ALU.mult))
                await_("sum_ready", "sum")
                mean(PS[6], parts * L, D)
                await_("rstd_ready", "rstd")
                for k in range(KD):
                    for j in range(parts):
                        t = slice(j * L, (j + 1) * L)
                        g = weight[:, k:k + 1] if final else gain[:, k, j:j + 1]
                        stt(hT[:, k, t], xT[:, k, t], g, rstd[:, t], ALU.mult, ALU.mult).then_inc(s["scaled"], 1)
                        c["scaled"].next()

            def add_out(par, which, parts, m):
                n = c["out"]
                await_("out_ready", "out")
                bank = PS[6 + n.place(2)]
                blk = lambda a, t: a[:, m, t] if isinstance(m, int) else a[:, bass.ds(m, 1), t].squeeze(1)
                for j in range(parts):
                    t = slice(j * L, (j + 1) * L)
                    if isinstance(m, int):
                        xv, gv = xT[:, m, t], mod[:, par, 24 * which + 16 + m, j:j + 1]
                    else:
                        xv = xT[:, bass.ds(m, 1), t]
                        gv = mod[:, par, bass.ds(m + (24 * which + 16), 1), j:j + 1]
                        xv, gv = xv.squeeze(1), gv.squeeze(1)
                    last = stt(xv, bank[:, t], gv, xv)
                last.then_inc(s["out_taken"], 1)

            def add_project_out(par, parts, panels):
                c["panels"].n += panels
                dve.wait_ge(s["ada_taken"], c["ada"].n)
                for m in range(8):
                    add_out(par, 0, parts, m)

            def item(bank_only=False):
                await_("proj_ready", "proj")
                return PS[c["proj"].place(4)]

            def ffn(width, par, bias, cond, nconds, norm_of):
                ada_acc(cond, nconds)
                norm_of()
                ada(bias, 1 - par, 0, nconds)
                nb = T2 // width

                def chunk(i):
                    for it in range(2 // nb):
                        await_("silu_ready", "gu")
                        pl = c["gu"].place(2)
                        f = i * 2 + it * nb
                        o = act_t[:, f:f + nb, 0:width] if isinstance(i, int) else act_t[:, bass.ds(f, nb), 0:width]
                        v = lambda t: t.rearrange("p (a b) -> p a b", a=nb)
                        tt(o, v(silu_t[:, pl, :]), v(PS[2 + pl][:, :])).then_inc(s["gu_taken"], 1)

                with turns(dve, 5, ada=(c["ada"], 2), gu=(c["gu"], 4 // nb), panels=(c["panels"], 4),
                           astep=(c["astep"], 14 * nconds)) as i:
                    for j in range(2):
                        c["panels"].next()
                        ada_acc(cond, nconds)
                        chunk(i * 2 + j)
                        ada(bias, 1 - par, i * 2 + (j + 1), nconds)
                c["panels"].next()
                ada_acc(cond, nconds)
                chunk(10)
                ada(bias, 1 - par, 11, nconds)
                c["panels"].n += 8
                with turns(dve, 2, out=(c["out"], 4)) as i:
                    for j in range(4):
                        add_out(par, 1, T2 // L if width == T2 else 1, i * 4 + j)

            for _ in range(2):
                dve.nop().then_inc(s["gu_taken"], 1)
            dve.wait_ge(s["packs_turned"], 1)
            for g, pack in enumerate(PACKS):
                n = sum(x for _, x in pack)
                V.tensor_copy(pack_cols[:, g, 0:n], PS[6][:, g * P:g * P + n]).then_inc(s["packs_copied"], 1)
            for k in range(8):
                dve.wait_ge(s["x_turned"], k + 1)
                V.tensor_copy(xT[:, k, :], PS[k % 4][:, :]).then_inc(s["x_copied"], 1)
            dve.wait_ge(s["rows_loaded"], NROW * 16)
            V.tensor_scalar(lgam[:, 1, :], lgam[:, 0, :], 256.0, None, ALU.mult).then_inc(s["dve_for_act"], 1)
            V.tensor_scalar(lgam[:, 2, :], lgam[:, 0, :], -1.0, None, ALU.mult).then_inc(s["dve_for_act"], 1)
            c["fa"].n = 2
            dve.wait_ge(s["packs_copied"], 4)
            for i in range(4):
                ada(col("ada_b", 0, 48), 0, i)
            c["panels"].n = 4
            dve.wait_ge(s["x_copied"], 8)

            def rope(dst, bank, tmp):
                link(tt(tmp[:, 0, :], dst, const("cos")))
                link(tt(tmp[:, 1, :], bank[:, 0:L], const("sin")))
                return tt(dst, tmp[:, 0, :], tmp[:, 1, :], ALU.add)

            if stop >= 1:
                norm(0, 0, col("norm_w", 0, 8), 2)
                V.memset(vext[:, :, :, HD:HD + 1], 1.0)
                bank = item()
                V.tensor_scalar(graw, bank[0:32, :], rowvec[0:32, 32:33], None, ALU.add).then_inc(s["proj_taken"], 1)
                c["panels"].n += 1
                more = [4]

                def ada_next():
                    c["panels"].n += 1
                    ada_acc(0, 2)

                def ada_end():
                    ada(col("ada_b", 0, 48), 0, more[0])
                    more[0] += 1

                for b in range(8):
                    if b % 4 == 0:
                        ada_next()
                    bank = item()
                    V.tensor_copy(qk[:, b, :], bank[:, :]).then_inc(s["proj_taken"], 1)
                    if b % 4 == 3:
                        ada_end()
                ada_next()
                for t in range(4):
                    bank = item()
                    V.tensor_copy(tok[:, 0, t, :], bank[:, :]).then_inc(s["proj_taken"], 1)
                ada_end()
                for b in range(8):
                    if b % 4 == 0:
                        ada_next()
                    bank = item()
                    w = lambda j: col("mlstm_conv_w", 8 * j + b, 1)
                    x3 = bank[:, :].rearrange("p (a t) -> p a t", a=2)
                    y3 = qk[:, 8 + b, :].rearrange("p (a t) -> p a t", a=2)
                    link(V.tensor_scalar(qk[:, 8 + b, :], bank[:, :], w(1), col("mlstm_conv_b", b, 1), ALU.mult, ALU.add))
                    link(stt(y3[:, :, 1:L], x3[:, :, 0:L - 1], w(0), y3[:, :, 1:L]))
                    stt(y3[:, :, 0:L - 1], x3[:, :, 1:L], w(2), y3[:, :, 0:L - 1]).then_inc(s["proj_taken"], 1)
                    if b % 4 == 3:
                        ada_end()
                ada_next()
                for t in range(4):
                    bank = item()
                    V.tensor_copy(vext[:, t, :, 0:HD], bank[:, :].rearrange("p (h n) -> p h n", h=8)).then_inc(s["proj_taken"], 1)
                ada_end()
                for kind in (1, 2):
                    ada_next()
                    for t in range(4):
                        bank = item()
                        V.tensor_copy(tok[:, kind, t, :], bank[:, :]).then_inc(s["proj_taken"], 1)
                    ada_end()
                dve.wait_ge(s["gates_split"], 64)
                for b in range(8):
                    bank = item()
                    if b == 0:
                        dve.wait_ge(s["proj_taken"], 33)
                    rope(qk[:, b, 0:L], bank, rope_tmp).then_inc(s["proj_taken"], 1)
                    dve.wait_ge(s["proj_taken"], c["proj"].n)
                fg, ig = gate[:, 1::2, :], gate[:, 0::2, :]
                post(stt(mrow, fg, -1.0, fg, ALU.mult, ALU.max), "dve_for_act", "fa")
                await_("act_for_dve", "act")
                link(stt(fg, fg, 0.0, mrow, ALU.min, ALU.subtract))
                ends = {}
                for d in range(2):
                    prev = None
                    for t in ORDER[d]:
                        a, z = t * P, (t + 1) * P
                        v = (lambda r: r[:, a:z]) if d == 0 else (lambda r: r[:, z - 1:(a - 1 if a else None):-1])
                        e = z - 1 if d == 0 else a
                        link(V.tensor_tensor_scan(v(mrow[:, d, :]), v(gate[:, 2 * d + 1, :]), v(gate[:, 2 * d, :]),
                                                  0.0 if prev is None else mrow[:, d, prev:prev + 1], ALU.add, ALU.max))
                        V.tensor_tensor_scan(v(rrow[:, d, :]), const("ones", (0, 8)), v(gate[:, 2 * d + 1, :]),
                                             0.0, ALU.mult, ALU.add).then_inc(s["dve_step"], 1)
                        c["step"].next()
                        prev = ends[d, t] = e
                dve.wait_ge(s["dve_step"], c["step"].n)
                off = rowvec[0:8, 36:48]
                for d in range(2):
                    for ki in range(3):
                        for qi in range(ki + 1, 4):
                            a = CROSS[d, ki, qi]
                            e = ends[d, ORDER[d][qi - 1]]
                            be = rrow[:, d, e:e + 1]
                            if qi == ki + 1:
                                link(V.tensor_copy(off[:, a:a + 1], be))
                            else:
                                link(tt(off[:, a:a + 1], off[:, a - 1:a], be, ALU.add))
                link(tt(ig, ig, rrow, ALU.subtract))
                link(tt(rrow, rrow, mrow, ALU.subtract))
                for (d, ki, qi), a in CROSS.items():
                    k = ORDER[d][ki]
                    last = V.tensor_scalar(arow[:, a, :], gate[:, 2 * d, k * P:(k + 1) * P], off[:, a:a + 1], None, ALU.add)
                last.then_inc(s["dve_for_pe"], 1)
                await_("pe_for_dve", "pe")
                V.tensor_copy(small[:, 0:224], PS[5][:, 0:224]).then_inc(s["dve_for_act"], 1)
                c["fa"].next()
                for h in range(8):
                    await_("act_for_dve", "act")
                    t0, t1, t2 = strip_tmp
                    link(tt(t0, t0, pconst("is_ahead")))
                    link(tt(t1, t1, pconst("is_behind")))
                    link(tt(strip_same, t0, t1, ALU.add))
                    link(tt(strip_from, strip_from, t2, ALU.add))
                    await_("score_ready", "score")
                    if h:
                        dve.wait_ge(s["retain_ready"], h)
                    for t in range(2):
                        win = slice(P - P * t, P - P * t + L)
                        stt(rprob[:, t * L:(t + 1) * L], PS[0][:, t * L:(t + 1) * L], HD ** -0.5, strip_same[:, win],
                            ALU.mult, ALU.mult)
                        a = T2 + t * T2
                        stt(rprob[:, a:a + L], PS[1 + t][:, 0:L], HD ** -0.5, strip_from[:, win], ALU.mult, ALU.mult)
                        last = stt(rprob[:, a + L:a + T2], PS[1 + t][:, L:T2], HD ** -0.5, strip_same[:, win],
                                   ALU.mult, ALU.mult)
                    last.then_inc(s["weight_ready"], 1)
                    dve.wait_ge(s["retain_ready"], h + 1)
                    V.tensor_copy(tok[:, 3, :, h * HD:(h + 1) * HD], PS[5][:, 0:L].rearrange("p (t n) -> p t n", t=4))\
                        .then_inc(s["retain_taken"], 1)
                dve.wait_ge(s["weight_ready"], 8)

                def rows(h):
                    dve.wait_ge(s["rows_ready"], h + 1)
                    for d in range(2):
                        V.tensor_copy(rowb[:, 2 * (h % 2) + d, 0, :], PS[3 + d][:, :])
                        m = const("upto" if d == 0 else "from").unsqueeze(1).to_broadcast([P, 4, P])
                        tt(rowb[:, 2 * (h % 2) + d, 1, :].rearrange("p (a t) -> p a t", a=4),
                           PS[3 + d][:, :].rearrange("p (a t) -> p a t", a=4), m, ALU.add).then_inc(s["masked_ready"], 1)

                rows(0)
                for h in range(8):
                    await_("score_ready", "score")
                    if h < 7:
                        rows(h + 1)
                    for g in range(8):
                        d, qi = g // 4, g % 4
                        q = ORDER[d][qi]
                        n = h * 8 + g
                        await_("exp_ready", "exp")
                        if n >= 3:
                            dve.wait_ge(s["o_ready"], n - 2)
                        for ki in range(qi + 1):
                            last = stt(prob[:, n % 3, ki, :], held(None, ORDER[d][ki], q), HD ** -0.5, expo[:, n % 2, ki, :],
                                       ALU.mult, ALU.mult)
                        last.then_inc(s["pair_ready"], 1)
                        if qi == 3:
                            dve.wait_ge(s["o_ready"], n + 1)
                            V.tensor_copy(hout[:, d, :, h, :], PS[5 + d][:, 0:260].rearrange("p (t n) -> p t n", t=4))\
                                .then_inc(s["o_taken"], 1)
                c["o"].n, c["ot"].n = 64, 16
                dve.wait_ge(s["o_taken"], 16)
                dve.wait_ge(s["dve_step"], c["step"].n)
                fl = mcol.rearrange("p (d t h) -> p d t h", d=2, t=4)
                for d in range(2):
                    link(stt(fl[:, d, :, :], hout[:, d, :, :, HD], 1.0, fl[:, d, :, :], ALU.mult, ALU.max))
                    link(stt(fl[:, d, :, :], hout[:, d, :, :, HD], -1.0, fl[:, d, :, :], ALU.mult, ALU.max))
                link(V.reciprocal(mcol, mcol))
                ym = y_tok.rearrange("p t (m h n) -> p t m h n", m=2, h=8)[:, :, 1, :, :]
                yt = y_tmp.rearrange("p t (h n) -> p t h n", h=8)
                for d, o in ((0, ym), (1, yt)):
                    link(tt(o, hout[:, d, :, :, 0:HD], fl[:, d, :, :].unsqueeze(3).to_broadcast([P, 4, 8, HD])))
                link(tt(y_tok[:, :, T2:D], y_tok[:, :, T2:D], y_tmp, ALU.add))
                link(tt(y_sq[:, :, T2:D], y_tok[:, :, T2:D], y_tok[:, :, T2:D]))
                link(tt(y_sq[:, :, 0:T2], tok[:, 3, :, :], tok[:, 3, :, :]))
                rs = small[:, 0:64]
                link(V.tensor_reduce(rs, y_sq.rearrange("p t (h n) -> p (t h) n", n=HD), X, ALU.add))
                link(scale(rs, rs, 1.0 / HD, EPS))
                post(V.reciprocal(rs, rs), "dve_for_act", "fa")
                await_("act_for_dve", "act")
                r4 = rs.rearrange("p (t h) -> p t h", t=4)
                y4 = y_tok.rearrange("p t (h n) -> p t h n", n=HD)
                link(tt(y4[:, :, 0:8, :], tok[:, 3, :, :].rearrange("p t (h n) -> p t h n", n=HD),
                        r4[:, :, 0:8].unsqueeze(3).to_broadcast([P, 4, 8, HD])))
                link(tt(y4[:, :, 8:16, :], y4[:, :, 8:16, :], r4[:, :, 8:16].unsqueeze(3).to_broadcast([P, 4, 8, HD])))
                link(tt(y_tok[:, :, 0:T2], y_tok[:, :, 0:T2], tok[:, 1, :, :]))
                tt(y_tok[:, :, T2:D], y_tok[:, :, T2:D], tok[:, 2, :, :]).then_inc(s["dve_for_pe"], 1)
                for b in range(8):
                    bank = item()
                    w = col("ret_norm_w", b, 1) if b < 4 else col("mlstm_norm_w", b - 4, 1)
                    V.tensor_scalar(hT[:, b, :], bank[:, :], w, None, ALU.mult).then_inc(s["proj_taken"], 1)
                add_project_out(0, 2, 2)

            if stop >= 2:
                ffn(T2, 0, col("ada_b", 48, 48), 0, 2, lambda: norm(0, 1, col("norm_w", 8, 8), 2))

            mx, nmx, dsum, esink, rec = (a_mx[:, i, :] for i in range(5))

            def attention(items, keys, sink, scaled):
                N = len(items)
                ready0, turn0, o0 = c["st"].n, c["turn"].n, c["o"].n
                for step in range(N + 2):
                    if step < N:
                        h, q = items[step]
                        nk = keys(items[step])
                        await_("score_ready", "score")
                        if step >= 3:
                            dve.wait_ge(s["turn_ready"], turn0 + step - 2)
                        scaled(items[step], step)
                        link(V.reduce_max(mx[:, step:step + 1], a_prob[:, step % 3, 0:nk], X))
                        if sink is not None:
                            link(tt(mx[:, step:step + 1], mx[:, step:step + 1], sink[:, h:h + 1], ALU.max))
                        V.tensor_scalar(nmx[:, step:step + 1], mx[:, step:step + 1], -1.0, None, ALU.mult)\
                            .then_inc(s["max_ready"], 1)
                    if step - 2 >= 0:
                        n = step - 2
                        h, q = items[n]
                        await_("exp_ready", "exp")
                        if sink is not None:
                            link(tt(dsum[:, n:n + 1], dsum[:, n:n + 1], esink[:, n:n + 1], ALU.add))
                        link(V.reciprocal(rec[:, n:n + 1], dsum[:, n:n + 1]))
                        await_("o_ready", "o")
                        V.tensor_scalar(a_y[:, q, h * HD:(h + 1) * HD], PS[4 + n % 2][:, 0:HD], rec[:, n:n + 1], None, ALU.mult)\
                            .then_inc(s["o_taken"], 1)
                        c["ot"].next()
                c["turn"].n += N
                dve.wait_ge(s["o_taken"], c["ot"].n)
                dve.nop().then_inc(s["dve_for_pe"], 1)

            if stop >= 3:
                norm(1, 0, col("norm_w", 16, 8), 2)
                for b in range(8):
                    bank = item()
                    V.tensor_copy(a_q[:, b, :], bank[:, 0:L]).then_inc(s["proj_taken"], 1)
                for b in range(2):
                    bank = item()
                    V.tensor_copy(a_k2[:, b, :], bank[:, :]).then_inc(s["proj_taken"], 1)
                for t in range(4):
                    bank = item()
                    V.tensor_copy(a_v[:, t, :], bank[:, 0:L]).then_inc(s["proj_taken"], 1)
                sq2 = lambda b: a_sq[:, 8 + 2 * b:10 + 2 * b, :].rearrange("p a t -> p (a t)")
                for b in range(10):
                    bank = item()
                    o, i = (a_sq[:, b, :], bank[:, 0:L]) if b < 8 else (sq2(b - 8), bank[:, :])
                    scale(o, i, 1.0 / HD, EPS).then_inc(s["proj_taken"], 1)
                dve.wait_ge(s["proj_taken"], c["proj"].n)
                V.reciprocal(a_sq, a_sq).then_inc(s["mean_ready"], 1)
                await_("rstd_ready", "rstd")
                for b in range(8):
                    stt(a_q[:, b, :], a_q[:, b, :], col("attn_q_norm_w"), a_sq[:, b, :], ALU.mult, ALU.mult)
                for b in range(2):
                    last = stt(a_k2[:, b, :], a_k2[:, b, :], col("attn_k_norm_w"), sq2(b), ALU.mult, ALU.mult)
                last.then_inc(s["dve_for_pe"], 1)
                for b in range(10):
                    bank = item()
                    dst = a_q[:, b, :] if b < 8 else a_k2[:, b - 8, 0:L]
                    rope(dst, bank, a_rs).then_inc(s["proj_taken"], 1)
                    dve.wait_ge(s["proj_taken"], c["proj"].n)
                for kv in range(4):
                    r = (kv % 2) * HD
                    for half in range(2):
                        last = V.tensor_copy(a_kdup[half * HD:(half + 1) * HD, kv, :], a_k2[r:r + HD, kv // 2, :])
                last.then_inc(s["dve_for_pe"], 1)
                dve.wait_ge(s["phase_loaded"], 32)
                wmask = at(phase0, 2, T2)

                def scaled(it, n):
                    post(stt(a_prob[:, n % 3, :], PS[n % 2][:, :], HD ** -0.5, wmask[:, it[1], :]), "score_taken", "st")

                attention([(h, q) for h in range(16) for q in range(2)], lambda it: T2, rowvec[:, 16:32], scaled)
                for b in range(8):
                    bank = item()
                    V.tensor_copy(hT[:, b, 0:L], bank[:, 0:L]).then_inc(s["proj_taken"], 1)
                add_project_out(1, 1, 5)

            if stop >= 4:
                ffn(L, 1, col("ada_b_2", 0, 48), 2, 1, lambda: norm(1, 1, col("norm_w", 24, 8), 1))

            if stop >= 5:
                norm(0, 0, col("norm_mix_2", 0, 8), 1)
                for b in range(6):
                    bank = item()
                    V.tensor_copy(m_lat[:, b, :], bank[:, 0:L]).then_inc(s["proj_taken"], 1)
                bank = item()
                V.tensor_copy(m_kr[64:96, :], bank[64:96, 0:L]).then_inc(s["proj_taken"], 1)
                for j, n in ((0, Q_LORA), (1, KV_LORA)):
                    bank = item()
                    scale(a_rs[:, j, :], bank[:, 0:L], 1.0 / n, EPS).then_inc(s["proj_taken"], 1)
                dve.wait_ge(s["proj_taken"], c["proj"].n)
                V.reciprocal(a_rs[:, 0:2, :], a_rs[:, 0:2, :]).then_inc(s["mean_ready"], 1)
                await_("rstd_ready", "rstd")
                for b in range(6):
                    w = col("mla_q_norm_2", b, 1) if b < 4 else col("mla_kv_norm_2", b - 4, 1)
                    last = stt(m_lat[:, b, :], m_lat[:, b, :], w, a_rs[:, b // 4, :], ALU.mult, ALU.mult)
                last.then_inc(s["dve_for_pe"], 1)
                R = slice(64, 96)
                ang, kf, cosr = m_cs[R, 0, :], m_cs[R, 1, :], m_cs[R, 2, :]
                ki = m_cs[R, 3, :].bitcast(I32)
                dve.wait_ge(s["rows_loaded"], (NROW + 1) * 16)
                link(V.tensor_copy(ang, pos[R, :].bitcast(I32)))
                link(V.tensor_scalar(ang, ang, const("invf", (64, 96)), None, ALU.mult))
                link(scale(kf, ang, 1.0 / TWO_PI))
                link(V.tensor_copy(ki, kf))
                link(V.tensor_copy(kf, ki))
                for part in TWO_PI_PARTS:
                    link(stt(ang, kf, -part, ang))
                link(V.tensor_scalar(kf, ang, PI, -TWO_PI, ALU.is_gt, ALU.mult))
                link(tt(ang, ang, kf, ALU.add))
                link(V.tensor_scalar(kf, ang, -PI, TWO_PI, ALU.is_lt, ALU.mult))
                link(tt(ang, ang, kf, ALU.add))
                link(V.tensor_scalar(cosr, ang, HALF_PI, None, ALU.add))
                link(V.tensor_scalar(kf, cosr, PI, -TWO_PI, ALU.is_gt, ALU.mult))
                link(tt(cosr, cosr, kf, ALU.add))
                link(V.tensor_scalar(ang, ang, -PI, PI, ALU.max, ALU.min))
                post(V.tensor_scalar(cosr, cosr, -PI, PI, ALU.max, ALU.min), "dve_for_act", "fa")
                await_("act_for_dve", "act")
                bank = item()
                t1 = a_rs[R, 2, :]
                link(tt(t1, bank[R, 0:L], ang))
                link(tt(m_kr[R, :], m_kr[R, :], cosr))
                tt(m_kr[R, :], m_kr[R, :], t1, ALU.add).then_inc(s["proj_taken"], 1)
                dve.wait_ge(s["proj_taken"], c["proj"].n)
                V.tensor_copy(a_k[R, :, :], m_kr[R, :].unsqueeze(1).to_broadcast([32, 16, L]))
                for h in range(16):
                    bank = item()
                    V.tensor_copy(a_q[0:96, h, :], bank[0:96, 0:L]).then_inc(s["proj_taken"], 1)
                for h in range(16):
                    bank = item()
                    V.tensor_copy(a_k[0:HD, h, :], bank[0:HD, 0:L]).then_inc(s["proj_taken"], 1)
                for t in range(2):
                    for half in range(2):
                        bank = item()
                        V.tensor_copy(m_v[:, t, half * 512:(half + 1) * 512], bank[:, :]).then_inc(s["proj_taken"], 1)
                for b in range(8):
                    bank = item()
                    q2 = a_q[R, 2 * b:2 * b + 2, :]
                    t2 = a_rs[R, 2:4, :]
                    bc = lambda v: v.unsqueeze(1).to_broadcast([32, 2, L])
                    if b == 0:
                        dve.wait_ge(s["proj_taken"], c["proj"].n - 1)
                    link(tt(t2, bank[R, :].rearrange("p (a t) -> p a t", a=2), bc(ang)))
                    link(tt(q2, q2, bc(cosr)))
                    tt(q2, q2, t2, ALU.add).then_inc(s["proj_taken"], 1)
                    dve.wait_ge(s["proj_taken"], c["proj"].n)
                dve.nop().then_inc(s["dve_for_pe"], 1)
                SC = (64 + 32) ** -0.5

                def scaled_m(it, n):
                    if it[1]:
                        scale(a_prob[:, n % 3, 0:P], PS[n % 2][:, 0:P], SC)
                    a = it[1] * P
                    post(stt(a_prob[:, n % 3, a:a + P], PS[n % 2][:, a:a + P], SC, const("from")), "score_taken", "st")

                attention([(h, q) for h in range(16) for q in range(2)], lambda it: (it[1] + 1) * P, None, scaled_m)
                for b in range(8):
                    bank = item()
                    V.tensor_copy(hT[:, b, 0:L], bank[:, 0:L]).then_inc(s["proj_taken"], 1)
                add_project_out(0, 1, 7)

            if stop >= 6:
                ffn(L, 0, col("ada_b_2", 48, 48), 2, 1, lambda: norm(0, 1, col("norm_ffn_2", 0, 8), 1))

            if stop >= 7:
                norm(1, 0, col("norm_mix_2", 8, 8), 1)
                bank = item()
                V.tensor_copy(g_rows.rearrange("p a t -> p (a t)"), bank[0:8, :]).then_inc(s["proj_taken"], 1)
                for b in range(24):
                    bank = item()
                    await_("act_for_dve", "act")
                    acc = g_acc[:, b % 4, :]
                    w = lambda j: col("gdn_conv_w_2", 24 * j + b, 1)
                    link(stt(acc[:, 1:L], bank[:, 0:L - 1], w(2), acc[:, 1:L]))
                    link(stt(acc[:, 2:L], bank[:, 0:L - 2], w(1), acc[:, 2:L]))
                    stt(acc[:, 3:L], bank[:, 0:L - 3], w(0), acc[:, 3:L]).then_inc(s["proj_taken"], 1)
                for half in range(2):
                    for t in range(2):
                        bank = item()
                        V.tensor_copy(g_z[:, t, half * 512:(half + 1) * 512], bank[:, :]).then_inc(s["proj_taken"], 1)
                for b in range(16):
                    bank = item()
                    V.tensor_scalar(g_sq[:, b, :], bank[:, 0:L], EPS, None, ALU.add).then_inc(s["proj_taken"], 1)
                dve.wait_ge(s["proj_taken"], c["proj"].n)
                V.reciprocal(g_sq, g_sq).then_inc(s["mean_ready"], 1)
                beta_raw, a_raw = g_rows[:, 0, :], g_rows[:, 1, :]
                xx, ab, gg = (g_row2[:, i, :] for i in range(3))
                link(V.tensor_scalar(xx, a_raw, rowvec[0:8, 34:35], None, ALU.add))
                post(stt(ab, xx, -1.0, xx, ALU.mult, ALU.max), "dve_for_act", "fa")
                await_("act_for_dve", "act")
                link(stt(xx, xx, 0.0, ab, ALU.max, ALU.add))
                link(V.tensor_scalar(xx, xx, rowvec[0:8, 35:36], -1.0, ALU.mult, ALU.mult))
                for t in range(2):
                    link(V.tensor_tensor_scan(g_rows[:, 0, t * P:(t + 1) * P], const("ones", (0, 8)),
                                              xx[:, t * P:(t + 1) * P], 0.0, ALU.mult, ALU.add))
                V.tensor_copy(g_rows[:, 1, :], gg).then_inc(s["dve_for_pe"], 1)
                await_("pe_for_dve", "pe")
                gcols = small[:, 0:32]
                link(V.tensor_copy(gcols, PS[7][:, 0:32]))
                post(V.tensor_scalar(small[:, 32:48], gcols[:, 0:16], -1.0, None, ALU.mult), "dve_for_act", "fa")
                await_("rstd_ready", "rstd")
                stt(g_x[:, 0:8, :], g_x[:, 0:8, :], P ** -0.5, g_sq[:, 0:8, :], ALU.mult, ALU.mult)
                tt(g_x[:, 8:16, :], g_x[:, 8:16, :], g_sq[:, 8:16, :]).then_inc(s["dve_for_pe"], 1)
                b3 = lambda v: v.unsqueeze(1).to_broadcast([P, 2, P])
                r3 = lambda v: v.rearrange("p (a t) -> p a t", a=2)

                def gmask(h):
                    await_("score_ready", "score")
                    V.tensor_copy(g_tmp[:, h % 2, 2, P:L], PS[h % 2][:, P:L])
                    tt(r3(g_tmp[:, h % 2, 0, :]), r3(PS[h % 2][:, 0:L]), b3(const("upto")), ALU.add)\
                        .then_inc(s["masked_ready"], 1)

                gmask(0)
                for h in range(8):
                    await_("exp_ready", "exp")
                    if h < 7:
                        gmask(h + 1)
                    g = h % 2
                    et, tm = g_tmp[:, g, 1, :], g_tmp[:, g, 0, :]
                    tt(g_att[:, h, :], PS[2 + g][:, L:T2], et)
                    link(tt(tm, PS[2 + g][:, 0:L], et))
                    link(tt(tm, tm, PS[g][:, L:T2]))
                    tt(r3(g_at[:, h, :]), r3(tm), b3(const("before")))
                    tt(g_qd[:, h, :], g_x[:, h, P:L], g_tmp[:, g, 2, 0:P])
                    tt(small[:, 80 + h:81 + h], PS[g][:, P - 1:P], gcols[:, h:h + 1], ALU.subtract).then_inc(s["pair_ready"], 1)
                dve.wait_ge(s["pair_ready"], c["pair"].n + 72)
                dve.wait_ge(s["phase_loaded"], 48)
                for h in range(8):
                    tm = g_tmp[:, h % 2, 0, :]
                    link(tt(r3(tm), r3(g_at[:, h, :]), b3(imask(0))))
                    stt(r3(g_tt[:, h, :]), r3(tm), -1.0, b3(ident)).then_inc(s["inv_copied"], 1)
                for h in range(8):
                    await_("inv_ready", "inv")
                    V.tensor_copy(g_t[:, h, :], PS[4 + h % 2][:, 0:L]).then_inc(s["inv_copied"], 1)
                for lev in range(6):
                    for h in range(8):
                        await_("inv_ready", "inv")
                        V.tensor_copy(g_u[:, h, :], PS[4 + h % 2][:, 0:L]).then_inc(s["inv_copied"], 1)
                    for h in range(8):
                        await_("inv_ready", "inv")
                        tt(g_t[:, h, :], g_t[:, h, :], PS[6 + h % 2][:, 0:L], ALU.subtract)
                        tt(g_tt[:, h, :], g_tt[:, h, :], PS[6 + h % 2][:, L:T2], ALU.subtract).then_inc(s["inv_copied"], 1)
                await_("act_for_dve", "act")
                link(tt(small[:, 64:80], small[:, 64:80], gcols[:, 16:32]))
                for h in range(8):
                    await_("turn_ready", "turn")
                    g = h % 2
                    for j, (o, sc) in enumerate(((L, gcols[:, 16 + h:17 + h]), (L + P, gcols[:, 24 + h:25 + h]),
                                                 (P, small[:, 72 + h:73 + h]), (0, small[:, 80 + h:81 + h]))):
                        last = V.tensor_scalar(g_tok[:, g, j, :], PS[g][:, o:o + P], sc, None, ALU.mult)
                    last.then_inc(s["turn_copied"], 1)
                    await_("pe_for_dve", "pe")
                    V.tensor_copy(g_tok[:, g, 5, :], PS[2][:, 0:P])
                    V.tensor_scalar(g_tok[:, g, 4, :], PS[2][:, P:L], -1.0, None, ALU.mult).then_inc(s["dve_for_pe"], 1)
                    await_("pe_for_dve", "pe")
                    V.tensor_copy(g_s, PS[3][:, 0:P]).then_inc(s["dve_for_pe"], 1)
                    await_("pe_for_dve", "pe")
                    V.tensor_copy(g_tok[:, g, 6, :], PS[2][:, L:L + P]).then_inc(s["dve_for_pe"], 1)
                    await_("o_ready", "o")
                    V.tensor_copy(g_o[:, :, h * P:(h + 1) * P], r3(PS[4][:, 0:L])).then_inc(s["o_taken"], 1)
                    c["ot"].next()
                dve.wait_ge(s["o_taken"], c["ot"].n)
                sqo = work(8192, 2, D)
                rs = small[:, 96:112]
                link(tt(sqo, g_o, g_o))
                link(V.tensor_reduce(rs, sqo.rearrange("p t (h n) -> p (t h) n", n=P), X, ALU.add))
                link(scale(rs, rs, 1.0 / P, EPS))
                post(V.reciprocal(rs, rs), "dve_for_act", "fa")
                await_("act_for_dve", "act")
                o3 = g_o.rearrange("p t (h n) -> p (t h) n", n=P)
                link(tt(o3, o3, rs.unsqueeze(2).to_broadcast([P, 16, P])))
                tt(g_z, g_z, g_o).then_inc(s["dve_for_pe"], 1)
                for b in range(8):
                    bank = item()
                    V.tensor_scalar(hT[:, b, 0:L], bank[:, 0:L], col("gdn_out_norm_2"), None, ALU.mult).then_inc(s["proj_taken"], 1)
                add_project_out(1, 1, 11)

            if stop >= 8:
                norm(1, 1, col("norm_ffn_2", 8, 8), 1)
                await_("pe_for_dve", "pe")
                lg = r_tmp[:, 0:16].rearrange("p (t e) -> p t e", t=2)
                link(V.tensor_copy(r_tmp[:, 0:16], PS[7][:, 0:16]))
                m1, sel, rank, tot = r_tmp[:, 16:18], r_tmp[:, 32:48], r_tmp[:, 48:64], r_tmp[:, 64:66]
                link(V.tensor_reduce(m1, lg, X, ALU.max))
                for t in range(2):
                    gt, eq = r_tmp[:, 128:192], r_tmp[:, 192:256]
                    v = lambda z: z.rearrange("p (a b) -> p a b", a=8)
                    other, own = lg[:, t, :].unsqueeze(1).to_broadcast([P, 8, 8]), lg[:, t, :].unsqueeze(2).to_broadcast([P, 8, 8])
                    link(tt(v(gt), other, own, ALU.is_gt))
                    link(tt(v(eq), other, own, ALU.is_equal))
                    link(tt(eq, eq, const("earlier")))
                    link(tt(gt, gt, eq, ALU.add))
                    link(V.tensor_reduce(rank[:, t * 8:t * 8 + 8], v(gt), X, ALU.add))
                link(V.tensor_scalar(sel, rank, 1.5, None, ALU.is_lt))
                post(tt(lg, lg, m1.unsqueeze(2).to_broadcast([P, 2, NE]), ALU.subtract), "dve_for_act", "fa")
                await_("act_for_dve", "act")
                link(tt(sel, sel, r_tmp[:, 0:16]))
                s3 = sel.rearrange("p (t e) -> p t e", t=2)
                link(V.tensor_reduce(tot, s3, X, ALU.add))
                link(V.reciprocal(tot, tot))
                tt(r_comb, s3, tot.unsqueeze(2).to_broadcast([P, 2, NE])).then_inc(s["dve_for_pe"], 1)
                await_("pe_for_dve", "pe")
                link(V.tensor_copy(r_crow, PS[7][0:8, 128:128 + L]))
                own, count, slot_of = (r_row[:, i, :] for i in range(3))
                link(V.tensor_scalar(own, r_crow, 0.0, None, ALU.is_gt))
                link(V.tensor_tensor_scan(count, const("ones", (0, 8))[:, 0:1].to_broadcast([8, L]), own, 0.0, ALU.mult, ALU.add))
                link(tt(slot_of, count, own))
                V.tensor_scalar(slot_of, slot_of, -1.0, None, ALU.add).then_inc(s["dve_for_pe"], 1)
                V.memset(slots, -1.0)
                V.memset(weights, 0.0).then_inc(s["dve_step"], 1)
                c["step"].next()
                await_("pe_for_dve", "pe")
                for n in range(4):
                    V.tensor_copy(h_tok[:, n // 2, (n % 2) * 512:(n % 2 + 1) * 512], PS[n][:, :])
                dve.wait_ge(s["dve_step"], c["step"].n)
                V.tensor_copy(weights[:, 0:NE, :].rearrange("p e t -> p t e"), r_comb)
                await_("pe_for_dve", "pe")
                V.tensor_copy(slots[:, 0:NE, :].rearrange("p e t -> p t e"), PS[7][:, 0:16].rearrange("p (t e) -> p t e", t=2))
                link(V.tensor_reduce(most_f[:, 0:1], PS[7][0:1, 16:24], X, ALU.max))
                V.tensor_copy(most_i, most_f[:, 0:1]).then_inc(s["most_ready"], 1)
                dve.wait_ge(s["most_ready"], 1)
                most = dve.value_load(most_i, min_val=0, max_val=L)
                at_start = {n: (x.n, x.i, x.per) for n, x in c.items()}

                def picks(e):
                    for t in range(2):
                        sl, wt = (v[:, bass.ds(e, 1), t:t + 1].squeeze(1) if not isinstance(e, int) else v[:, e, t:t + 1]
                                  for v in (slots, weights))
                        V.tensor_scalar(pick[:, t, :], imask(7), sl, None, ALU.is_equal)
                        last = V.tensor_scalar(pick[:, 2 + t, :], imask(7), sl, wt, ALU.is_equal, ALU.mult)
                    last.then_inc(s["picks_ready"], 1)

                with dve.If(most <= P):
                    picks(0)
                    with turns(dve, NE // 2, gu=(c["gu"], 12), out=(c["out"], 16)) as i:
                        for j in range(2):
                            for q in range(6):
                                nb = 2 if q < 5 else 1
                                await_("silu_ready", "gu")
                                pl = c["gu"].place(2)
                                v = lambda z: z.rearrange("p (a b) -> p a b", a=nb)
                                tt(e_own[:, 2 * q:2 * q + nb, :], v(e_silu[:, pl, 0:nb * P]), v(PS[2 + pl][:, 0:nb * P]))\
                                    .then_inc(s["gu_taken"], 1)
                                if q == 0:
                                    picks(i * 2 + (j + 1))
                            for m in range(8):
                                add_out(1, 1, 1, m)
                for n, x in c.items():
                    x.n, x.i, x.per = at_start[n]
                with dve.Else():
                    dve.wait_ge(s["moved_ready"], 1)
                    for b in range(4):
                        last = V.tensor_copy(e_row[:, 2 * b:2 * b + 2, :].rearrange("p a t -> p (a t)"), PS[b][:, :])
                    last.then_inc(s["picks_ready"], 1)
                    dve.wait_ge(s["picks_ready"], 1)
                    with turns(dve, NE // 2, gu=(c["gu"], 12), out=(c["out"], 16), astep=(c["astep"], 12)) as i:
                        for j in range(2):
                            e = i * 2 + j
                            for q in range(6):
                                nb = 2 if q < 5 else 1
                                await_("silu_ready", "gu")
                                pl = c["gu"].place(2)
                                v = lambda z: z.rearrange("p (a b) -> p a b", a=nb)
                                sv = v(e_silu[:, pl, 0:nb * L])
                                tt(sv, sv, e_row[:, bass.ds(e, 1), :].to_broadcast([P, nb, L])).then_inc(s["acc_step"], 1)
                                dve.wait_ge(s["acc_step"], c["astep"].next())
                                tt(e_act[:, 2 * q:2 * q + nb, :], sv, v(PS[2 + pl][:, 0:nb * L])).then_inc(s["gu_taken"], 1)
                            for m in range(8):
                                add_out(1, 1, 1, m)
            dve.wait_ge(s["out_taken"], c["out"].n)
            norm(0, 0, col("final_norm_2"), 1, final=True)
            dve.wait_ge(s["scaled"], c["scaled"].n)
            dve.nop().then_inc(s["dve_for_pe"], 1)
            for n in range(4):
                dve.wait_ge(s["x_turned"], 8 + n + 1)
                V.tensor_copy(work(0, 2, D)[:, n // 2, (n % 2) * 512:(n % 2 + 1) * 512], PS[n][:, :]).then_inc(s["final_copied"], 1)

        @block.scalar
        def _(act):
            c = {n: Count() for n in ("gu", "out", "proj", "mean", "scaled", "h", "fa", "exp", "max", "turn", "o", "tr", "pair", "step", "moved")}
            ac = lambda o, i, f, **k: nc.scalar.activation(o, i, f, **k)

            def await_(name, stream):
                act.wait_ge(s[name], c[stream].next())

            def link(ins):
                ins.then_inc(s["act_step"], 1)
                act.wait_ge(s["act_step"], c["step"].next())

            def squares(src, blocks, width):
                for k in range(blocks):
                    ac(hT[:, k, 0:width], src[:, k, 0:width], ACT.Square).then_inc(s["square_ready"], 1)

            def root(v, width=None):
                await_("mean_ready", "mean")
                ac(v, v, ACT.Sqrt).then_inc(s["rstd_ready"], 1)

            def norm(par, which, parts):
                if c["out"].n:
                    act.wait_ge(s["out_taken"], c["out"].n)
                squares(xT, KD, parts * L)
                root(rstd[:, 0:parts * L])
                for k in range(KD):
                    for j in range(parts):
                        await_("scaled", "scaled")
                        v = hT[:, k, j * L:(j + 1) * L]
                        ac(v, v, ACT.Identity, bias=mod[:, par, 24 * which + k, j:j + 1]).then_inc(s["h_ready"], 1)

            def ffn(width):
                nb = T2 // width

                def chunk():
                    for _ in range(2 // nb):
                        await_("gu_ready", "gu")
                        act.wait_ge(s["gu_taken"], c["gu"].ahead(0))
                        pl = c["gu"].place(2)
                        ac(silu_t[:, pl, :], PS[pl][:, :], ACT.Silu).then_inc(s["silu_ready"], 1)

                with turns(act, 5, gu=(c["gu"], 4 // nb)):
                    chunk()
                    chunk()
                chunk()
                c["out"].n += 8

            act.dma_start(at(const0, NCONST), A["consts"]).then_inc(s["const_loaded"], 16)
            nvec = 0
            for g, r, src in vector_rows():
                act.dma_start(pack_rows[r:r + src.shape[0], g, 0:src.shape[1]] if src.shape[1] == P else
                              pack_rows[r:r + 1, g, :].rearrange("a (b n) -> a b n", b=2)[:, 0, :], src)\
                    .then_inc(s["vectors_loaded"], 16)
                if src.shape[1] != P:
                    act.dma_start(pack_rows[r:r + 1, g, HD:P], src).then_inc(s["vectors_loaded"], 16)
            for j, name in enumerate(("x", "ctx")):
                act.dma_start(xin[:, 2 * j:2 * j + 2, :], A[name].rearrange("a (t p) n -> p (a t) n", p=P))\
                    .then_inc(s["x_loaded"], 16)
            act.dma_start(at(phase0, NPHASE_A), A["phase_a"]).then_inc(s["phase_loaded"], 16)
            with nc.allow_non_contiguous_dma(reason="a few small vectors"):
                act.dma_start(lgam[:, 0, :], A["ret_log_gamma"].rearrange("a d h -> a (d h)").to_broadcast([P, 16])).then_inc(s["rows_loaded"], 16)
                act.dma_start(rowvec[:, 16:32], A["attn_sink"].to_broadcast([P, 16])).then_inc(s["rows_loaded"], 16)
                act.dma_start(rowvec[0:32, 32:33], A["mlstm_gate_b"].rearrange("a k h -> (k h) a")).then_inc(s["rows_loaded"], 16)
                act.dma_start(rowvec[0:8, 33:34], A["gdn_a_log_2"].rearrange("a h -> h a")).then_inc(s["rows_loaded"], 16)
                act.dma_start(rowvec[0:8, 34:35], A["gdn_dt_bias_2"].rearrange("a h -> h a")).then_inc(s["rows_loaded"], 16)
                act.dma_start(rw, A["moe_w_router_2"][0].rearrange("(k p) n -> p k n", p=P)).then_inc(s["rows_loaded"], 16)
            act.wait_ge(s["packs_copied"], 1)
            for i, name in enumerate(("c", "c_ctx", "c_2", "c_2")):
                ac(conds[:, i, :], col(name), ACT.Silu).then_inc(s["cond_ready"], 1)

            if stop >= 1:
                act.wait_ge(s["x_copied"], 8)
                norm(0, 0, 2)
                act.wait_ge(s["proj_ready"], 33)
                act.wait_ge(s["proj_taken"], 1)
                for k in range(4):
                    act.dma_start(gate[:, k, :], graw[8 * k:8 * k + 8, :]).then_inc(s["gates_split"], 16)
                act.wait_ge(s["proj_taken"], 33)
                for b in range(4):
                    v = qk[:, 8 + 2 * b:10 + 2 * b, :]
                    last = ac(v, v, ACT.Silu)
                last.then_inc(s["act_for_pe"], 1)
                for t in range(2):
                    v = tok[:, 1, 2 * t:2 * t + 2, :]
                    ac(v, v, ACT.Silu)
                for t in range(2):
                    v = tok[:, 2, 2 * t:2 * t + 2, :]
                    ac(v, v, ACT.Sigmoid)
                act.wait_ge(s["dve_for_act"], 3)
                c["fa"].n = 3
                link(ac(mrow, mrow, ACT.Exp, scale=-1.0))
                ac(mrow, mrow, ACT.Ln, bias=1.0).then_inc(s["act_for_dve"], 1)
                await_("dve_for_act", "fa")
                link(ac(mcol, mcol, ACT.Exp, scale=-1.0))
                act.wait_ge(s["phase_loaded"], 16)
                for h in range(8):
                    if h:
                        act.wait_ge(s["weight_ready"], h)
                    f, b = slice(h, h + 1), slice(8 + h, 9 + h)
                    ac(strip_tmp[0], pconst("ahead"), ACT.Exp, scale=lgam[:, 0, f])
                    ac(strip_tmp[1], pconst("behind"), ACT.Exp, scale=lgam[:, 0, b])
                    ac(strip_from, pconst("dist"), ACT.Exp, scale=lgam[:, 0, f], bias=lgam[:, 1, f])
                    ac(strip_tmp[2], pconst("dist"), ACT.Exp, scale=lgam[:, 2, b], bias=lgam[:, 1, b])\
                        .then_inc(s["act_for_dve"], 1)
                for h in range(8):
                    for g in range(8):
                        n = h * 8 + g
                        d, qi = g // 4, g % 4
                        q = ORDER[d][qi]
                        act.wait_ge(s["masked_ready"], 2 * h + d + 1)
                        if n >= 2:
                            act.wait_ge(s["pair_ready"], n - 1)
                        for ki in range(qi + 1):
                            k = ORDER[d][ki]
                            a = 4 * d + k if ki == qi else 8 + CROSS[d, ki, qi]
                            src = rowb[:, 2 * (h % 2) + d, int(ki == qi), q * P:(q + 1) * P]
                            last = ac(expo[:, n % 2, ki, :], src, ACT.Exp, bias=acol[:, a, h:h + 1])
                        last.then_inc(s["exp_ready"], 1)
                await_("dve_for_act", "fa")
                ac(small[:, 0:64], small[:, 0:64], ACT.Sqrt).then_inc(s["act_for_dve"], 1)
                c["out"].n += 8

            if stop >= 2:
                norm(0, 1, 2)
                ffn(T2)

            def attention(N, sink, width):
                turn0, o0 = c["turn"].n, c["o"].n
                for step in range(N + 1):
                    if step < N:
                        h = step // 2
                        await_("max_ready", "max")
                        v = a_prob[:, step % 3, 0:width(step)]
                        last = ac(v, v, ACT.Exp, bias=a_mx[:, 1, step:step + 1], accum_out=a_mx[:, 2, step:step + 1])
                        if sink is not None:
                            last = ac(a_mx[:, 3, step:step + 1], sink[:, h:h + 1], ACT.Exp, bias=a_mx[:, 1, step:step + 1])
                        last.then_inc(s["exp_ready"], 1)
                    if step >= 1:
                        n = step - 1
                        await_("turn_ready", "turn")
                        if n >= 3:
                            act.wait_ge(s["o_ready"], c["o"].n + n - 2)
                        w = width(n) // P
                        ac(a_turn[:, n % 3, 0:w, :].rearrange("p a b -> p (a b)"), PS[2 + n % 2][:, 0:width(n)], ACT.Copy)\
                            .then_inc(s["turn_copied"], 1)
                c["o"].n += N

            c["o"].n = 64
            if stop >= 3:
                act.wait_ge(s["out_taken"], c["out"].n)
                act.dma_start(at(phase0, NPHASE_B), A["phase_b"]).then_inc(s["phase_loaded"], 16)
                norm(1, 0, 2)
                c["proj"].n = 49
                for b in range(8):
                    act.wait_ge(s["proj_taken"], 49 + b + 1)
                    ac(a_sq[:, b, :], a_q[:, b, :], ACT.Square).then_inc(s["square_ready"], 1)
                for b in range(2):
                    act.wait_ge(s["proj_taken"], 49 + 8 + b + 1)
                    ac(a_sq[:, 8 + 2 * b:10 + 2 * b, :].rearrange("p a t -> p (a t)"), a_k2[:, b, :], ACT.Square)\
                        .then_inc(s["square_ready"], 1)
                root(a_sq)
                attention(32, rowvec[:, 16:32], lambda n: T2)
                c["out"].n += 8

            if stop >= 4:
                norm(1, 1, 1)
                ffn(L)

            if stop >= 5:
                act.wait_ge(s["out_taken"], c["out"].n)
                act.dma_start(pos[64:96, :].bitcast(I32), A["positions_2"].to_broadcast([32, L])).then_inc(s["rows_loaded"], 16)
                norm(0, 0, 1)
                for b in range(6):
                    act.wait_ge(s["proj_taken"], 91 + b + 1)
                    ac(a_sq[:, b, :], m_lat[:, b, :], ACT.Square).then_inc(s["square_ready"], 1)
                root(a_rs[:, 0:2, :])
                await_("dve_for_act", "fa")
                for j in (0, 2):
                    v = m_cs[64:96, j, :]
                    last = ac(v, v, ACT.Sin)
                last.then_inc(s["act_for_dve"], 1)
                attention(32, None, lambda n: (n % 2 + 1) * P)
                c["out"].n += 8

            if stop >= 6:
                norm(0, 1, 1)
                ffn(L)

            if stop >= 7:
                act.wait_ge(s["out_taken"], c["out"].n)
                act.dma_start(at(phase0, NPHASE_G), A["phase_g"]).then_inc(s["phase_loaded"], 16)
                norm(1, 0, 1)
                p0 = NPROJ["gdn"] + 1

                def tap_silu(b):
                    act.wait_ge(s["proj_taken"], p0 + b + 1)
                    ac(g_x[:, b, :], g_acc[:, b % 4, :], ACT.Silu).then_inc(s["act_step"], 1)
                    c["step"].next()

                for b in range(24 + 2):
                    if b < 24:
                        act.wait_ge(s["proj_ready"], p0 + b + 1)
                        if b >= 4:
                            act.wait_ge(s["act_step"], c["step"].n - 1)
                        ac(g_acc[:, b % 4, :], PS[(p0 + b) % 4][:, 0:L], ACT.Identity, scale=col("gdn_conv_w_2", 72 + b, 1))\
                            .then_inc(s["act_for_dve"], 1)
                    if b >= 2:
                        tap_silu(b - 2)
                act.wait_ge(s["proj_taken"], p0 + 28)
                for t in range(2):
                    ac(g_z[:, t, :], g_z[:, t, :], ACT.Silu)
                act.wait_ge(s["act_step"], c["step"].n)
                for b in range(16):
                    ac(g_sq[:, b, :], g_x[:, b, :], ACT.Square).then_inc(s["square_ready"], 1)
                root(g_sq)
                await_("dve_for_act", "fa")
                ab = g_row2[:, 1, :]
                ac(g_row2[:, 2, :], g_rows[:, 0, :], ACT.Sigmoid)
                ac(rowvec[0:8, 35:36], rowvec[0:8, 33:34], ACT.Exp)
                link(ac(ab, ab, ACT.Exp, scale=-1.0))
                ac(ab, ab, ACT.Ln, bias=1.0).then_inc(s["act_for_dve"], 1)
                await_("dve_for_act", "fa")
                for h in range(8):
                    act.wait_ge(s["masked_ready"], 16 + h + 1)
                    if h >= 2:
                        act.wait_ge(s["pair_ready"], 64 + h - 1)
                    g = h % 2
                    for t in range(2):
                        ac(g_tmp[:, g, 1, t * P:(t + 1) * P], g_tmp[:, g, 0, t * P:(t + 1) * P], ACT.Exp,
                           bias=small[:, 32 + 8 * t + h:33 + 8 * t + h])
                    ac(g_tmp[:, g, 2, 0:P], g_tmp[:, g, 2, P:L], ACT.Exp).then_inc(s["exp_ready"], 1)
                ac(small[:, 64:80], small[:, 0:16], ACT.Exp)
                act.wait_ge(s["pair_ready"], 64 + 8)
                ac(small[:, 80:88], small[:, 80:88], ACT.Exp).then_inc(s["act_for_dve"], 1)
                await_("dve_for_act", "fa")
                ac(small[:, 96:112], small[:, 96:112], ACT.Sqrt).then_inc(s["act_for_dve"], 1)
                c["out"].n += 8

            if stop >= 8:
                norm(1, 1, 1)
                await_("dve_for_act", "fa")
                ac(r_tmp[:, 0:16], r_tmp[:, 0:16], ACT.Exp).then_inc(s["act_for_dve"], 1)
                act.wait_ge(s["most_ready"], 1)
                most = act.value_load(most_i, min_val=0, max_val=L)
                at_start = {n: (x.n, x.i, x.per) for n, x in c.items()}

                def moved(o, width):
                    await_("moved_ready", "moved")
                    ac(o, PS[4 + c["moved"].place(2)][:, 0:width], ACT.Copy).then_inc(s["moved_taken"], 1)

                def gathered(j):
                    for half in range(2):
                        moved(h_own[:, j, half * 4:half * 4 + 4, :].rearrange("p a b -> p (a b)"), 512)
                    moved(back[:, j, :], L)

                with act.If(most <= P):
                    gathered(0)
                    with turns(act, NE // 2, gu=(c["gu"], 12), moved=(c["moved"], 14)):
                        for j in range(2):
                            for q in range(6):
                                nb = 2 if q < 5 else 1
                                await_("gu_ready", "gu")
                                act.wait_ge(s["gu_taken"], c["gu"].ahead(0))
                                pl = c["gu"].place(2)
                                ac(e_silu[:, pl, 0:nb * P], PS[pl][:, 0:nb * P], ACT.Silu).then_inc(s["silu_ready"], 1)
                            gathered(1 - j)
                            for q in range(4):
                                moved(y_own[:, q * L:(q + 1) * L], L)
                for n, x in c.items():
                    x.n, x.i, x.per = at_start[n]
                with act.Else():
                    with turns(act, NE // 2, gu=(c["gu"], 12)):
                        for _ in range(2):
                            for q in range(6):
                                nb = 2 if q < 5 else 1
                                await_("gu_ready", "gu")
                                act.wait_ge(s["gu_taken"], c["gu"].ahead(0))
                                pl = c["gu"].place(2)
                                ac(e_silu[:, pl, 0:nb * L], PS[pl][:, 0:nb * L], ACT.Silu).then_inc(s["silu_ready"], 1)
                c["out"].n += 64
            if c["out"].n:
                act.wait_ge(s["out_taken"], c["out"].n)
            else:
                act.wait_ge(s["x_copied"], 8)
            squares(xT, KD, L)
            root(rstd[:, 0:L])

        @block.gpsimd
        def _(pool):
            if stop >= 7:
                b3 = lambda v: v.unsqueeze(1).to_broadcast([P, 2, P])
                r3 = lambda v: v.rearrange("p (a t) -> p a t", a=2)
                pool.wait_ge(s["phase_loaded"], 48)
                pool.wait_ge(s["pair_ready"], 64 + 8)
                for lev in range(6):
                    for h in range(8):
                        n = lev * 8 + h
                        if n >= 2:
                            m = n - 2
                            pool.wait_ge(s["inv_ready"], 8 + (m // 8) * 16 + m % 8 + 1)
                        nc.gpsimd.tensor_tensor(r3(g_mask[:, n % 2, :]), r3(g_at[:, h, :]), b3(imask(lev + 1)), ALU.mult)\
                            .then_inc(s["blocks_masked"], 1)


def host_constants():
    import numpy as np

    p, f = np.arange(P)[:, None], np.arange(P)[None, :]
    c = np.zeros((P, NCONST), np.float32)

    def put(name, v):
        a, w = CONST[name]
        c[:, a:a + w] = v

    put("ident", p == f)
    put("ones", 1.0)
    put("halves", p // 64 == f // 64)
    rot = np.zeros((P, P))
    for head in range(2):
        for d in range(32):
            rot[head * 64 + d + 32, head * 64 + d] = -1.0
            rot[head * 64 + d, head * 64 + d + 32] = 1.0
    put("rot", rot)
    put("upto", np.where(p <= f, 0.0, NEG))
    put("from", np.where(p >= f, 0.0, NEG))
    put("before", p < f)
    n = HD // 4
    inv = (np.float32(10000.0) ** (-np.arange(n, dtype=np.float32) / np.float32(n))).astype(np.float32)
    t = np.arange(L, dtype=np.float32)
    ang = np.concatenate([np.floor(t / 64)[:, None] * inv, (t % 64)[:, None] * inv], axis=-1).astype(np.float32)
    put("cos", np.tile(np.cos(ang).T, (4, 1)))
    put("sin", np.tile(np.sin(ang).T, (4, 1)))
    r32 = np.zeros((P, 32))
    for d in range(16):
        r32[64 + d + 16, d] = -1.0
        r32[64 + d, d + 16] = 1.0
    put("rot32", r32)
    inv16 = (np.float32(10000.0) ** (-np.arange(16, dtype=np.float32) / np.float32(16))).astype(np.float32)
    put("invf", np.tile(inv16, 8)[:, None])
    e = np.arange(64)
    put("earlier", (e % 8 < e // 8)[None, :])
    a = np.zeros((P, NPHASE_A), np.float32)
    dist = np.arange(STRIP)[None, :] - P - p
    for name, v in (("dist", dist), ("ahead", np.maximum(dist, 0)), ("behind", np.maximum(-dist, 0)),
                    ("is_ahead", dist >= 0), ("is_behind", dist <= 0)):
        o, w = PHASE_A[name]
        a[:, o:o + w] = v
    b = np.zeros((P, 2, T2), np.float32)
    for q in range(2):
        far = np.abs(q * P + p - np.arange(L)[None, :]) > 128
        b[:, q, 0:L] = np.where(far, NEG, 0.0)
    g = np.zeros((P, 8, P), np.float32)
    g[:, 7, :] = f
    for lev in range(7):
        w = 1 << lev
        g[:, lev, :] = (p // (2 * w) == f // (2 * w)) & (p % (2 * w) < w) & (f % (2 * w) >= w)
    return {"consts": c, "phase_a": a, "phase_b": b.reshape(P, 2 * T2), "phase_g": g.reshape(P, 8 * P)}


def kernel(**inputs):
    import numpy as np
    import concourse.bacc as bacc
    from concourse import mybir as mb
    from concourse.bass_utils import run_bass_kernel_spmd

    nc = bacc.Bacc("TRN2", target_bir_lowering=False, num_devices=1)
    arrays, A = {}, {}
    for name, value in {**inputs, **host_constants()}.items():
        a = np.ascontiguousarray(value)
        arrays[f"in_{name}"] = a
        A[name] = nc.dram_tensor(f"in_{name}", a.shape, mb.dt.from_np(a.dtype), kind="ExternalInput").ap()
    out = nc.dram_tensor("out_x", (1, L, D), F32, kind="ExternalOutput").ap()
    build(nc, A, out)
    return run_bass_kernel_spmd(nc, [arrays], core_ids=[0]).results[0]["out_x"]
```

```python
from contextlib import ExitStack, contextmanager

import concourse.bass as bass
from concourse import mybir

F32 = mybir.dt.float32
I32 = mybir.dt.int32
ALU = mybir.AluOpType
ACT = mybir.ActivationFunctionType
X = mybir.AxisListType.X

P = 128
D = 1024
KD = D // P
L = 256
T2 = 512
EPS = 1e-6
HD = 64
FF = 2816
KF = FF // P
FE = 1408
KE = FE // P
NE = 8
NSLOT = 4
SLOT = 4096
NEG = -1e30

CONST, _at = {}, 0
for _name, _width in (("ident", P), ("ones", P), ("halves", P), ("rot", P), ("upto", P), ("from", P),
                      ("before", P), ("cos", L), ("sin", L), ("rot32", 32), ("invf", 1), ("earlier", 64)):
    CONST[_name] = (_at, _width)
    _at += _width
NCONST = _at
STRIP = 3 * P
PHASE_A = {n: (i * STRIP, STRIP) for i, n in enumerate(("dist", "ahead", "behind", "is_ahead", "is_behind"))}
NPHASE_A = 5 * STRIP
NPHASE_B = 2 * T2
NPHASE_G = 8 * P
NPHASE = NPHASE_A

PACKS = (
    (("c", 8), ("c_ctx", 8), ("c_2", 8), ("norm_w", 32), ("norm_mix_2", 16), ("norm_ffn_2", 16), ("final_norm_2", 8),
     ("ret_norm_w", 4), ("mlstm_norm_w", 4), ("gdn_out_norm_2", 1), ("mla_q_norm_2", 4), ("mla_kv_norm_2", 2),
     ("attn_q_norm_w", 1), ("attn_k_norm_w", 1)),
    (("ada_b", 96), ("mlstm_conv_w", 24), ("mlstm_conv_b", 8)),
    (("ada_b_2", 96),),
    (("gdn_conv_w_2", 96),),
)


NVEC = sum(len(p) for p in PACKS) + 2
NROW = 6
Q_LORA, KV_LORA = 512, 256
PI = 3.1415925
HALF_PI = 1.5707964
TWO_PI = 6.2831855
TWO_PI_PARTS = (6.28125, 0.0019350051879882812, 3.019916050561733e-07)
NPROJ = {"gdn": 153}


class Count:

    def __init__(self):
        self.n, self.i, self.per = 0, None, 0

    def next(self):
        self.n += 1
        return self.n if self.i is None else self.i * self.per + self.n

    def ahead(self, k):
        return self.n - k if self.i is None else self.i * self.per + (self.n - k)

    def place(self, places):
        assert self.i is None or self.per % places == 0
        return (self.n - 1) % places


@contextmanager
def turns(engine, times, **counts):
    with engine.Fori(0, times) as i:
        before = {}
        for name, (count, per) in counts.items():
            before[name] = count.n
            count.i, count.per = i, per
        yield i
        for name, (count, per) in counts.items():
            assert count.n - before[name] == per, (name, count.n - before[name], per)
            count.n, count.i = before[name] + per * times, None


def build(nc, A, out, stop=99):
    ctx = ExitStack()
    with ctx:
        free = [0]
        total = 53200
        mem = ctx.enter_context(nc.sbuf_tensor("mem", [P, total], F32))

        def room(width):
            free[0] += width
            assert free[0] <= total, free[0]
            return free[0] - width

        def at(start, *shape, rows=(0, P)):
            width = 1
            for s in shape:
                width *= s
            v = mem[rows[0]:rows[1], start:start + width]
            if len(shape) == 2:
                return v.rearrange("p (a b) -> p a b", a=shape[0])
            if len(shape) == 3:
                return v.rearrange("p (a b c) -> p a b c", a=shape[0], b=shape[1])
            if len(shape) == 4:
                return v.rearrange("p (a b c d) -> p a b c d", a=shape[0], b=shape[1], c=shape[2])
            return v

        ring0 = room(NSLOT * SLOT)
        xT = at(room(KD * T2), KD, T2)
        h0 = room(KD * T2)
        hT = at(h0, KD, T2)
        const0 = room(NCONST)
        phase0 = room(NPHASE)
        pack_cols = at(room(4 * P), 4, P)
        mod = at(room(2 * 48 * 2), 2, 48, 2)
        gain = at(room(16), KD, 2)
        conds = at(room(4 * KD), 4, KD)
        rw = at(room(KD * NE), KD, NE)
        rowvec = at(room(64), 64)
        small = at(room(256), 256)
        lgam = at(room(48), 3, 16)
        rstd = at(room(T2), T2)
        work0 = room(0)
        nwork = total - work0

        def work(start, *shape, rows=(0, P)):
            width = 1
            for s in shape:
                width *= s
            assert start + width <= nwork, (start + width, nwork)
            return at(work0 + start, *shape, rows=rows)

        def const(name, rows=(0, P)):
            a, w = CONST[name]
            return at(const0 + a, w, rows=rows)

        ident = const("ident")

        def pconst(name):
            a, w = PHASE_A[name]
            return at(phase0 + a, w)

        def imask(lev):
            return at(phase0 + lev * P, P)

        def vector_rows():
            for g, pack in enumerate(PACKS):
                r = 0
                for name, n in pack:
                    v = A[name].flatten()
                    yield g, r, (v.rearrange("(r p) -> r p", p=P) if v.shape[0] % P == 0 else
                                 v.rearrange("(r p) -> r p", r=1))
                    r += n

        PS = [ctx.enter_context(nc.psum_tensor(f"bank{i}", [P, 512], F32)) for i in range(8)]

        def slot(s, k, n):
            return at(ring0 + s * SLOT, k, n)

        col_at = {}
        for g, pack in enumerate(PACKS):
            r = 0
            for name, n in pack:
                col_at[name] = (g, r, n)
                r += n

        def col(name, first=0, n=None):
            g, r, m = col_at[name]
            n = m - first if n is None else n
            return pack_cols[:, g, r + first:r + first + n]

        s = {}
        for name in (
            "const_loaded", "vectors_loaded", "x_loaded", "phase_loaded", "rows_loaded", "packs_turned", "packs_copied",
            "cond_ready", "x_turned", "x_copied", "panel_used", "ada_ready", "ada_taken", "gain_ready",
            "square_ready", "sum_ready", "mean_ready", "rstd_ready", "scaled", "h_ready",
            "gu_ready", "silu_ready", "gu_taken", "out_ready", "out_taken", "proj_ready", "proj_taken",
            "dve_step", "act_step", "pool_step",
            "act_for_dve", "dve_for_act", "act_for_pe", "dve_for_pe", "pe_for_dve",
            "score_ready", "score_taken", "max_ready", "exp_ready", "turn_ready", "turn_copied", "o_ready", "o_taken",
            "gates_split", "moved_ready", "moved_taken", "picks_ready", "most_ready", "acc_ready", "acc_step", "rows_ready", "out_stored", "retain_ready", "retain_taken", "head_ready",
            "weight_ready", "pair_ready", "masked_ready", "blocks_masked", "inv_ready", "inv_copied", "final_copied",
        ):
            s[name] = ctx.enter_context(nc.semaphore(name))
        panel_loaded = [ctx.enter_context(nc.semaphore(f"panel_loaded{i}")) for i in range(NSLOT)]
        block = ctx.enter_context(nc.Block())

        def cols_panel(w, c, n):
            v = w.rearrange("(k p) n -> p k n", p=P)
            k = v.shape[1]
            h = (k + 1) // 2
            return k, n, [(slice(0, h), slice(0, n), v[:, 0:h, c:c + n]), (slice(h, k), slice(0, n), v[:, h:k, c:c + n])]


        xin = work(0, 4, D)
        pack_rows = work(4096, 4, P)
        qk = work(0, 16, T2)
        tok = work(8192, 4, 4, T2)
        vext = work(16384, 4, 8, HD + 1)
        rrow = work(18464, 2, T2, rows=(0, 8))
        prob = work(19488, 3, 4, P)
        expo = work(21024, 2, 4, P)
        strips = [[work(21024 + i * STRIP, STRIP) for i in range(5)], [at(h0 + 1536 + i * STRIP, STRIP) for i in range(5)]]
        rprob = [work(19488, 1536), at(h0, 1536)]
        RET_BANKS = ((0, 1, 2), (3, 4, 6))
        rowb = work(0, 4, 2, T2)
        rope_tmp = work(14336, 2, L)
        gate = work(20512, 4, T2, rows=(0, 8))
        mrow = work(14848, 2, T2, rows=(0, 8))
        arow = at(h0, 12, P, rows=(0, 8))
        graw = work(15872, T2, rows=(0, 32))
        y_back = at(h0 + 3584, 4, HD)
        y_ms = at(h0 + 3520, 2, 4, 8)
        acol = small[:, 0:160].rearrange("p (a h) -> p a h", h=8)
        mcol = small[:, 160:224]
        ORDER = ((2, 3, 0, 1), (3, 2, 1, 0))

        def held(t, key, q):
            a = key * L + q * P if key < 2 else T2 + (key - 2) * T2 + q * P
            return t[:, a:a + P]

        def mlstm_scores(h, key, q):
            if q < 2:
                a = (key % 2) * L + q * P
                return PS[key // 2][:, a:a + P]
            a = (key - 2) * L + (q - 2) * P
            return PS[2 if h % 2 == 0 else 7][:, a:a + P]

        GROUPS = ((0, 0), (0, 1), (1, 0), (1, 1), (0, 2), (0, 3), (1, 2), (1, 3))

        CROSS = {}
        for d in range(2):
            for ki in range(4):
                for qi in range(ki + 1, 4):
                    CROSS[d, ki, qi] = len(CROSS)
        a_q = work(0, 16, L)
        a_k = work(4096, 16, L)
        a_kdup = work(4096, 4, T2)
        a_k2 = work(6144, 2, T2)
        a_v = work(8192, 4, L)
        m_v = work(8192, 2, D)
        a_sq = work(10240, 12, L)
        a_prob = work(12288, 3, T2)
        a_turn = work(13824, 3, 4, P)
        a_y = work(15360, 2, D)
        a_mx = work(17408, 6, 32)
        a_rs = work(17600, 8, L)
        m_lat = work(19648, 6, L)
        m_kr = work(21184, L)
        m_cs = work(21440, 4, L)
        pos = work(22464, L)
        ROW_BANKS, KEY_BANKS = (0, 1, 4, 5), (2, 3, 6, 7)
        squares_t = work(0, KD, T2)
        g_x = work(0, 24, L)
        g_z = work(6144, 2, D)
        g_at = work(8192, 8, L)
        g_t = work(10240, 8, L)
        g_tt = work(12288, 8, L)
        g_u = work(14336, 8, L)
        g_att = work(16384, 8, L)
        g_qd = work(18432, 8, P)
        g_tmp = work(20736, 2, 3, L)
        g_mask = work(20224, 2, L)
        g_tok = work(20736, 2, 7, P)
        g_s = work(22528, 2, P)
        g_acc = work(14336, 4, L)
        g_sq = work(8192, 16, L)
        g_rows = work(22656, 2, L, rows=(0, 8))
        g_row2 = work(19456, 3, L, rows=(0, 8))
        g_o = at(h0, 2, D)
        acc_t = work(19488, 2, T2)
        acc_t2 = work(8192, 2, T2)
        act_t = work(0, KF, T2)
        silu_t = work(11264, 2, T2)
        e_act = work(0, KE, L)
        e_own = e_act[:, :, 0:P]
        e_silu = work(2816, 2, T2)
        e_row = work(3840, NE, L)
        r_tmp = work(5888, 640)
        r_comb = work(6528, 2, NE)
        r_crow = work(6544, L, rows=(0, 8))
        h_tok = work(7168, 2, D)
        h_own = work(9216, 2, KD, P)
        pick = work(11264, 4, P)
        back = work(11776, 2, L)
        y_own = work(12288, D)
        slots = work(13312, NE + 2, 2)
        weights = work(13332, NE + 2, 2)
        r_row = work(13376, 3, L, rows=(0, 8))
        most_i = work(14144, 1, rows=(0, 1)).bitcast(I32)
        most_f = work(14145, 9, rows=(0, 1))

        @block.sync
        def _(sp):
            panels = Count()

            def load(k, n, halves):
                m = panels.next()
                place = panels.place(NSLOT)
                if panels.i is not None or panels.n > NSLOT:
                    sp.wait_ge(s["panel_used"], panels.ahead(NSLOT))
                dst = slot(place, k, n)
                for ks, ns, src in halves:
                    sp.dma_start(dst[:, ks, ns], src).then_inc(panel_loaded[place], 16)

            def ada_panel(w, i):
                v = w.rearrange("(k p) n -> p k n", p=P)
                load(8, 512, [(slice(0, 4), slice(0, 512), v[:, 0:4, bass.ds(i * 512, 512)]),
                              (slice(4, 8), slice(0, 512), v[:, 4:8, bass.ds(i * 512, 512)])])

            def gu_panel(w, i, half, width=256):
                v = w.rearrange("(k p) n -> p k n", p=P)
                load(8, 2 * width, [(slice(0, 8), slice(0, width), v[:, :, bass.ds(i * 256, width)]),
                                    (slice(0, 8), slice(width, 2 * width), v[:, :, bass.ds(i * 256 + half, width)])])

            def plain(w, parts):
                for c, n in parts:
                    load(*cols_panel(w, c, n))

            def ffn(w_in, w_out, ada):
                ada_panel(ada, 0)
                with turns(sp, 5, panels=(panels, 4)) as i:
                    for j in range(2):
                        gu_panel(w_in, i * 2 + j, FF)
                        ada_panel(ada, i * 2 + (j + 1))
                gu_panel(w_in, 10, FF)
                ada_panel(ada, 11)
                v = w_out.rearrange("(k p) n -> p k n", p=P)
                with turns(sp, 2, panels=(panels, 4)) as i:
                    for j in range(4):
                        c = (i * 4 + j) * P
                        load(KF, P, [(slice(0, 11), slice(0, P), v[:, 0:11, bass.ds(c, P)]),
                                     (slice(11, 22), slice(0, P), v[:, 11:22, bass.ds(c, P)])])

            for j, name in enumerate(("x", "ctx")):
                sp.dma_start(work(2 * j * D, 2, D), A[name].rearrange("a (t p) n -> p (a t) n", p=P)).then_inc(s["x_loaded"], 16)
            sp.wait_ge(s["vectors_loaded"], NVEC * 16)
            for i in range(4):
                ada_panel(A["ada_w"][0], i)
            if stop >= 1:
                plain(A["ab_w_in"][0], [(4096, 32)])
                for i, cc in enumerate((0, 512, 1024, 2048, 2560, 3072, 1536, 3584)):
                    plain(A["ab_w_in"][0], [(cc, 512)])
                    ada_panel(A["ada_w"][0], 4 + i)
                plain(A["ab_w_out"][0], [(0, 512), (512, 512)])
            if stop >= 2:
                ffn(A["ffn_w_in"][0], A["ffn_w_out"][0], A["ada_w"][1])
            if stop >= 3:
                plain(A["attn_w_in"][0], [(0, 512), (512, 512), (1024, 512)])
                plain(A["attn_w_out"][0], [(0, 512), (512, 512)])
            if stop >= 4:
                ffn(A["ffn_w_in"][1], A["ffn_w_out"][1], A["ada_w_2"][0])
            if stop >= 5:
                plain(A["mla_w_in_2"][0], [(0, 512), (512, 288)])
                plain(A["mla_w_qb_2"][0], [(0, 768), (768, 768)])
                plain(A["mla_w_kvb_2"][0], [(0, 2048)])
                plain(A["mla_w_out_2"][0], [(0, 512), (512, 512)])
            if stop >= 6:
                ffn(A["ffn_w_gate_up_2"][0], A["ffn_w_down_2"][0], A["ada_w_2"][1])
            if stop >= 7:
                plain(A["gdn_w_in_2"][0], [(4096, 16)] + [(512 * i, 512) for i in range(8)])
                plain(A["gdn_w_out_2"][0], [(0, 512), (512, 512)])
            if stop >= 8:
                gu = A["moe_w_gate_up_2"][0].rearrange("e (k p) n -> p (e k) n", p=P)
                dn = A["moe_w_down_2"][0].rearrange("e (k p) n -> p (e k) n", p=P)
                with turns(sp, NE // 2, panels=(panels, 20)) as i:
                    for j in range(2):
                        e = i * 2 + j
                        for q in range(6):
                            w = 256 if q < 5 else 128
                            load(8, 2 * w, [(slice(0, 8), slice(0, w), gu[:, bass.ds(e * KD, KD), q * 256:q * 256 + w]),
                                            (slice(0, 8), slice(w, 2 * w),
                                             gu[:, bass.ds(e * KD, KD), FE + q * 256:FE + q * 256 + w])])
                        for q in range(4):
                            load(KE, 256, [(slice(0, 6), slice(0, 256), dn[:, bass.ds(e * KE, 6), q * 256:q * 256 + 256]),
                                           (slice(6, 11), slice(0, 256),
                                            dn[:, bass.ds(e * KE + 6, 5), q * 256:q * 256 + 256])])
            fin = work(0, 2, D)
            sp.wait_ge(s["final_copied"], 4)
            sp.dma_start(out.rearrange("a (t p) n -> p (a t) n", p=P), fin).then_inc(s["out_stored"], 16)
            sp.wait_ge(s["out_stored"], 16)

        @block.tensor
        def _(pe):
            c = {n: Count() for n in ("panels", "ada", "gu", "out", "proj", "sq", "h", "sum", "dve", "act", "pool",
                                      "score", "exp", "turn", "o", "ret", "inv", "acc", "moved", "picks")}
            fresh = [False]
            last_panel = [0]

            def mm(o, lhsT, rhs, start=True, stop=True):
                ins = nc.tensor.matmul(o, lhsT, rhs, start=start, stop=stop)
                if fresh[0]:
                    ins.then_inc(s["panel_used"], 1)
                    fresh[0] = False
                return ins

            def turn(o, i):
                n = i.partition_size()
                return nc.tensor.transpose(o, i, ident[0:n, 0:n])

            def panel(k, n):
                m = c["panels"]
                m.next()
                place = m.place(NSLOT)
                fills = (m.n - 1) // NSLOT + 1
                if m.i is not None:
                    fills = m.i * (m.per // NSLOT) + fills
                pe.wait_ge(panel_loaded[place], fills * 32)
                fresh[0] = not (m.i is None and m.n == 1)
                return slot(place, k, n)

            def await_(name, stream):
                pe.wait_ge(s[name], c[stream].next())

            def ada(cond):
                w = panel(8, 512)
                n = c["ada"].next()
                if c["ada"].i is not None or n > 2:
                    pe.wait_ge(s["ada_taken"], c["ada"].ahead(2))
                bank = PS[4 + c["ada"].place(2)]
                for b in range(4):
                    for k in range(8):
                        last = mm(bank[:, 2 * b:2 * b + 2], w[:, k, b * P:(b + 1) * P], conds[:, cond:cond + 2, k],
                                  k == 0, k == 7)
                last.then_inc(s["ada_ready"], 1)

            def ada_sum(nconds, acc=acc_t):
                m = c["panels"]
                m.next()
                fresh[0] = True
                await_("acc_ready", "acc")
                c["ada"].next()
                pe.wait_ge(s["ada_taken"], c["ada"].ahead(2))
                bank = PS[4 + c["ada"].place(2)]
                for b in range(4):
                    for j in range(nconds):
                        last = mm(bank[:, 2 * b + j:2 * b + j + 1], acc[:, j, b * P:(b + 1) * P], const("ones")[:, 0:1])
                last.then_inc(s["ada_ready"], 1)

            def norm_sum(blocks, width, lhsT, src=hT, bank=3):
                for k in range(blocks):
                    await_("square_ready", "sq")
                    last = nc.tensor.matmul(PS[bank][:, 0:width], lhsT, src[:, k, 0:width], start=k == 0, stop=k == blocks - 1)
                last.then_inc(s["sum_ready"], 1)

            pending = []

            def await_h(parts):
                c["h"].n += 8 * parts
                pending[:] = [parts]

            def block_ready(k):
                if pending:
                    pe.wait_ge(s["h_ready"], c["h"].n - pending[0] * (7 - k))
                    if k == 7:
                        pending.clear()

            def out_item():
                n = c["out"].next()
                if c["out"].i is not None or n > 2:
                    pe.wait_ge(s["out_taken"], c["out"].ahead(2))
                return PS[6 + c["out"].place(2)]

            def project_out(width):
                for _ in range(2):
                    w = panel(8, 512)
                    for b in range(4):
                        bank = out_item()
                        for k in range(8):
                            last = mm(bank[:, 0:width], w[:, k, b * P:(b + 1) * P], hT[:, k, 0:width], k == 0, k == 7)
                        last.then_inc(s["out_ready"], 1)

            def proj_item():
                n = c["proj"].next()
                if n > 4:
                    pe.wait_ge(s["proj_taken"], n - 4)
                return PS[c["proj"].place(4)]

            def project(w, lhs_cols, width, kb=8, src=None, rows=(0, P)):
                src = hT if src is None else src
                bank = proj_item()
                for k in range(kb):
                    if src is hT:
                        block_ready(k)
                    last = mm(bank[rows[0]:rows[1], 0:width], w[:, k, lhs_cols], src[:, k, 0:width], k == 0, k == kb - 1)
                last.then_inc(s["proj_ready"], 1)

            def project_tok(w, tile, cols, width, kb=8, src=None):
                src = hT if src is None else src
                bank = proj_item()
                for k in range(kb):
                    if src is hT:
                        block_ready(k)
                    last = mm(bank[:, 0:width], src[:, k, tile * P:(tile + 1) * P], w[:, k, cols], k == 0, k == kb - 1)
                last.then_inc(s["proj_ready"], 1)

            def ffn(width, nconds):
                ada_sum(nconds)
                await_h(2 if width == T2 else 1)
                nb = T2 // width

                def chunk():
                    w = panel(8, 512)
                    for item in range(2 // nb):
                        c["gu"].next()
                        pe.wait_ge(s["gu_taken"], c["gu"].ahead(0))
                        pl = c["gu"].place(2)
                        for bank, off in ((PS[pl], 0), (PS[2 + pl], 256)):
                            for b in range(nb):
                                f = off + (item * nb + b) * P
                                for k in range(8):
                                    block_ready(k)
                                    last = mm(bank[:, b * width:(b + 1) * width], w[:, k, f:f + P], hT[:, k, 0:width],
                                              k == 0, k == 7)
                        last.then_inc(s["gu_ready"], 1)

                with turns(pe, 5, panels=(c["panels"], 4), ada=(c["ada"], 2), acc=(c["acc"], 2), gu=(c["gu"], 4 // nb)):
                    for _ in range(2):
                        chunk()
                        ada_sum(nconds)
                chunk()
                ada_sum(nconds)
                pe.wait_ge(s["gu_taken"], c["gu"].n + 2)
                with turns(pe, 2, panels=(c["panels"], 4), out=(c["out"], 4)):
                    for _ in range(4):
                        w = panel(KF, P)
                        bank = out_item()
                        for k in range(KF):
                            last = mm(bank[:, 0:width], w[:, k, :], act_t[:, k, 0:width], k == 0, k == KF - 1)
                        last.then_inc(s["out_ready"], 1)

            pe.wait_ge(s["const_loaded"], 16)
            pe.wait_ge(s["vectors_loaded"], NVEC * 16)
            for g, pack in enumerate(PACKS):
                n = sum(x for _, x in pack)
                last = turn(PS[6][:, g * P:g * P + n], pack_rows[0:n, g, :])
            last.then_inc(s["packs_turned"], 1)
            pe.wait_ge(s["x_loaded"], 32)
            for k in range(8):
                if k >= 4:
                    pe.wait_ge(s["x_copied"], k - 3)
                for t in range(4):
                    last = turn(PS[k % 4][:, t * P:(t + 1) * P], xin[:, t, k * P:(k + 1) * P])
                last.then_inc(s["x_turned"], 1)
            pe.wait_ge(s["cond_ready"], 4)
            for _ in range(2):
                ada(0)
            ada_sum(2)
            ada_sum(2, acc_t2)

            pe.wait_ge(s["x_copied"], 8)
            if stop >= 1:
                norm_sum(8, T2, const("ones"))
                await_h(2)
                w = panel(8, 32)
                project(w, slice(0, 32), T2, rows=(0, 32))
                for n, kind in enumerate("fftffttt"):
                    w = panel(8, 512)
                    for b in range(4):
                        if kind == "f":
                            project(w, slice(b * P, (b + 1) * P), T2)
                        else:
                            project_tok(w, b, slice(0, 512), 512)
                        if n in (2, 5):
                            bank = proj_item()
                            if n == 2 and b == 0:
                                pe.wait_ge(s["proj_taken"], 9)
                            nc.tensor.matmul(bank[:, 0:L], const("rot"), qk[:, 4 * (n // 5) + b, 0:L], start=True, stop=True)\
                                .then_inc(s["proj_ready"], 1)
                    ada_sum(2)
                await_("dve_for_pe", "dve")
                for d in range(2):
                    for a in range(4):
                        last = turn(PS[5][:, (d * 4 + a) * 8:(d * 4 + a) * 8 + 8], gate[:, 2 * d, a * P:(a + 1) * P])
                for a in range(12):
                    last = turn(PS[5][:, (8 + a) * 8:(9 + a) * 8], arow[:, a, :])
                for d in range(2):
                    for a in range(4):
                        last = turn(PS[5][:, 160 + (d * 4 + a) * 8:168 + (d * 4 + a) * 8], mrow[:, d, a * P:(a + 1) * P])
                last.then_inc(s["pe_for_dve"], 1)

                def scores(h):
                    r = (h % 2) * HD
                    banks = RET_BANKS[h % 2]
                    for t in range(4):
                        qn = L if t < 2 else T2
                        o = PS[banks[0]][:, t * L:(t + 1) * L] if t < 2 else PS[banks[t - 1]][:, :]
                        last = nc.tensor.matmul(o, qk[r:r + HD, 4 + h // 2, t * P:(t + 1) * P],
                                                qk[r:r + HD, h // 2, 0:qn], start=True, stop=True)
                    last.then_inc(s["score_ready"], 1)

                pe.wait_ge(s["proj_taken"], c["proj"].n)
                scores(0)
                scores(1)
                for h in range(8):
                    pe.wait_ge(s["weight_ready"], h + 1)
                    if h >= 2:
                        pe.wait_ge(s["retain_taken"], h - 1)
                    for q in range(4):
                        keys = (0, 1, 2, 3) if q < 2 else (2, 3)
                        for t in keys:
                            last = nc.tensor.matmul(PS[5 + 2 * (h % 2)][:, q * HD:(q + 1) * HD], held(rprob[h % 2], t, q),
                                                    tok[:, 0, t, h * HD:(h + 1) * HD], start=t == keys[0], stop=t == keys[-1])
                    last.then_inc(s["retain_ready"], 1)
                    if h < 6:
                        scores(h + 2)
                await_("act_for_pe", "act")
                group = 0

                def rows(h):
                    if h:
                        pe.wait_ge(s["masked_ready"], 2 * h)
                    sel = ident[0:8, h:h + 1].to_broadcast([8, P])
                    for d in range(2):
                        last = nc.tensor.matmul(PS[3 + d][:, :], sel, rrow[:, d, :], start=True, stop=True)
                    last.then_inc(s["rows_ready"], 1)

                def mlstm(h, q, keys):
                    r = (h % 2) * HD
                    for t in keys:
                        o = PS[t // 2 if q < 2 else (2 if h % 2 == 0 else 7)][:, (t % 2) * L:(t % 2 + 1) * L]
                        last = nc.tensor.matmul(o, qk[r:r + HD, 12 + h // 2, t * P:(t + 1) * P],
                                                qk[r:r + HD, 8 + h // 2, q * P:(q + 2) * P], start=True, stop=True)
                    last.then_inc(s["score_ready"], 1)

                pe.wait_ge(s["retain_taken"], 7)
                rows(0)
                mlstm(0, 0, range(4))
                pe.wait_ge(s["retain_taken"], 8)
                mlstm(0, 2, (2, 3))
                for h in range(8):
                    if h < 7:
                        rows(h + 1)
                    for g, (d, qi) in enumerate(GROUPS):
                        q = ORDER[d][qi]
                        if g == 1 and h < 7:
                            mlstm(h + 1, 2, (2, 3))
                        if h and qi == 0:
                            pe.wait_ge(s["o_taken"], 2 * (h - 1) + d + 1)
                        pe.wait_ge(s["pair_ready"], group + 1)
                        for ki in range(qi + 1):
                            last = nc.tensor.matmul(PS[5 + d][:, q * (HD + 1):(q + 1) * (HD + 1)],
                                                    prob[:, group % 3, ki, :], vext[:, ORDER[d][ki], h, :],
                                                    start=ki == 0, stop=ki == qi)
                        last.then_inc(s["o_ready"], 1)
                        group += 1
                    if h < 7:
                        mlstm(h + 1, 0, range(4))
                for b in range(8):
                    if b % 4 == 0:
                        await_("dve_for_pe", "dve")
                    bank = proj_item()
                    for t in range(4):
                        last = turn(bank[:, t * P:(t + 1) * P], tok[:, 1 + b // 4, t, (b % 4) * P:(b % 4 + 1) * P])
                    last.then_inc(s["proj_ready"], 1)
                pe.wait_ge(s["proj_taken"], c["proj"].n)
                project_out(T2)

            if stop >= 2:
                norm_sum(8, T2, const("ones"), squares_t)
                ffn(T2, 2)

            def attention(items, qv, kv, keys, vv, sm):
                n0, t0, o0 = c["score"].n, c["turn"].n, c["o"].n
                N = len(items)
                for step in range(N + 2):
                    if step < N:
                        if step >= 2:
                            pe.wait_ge(s["score_taken"], SC[0] + step - 1)
                        last = nc.tensor.matmul(PS[step % 2][:, 0:keys(items[step])], qv(items[step]), kv(items[step]),
                                                start=True, stop=True)
                        last.then_inc(s["score_ready"], 1)
                    if 0 <= step - 1 < N:
                        n = step - 1
                        await_("exp_ready", "exp")
                        if n >= 2:
                            pe.wait_ge(s["turn_copied"], TC[0] + n - 1)
                        for t in range(keys(items[n]) // P):
                            last = turn(PS[2 + n % 2][:, t * P:(t + 1) * P], a_prob[:, n % 3, t * P:(t + 1) * P])
                        last.then_inc(s["turn_ready"], 1)
                    if step - 2 >= 0:
                        n = step - 2
                        pe.wait_ge(s["turn_copied"], TC[0] + n + 1)
                        if n >= 2:
                            pe.wait_ge(s["o_taken"], OT[0] + n - 1)
                        nk = keys(items[n]) // P
                        for t in range(nk):
                            last = nc.tensor.matmul(PS[4 + n % 2][:, 0:HD], a_turn[:, n % 3, t, :], vv(items[n], t),
                                                    start=t == 0, stop=t == nk - 1)
                        last.then_inc(s["o_ready"], 1)
                SC[0] += N
                TC[0] += N
                OT[0] += N

            SC, TC, OT = [0], [0], [16]
            c["exp"].n = 64
            if stop >= 3:
                norm_sum(8, T2, const("ones"))
                await_h(2)
                for _ in range(2):
                    w = panel(8, 512)
                    for b in range(4):
                        project(w, slice(b * P, (b + 1) * P), L)

                def square_sum(b):
                    await_("square_ready", "sq")
                    bank = proj_item()
                    if b < 8:
                        o, i = bank[:, 0:L], a_sq[:, b, :]
                    else:
                        o, i = bank[:, :], a_sq[:, 8 + 2 * (b - 8):10 + 2 * (b - 8), :].rearrange("p a b -> p (a b)")
                    nc.tensor.matmul(o, const("halves"), i, start=True, stop=True).then_inc(s["proj_ready"], 1)

                w = panel(8, 512)
                for b in range(8):
                    square_sum(b)
                for b in range(2):
                    project(w, slice(b * P, (b + 1) * P), T2)
                project_tok(w, 0, slice(256, 512), 256)
                for b in range(8, 10):
                    square_sum(b)
                for t in range(1, 4):
                    project_tok(w, t, slice(256, 512), 256)
                await_("dve_for_pe", "dve")
                for b in range(10):
                    bank = proj_item()
                    i = a_q[:, b, :] if b < 8 else a_k2[:, b - 8, 0:L]
                    nc.tensor.matmul(bank[:, 0:L], const("rot"), i, start=True, stop=True).then_inc(s["proj_ready"], 1)
                await_("dve_for_pe", "dve")
                items = [(h, q) for h in range(16) for q in range(2)]
                attention(items, lambda it: a_q[(it[0] % 2) * HD:(it[0] % 2) * HD + HD, it[0] // 2, it[1] * P:(it[1] + 1) * P],
                          lambda it: a_kdup[(it[0] % 2) * HD:(it[0] % 2) * HD + HD, it[0] // 4, :], lambda it: T2,
                          lambda it, t: a_v[:, t, (it[0] // 4) * HD:(it[0] // 4 + 1) * HD], None)
                await_("dve_for_pe", "dve")
                for b in range(8):
                    bank = proj_item()
                    for t in range(2):
                        last = turn(bank[:, t * P:(t + 1) * P], a_y[:, t, b * P:(b + 1) * P])
                    last.then_inc(s["proj_ready"], 1)
                pe.wait_ge(s["proj_taken"], c["proj"].n)
                project_out(L)

            if stop >= 4:
                norm_sum(8, L, const("ones"), squares_t)
                ffn(L, 1)

            if stop >= 5:
                norm_sum(8, L, const("ones"))
                await_h(1)
                w = panel(8, 512)
                for b in range(4):
                    project(w, slice(b * P, (b + 1) * P), L)
                w = panel(8, 288)
                for b in range(2):
                    project(w, slice(b * P, (b + 1) * P), L)
                project(w, slice(256, 288), L, rows=(64, 96))
                for first, blocks in ((0, 4), (4, 2)):
                    bank = proj_item()
                    for k in range(blocks):
                        await_("square_ready", "sq")
                        last = nc.tensor.matmul(bank[:, 0:L], const("ones"), a_sq[:, first + k, :], start=k == 0, stop=k == blocks - 1)
                    last.then_inc(s["proj_ready"], 1)
                bank = proj_item()
                pe.wait_ge(s["proj_taken"], c["proj"].n - 3)
                nc.tensor.matmul(bank[64:96, 0:L], const("rot32", (64, 96)), m_kr[64:96, :], start=True, stop=True)\
                    .then_inc(s["proj_ready"], 1)
                await_("dve_for_pe", "dve")
                q_item = []

                def rotated(b):
                    bank = proj_item()
                    pe.wait_ge(s["proj_taken"], q_item[2 * b + 1])
                    nc.tensor.matmul(bank[64:96, :], const("rot32", (64, 96)), a_q[64:96, 2 * b:2 * b + 2, :],
                                     start=True, stop=True).then_inc(s["proj_ready"], 1)

                for q in range(2):
                    w = panel(4, 768)
                    for h in range(8):
                        project(w, slice(96 * h, 96 * h + 96), L, kb=4, src=m_lat, rows=(0, 96))
                        q_item.append(c["proj"].n)
                        n = len(q_item)
                        if n % 2 == 0 and n >= 4:
                            rotated(n // 2 - 2)
                rotated(7)
                w = panel(2, 2048)
                for h in range(16):
                    project(w, slice(P * h, P * h + HD), L, kb=2, src=m_lat[:, 4:6, :], rows=(0, HD))
                wv = w.rearrange("p k (h n) -> p k h n", h=16)
                for t in range(2):
                    for half in range(2):
                        bank = proj_item()
                        for k in range(2):
                            last = mm(bank[:, :].rearrange("p (h n) -> p h n", h=8), m_lat[:, 4 + k, t * P:(t + 1) * P],
                                      wv[:, k, half * 8:(half + 1) * 8, HD:P], k == 0, k == 1)
                        last.then_inc(s["proj_ready"], 1)
                await_("dve_for_pe", "dve")
                items = [(h, q) for h in range(16) for q in range(2)]
                attention(items, lambda it: a_q[0:96, it[0], it[1] * P:(it[1] + 1) * P],
                          lambda it: a_k[0:96, it[0], 0:(it[1] + 1) * P], lambda it: (it[1] + 1) * P,
                          lambda it, t: m_v[:, t, it[0] * HD:(it[0] + 1) * HD], None)
                await_("dve_for_pe", "dve")
                for b in range(8):
                    bank = proj_item()
                    for t in range(2):
                        last = turn(bank[:, t * P:(t + 1) * P], a_y[:, t, b * P:(b + 1) * P])
                    last.then_inc(s["proj_ready"], 1)
                pe.wait_ge(s["proj_taken"], c["proj"].n)
                project_out(L)

            if stop >= 6:
                norm_sum(8, L, const("ones"), squares_t)
                ffn(L, 1)

            if stop >= 7:
                norm_sum(8, L, const("ones"))
                await_h(1)
                w = panel(8, 16)
                bank = proj_item()
                for j in range(2):
                    for k in range(8):
                        block_ready(k)
                        last = mm(bank[0:8, j * L:(j + 1) * L], w[:, k, 8 * j:8 * j + 8], hT[:, k, 0:L], k == 0, k == 7)
                last.then_inc(s["proj_ready"], 1)
                for n in range(6):
                    w = panel(8, 512)
                    for b in range(4):
                        project(w, slice(b * P, (b + 1) * P), L)
                    if n == 4:
                        await_("dve_for_pe", "dve")
                        for j in range(2):
                            for t in range(2):
                                last = turn(PS[7][:, (2 * j + t) * 8:(2 * j + t + 1) * 8], g_rows[:, j, t * P:(t + 1) * P])
                        last.then_inc(s["pe_for_dve"], 1)
                    if n in (3, 5):
                        for b in range(8):
                            await_("square_ready", "sq")
                            bank = proj_item()
                            nc.tensor.matmul(bank[:, 0:L], const("ones"), g_sq[:, 8 * (n // 5) + b, :], start=True, stop=True)\
                                .then_inc(s["proj_ready"], 1)
                for _ in range(2):
                    w = panel(8, 512)
                    for t in range(2):
                        project_tok(w, t, slice(0, 512), 512)
                await_("dve_for_pe", "dve")
                for h in range(8):
                    if h >= 4:
                        pe.wait_ge(s["pair_ready"], 64 + h - 3)
                    sel = ident[0:8, h:h + 1].to_broadcast([8, P])
                    nc.tensor.matmul(PS[ROW_BANKS[h % 4]][:, :], sel, g_rows[:, :, :], start=True, stop=True)
                    for t in range(2):
                        nc.tensor.matmul(PS[KEY_BANKS[h % 4]][:, t * P:(t + 1) * P], g_x[:, 8 + h, t * P:(t + 1) * P],
                                         g_x[:, 8 + h, t * P:(t + 1) * P], start=True, stop=True)
                    for t in range(2):
                        last = nc.tensor.matmul(PS[KEY_BANKS[h % 4]][:, L + t * P:L + (t + 1) * P], g_x[:, 8 + h, t * P:(t + 1) * P],
                                                g_x[:, h, t * P:(t + 1) * P], start=True, stop=True)
                    last.then_inc(s["score_ready"], 1)
                for h in range(8):
                    pe.wait_ge(s["inv_copied"], h + 1)
                    if h >= 2:
                        pe.wait_ge(s["inv_copied"], 8 + h - 1)
                    for t in range(2):
                        last = turn(PS[4 + h % 2][:, t * P:(t + 1) * P], g_tt[:, h, t * P:(t + 1) * P])
                    last.then_inc(s["inv_ready"], 1)
                CI = 16
                for lev in range(6):
                    for h in range(8):
                        n = lev * 8 + h
                        pe.wait_ge(s["blocks_masked"], n + 1)
                        pe.wait_ge(s["inv_copied"], CI + (lev - 1) * 16 + 8 + h + 1 if lev else 8 + h + 1)
                        if h >= 2:
                            pe.wait_ge(s["inv_copied"], CI + lev * 16 + h - 1)
                        elif lev == 0:
                            pe.wait_ge(s["inv_copied"], 16)
                        for t in range(2):
                            last = nc.tensor.matmul(PS[4 + h % 2][:, t * P:(t + 1) * P], g_mask[:, n % 2, t * P:(t + 1) * P],
                                                    g_t[:, h, t * P:(t + 1) * P], start=True, stop=True)
                        last.then_inc(s["inv_ready"], 1)
                    for h in range(8):
                        pe.wait_ge(s["inv_copied"], CI + lev * 16 + h + 1)
                        if h >= 2:
                            pe.wait_ge(s["inv_copied"], CI + lev * 16 + 8 + h - 1)
                        for t in range(2):
                            o = t * P
                            nc.tensor.matmul(PS[6 + h % 2][:, o:o + P], g_tt[:, h, o:o + P], g_u[:, h, o:o + P],
                                             start=True, stop=True)
                        for t in range(2):
                            o = t * P
                            last = nc.tensor.matmul(PS[6 + h % 2][:, L + o:L + o + P], g_u[:, h, o:o + P], g_tt[:, h, o:o + P],
                                                    start=True, stop=True)
                        last.then_inc(s["inv_ready"], 1)
                pe.wait_ge(s["inv_copied"], CI + 96)

                def turn_head(h):
                    if h >= 2:
                        pe.wait_ge(s["turn_copied"], TC[0] + h - 1)
                    for t in range(2):
                        turn(PS[h % 2][:, t * P:(t + 1) * P], g_x[:, 8 + h, t * P:(t + 1) * P])
                    for t in range(2):
                        last = turn(PS[h % 2][:, L + t * P:L + (t + 1) * P], g_x[:, 16 + h, t * P:(t + 1) * P])
                    last.then_inc(s["turn_ready"], 1)

                turn_head(0)
                turn_head(1)
                for first in range(0, 8, 2):
                    pair = (first, first + 1)
                    for h in pair:
                        g = h % 2
                        pe.wait_ge(s["turn_copied"], TC[0] + h + 1)
                        if h >= 2:
                            pe.wait_ge(s["o_taken"], OT[0] + h - 1)
                        bank = PS[2 + 3 * g]
                        nc.tensor.matmul(bank[:, 0:P], g_tt[:, h, 0:P], g_tok[:, g, 0, :], start=True, stop=True)
                        nc.tensor.matmul(bank[:, P:L], g_tok[:, g, 2, :], g_tt[:, h, P:L], start=True, stop=True)\
                            .then_inc(s["pe_for_dve"], 1)
                    for h in pair:
                        g = h % 2
                        await_("dve_for_pe", "dve")
                        nc.tensor.matmul(PS[3 + 3 * g][:, 0:P], g_tok[:, g, 3, :], g_tok[:, g, 5, :], start=True, stop=True)\
                            .then_inc(s["pe_for_dve"], 1)
                    for h in pair:
                        g = h % 2
                        await_("dve_for_pe", "dve")
                        bank = PS[2 + 3 * g]
                        nc.tensor.matmul(bank[:, L:L + P], g_tt[:, h, P:L], g_tok[:, g, 1, :], start=True, stop=False)
                        nc.tensor.matmul(bank[:, L:L + P], g_tok[:, g, 4, :], g_s[:, g, :], start=False, stop=True)\
                            .then_inc(s["pe_for_dve"], 1)
                        bank = PS[4 + 3 * g]
                        nc.tensor.matmul(bank[:, 0:P], g_att[:, h, 0:P], g_tok[:, g, 5, :], start=True, stop=True)
                        nc.tensor.matmul(bank[:, P:L], g_qd[:, h, :], g_s[:, g, :], start=True, stop=False)
                    if first < 6:
                        turn_head(first + 2)
                        turn_head(first + 3)
                    for h in pair:
                        g = h % 2
                        await_("dve_for_pe", "dve")
                        nc.tensor.matmul(PS[4 + 3 * g][:, P:L], g_att[:, h, P:L], g_tok[:, g, 6, :], start=False, stop=True)\
                            .then_inc(s["o_ready"], 1)
                TC[0] += 8
                OT[0] += 8
                await_("dve_for_pe", "dve")
                for b in range(8):
                    bank = proj_item()
                    for t in range(2):
                        last = turn(bank[:, t * P:(t + 1) * P], g_z[:, t, b * P:(b + 1) * P])
                    last.then_inc(s["proj_ready"], 1)
                pe.wait_ge(s["proj_taken"], c["proj"].n)
                project_out(L)

            if stop >= 8:
                norm_sum(8, L, const("ones"), squares_t)
                await_h(1)
                for t in range(2):
                    for k in range(8):
                        block_ready(k)
                        last = nc.tensor.matmul(PS[7][:, t * NE:(t + 1) * NE], hT[:, k, t * P:(t + 1) * P], rw[:, k, :],
                                                start=k == 0, stop=k == 7)
                last.then_inc(s["pe_for_dve"], 1)
                await_("dve_for_pe", "dve")
                for t in range(2):
                    last = turn(PS[7][0:8, 128 + t * P:128 + (t + 1) * P], r_comb[:, t, :])
                last.then_inc(s["pe_for_dve"], 1)
                for n in range(4):
                    for b in range(4):
                        k = (n % 2) * 4 + b
                        last = turn(PS[n][:, b * P:(b + 1) * P], hT[:, k, (n // 2) * P:(n // 2 + 1) * P])
                last.then_inc(s["pe_for_dve"], 1)
                await_("dve_for_pe", "dve")
                for t in range(2):
                    turn(PS[7][:, 8 * t:8 * t + 8], r_row[:, 2, t * P:(t + 1) * P])
                turn(PS[7][0:1, 16:24], r_row[:, 1, L - 1:L]).then_inc(s["pe_for_dve"], 1)
                pe.wait_ge(s["most_ready"], 1)
                most = pe.value_load(most_i, min_val=0, max_val=L)
                at_start = {n: (x.n, x.i, x.per) for n, x in c.items()}

                def moved_item():
                    n = c["moved"].next()
                    if c["moved"].i is not None or n > 2:
                        pe.wait_ge(s["moved_taken"], c["moved"].ahead(2))
                    return PS[4 + c["moved"].place(2)]

                def gather(j):
                    await_("picks_ready", "picks")
                    for half in range(2):
                        bank = moved_item()
                        for b in range(4):
                            k = half * 4 + b
                            for t in range(2):
                                last = nc.tensor.matmul(bank[:, b * P:(b + 1) * P], h_tok[:, t, k * P:(k + 1) * P],
                                                        pick[:, t, :], start=t == 0, stop=t == 1)
                        last.then_inc(s["moved_ready"], 1)
                    bank = moved_item()
                    for t in range(2):
                        last = turn(bank[:, t * P:(t + 1) * P], pick[:, 2 + t, :])
                    last.then_inc(s["moved_ready"], 1)

                with pe.If(most <= P):
                    gather(0)
                    with turns(pe, NE // 2, panels=(c["panels"], 20), gu=(c["gu"], 12), out=(c["out"], 16),
                               moved=(c["moved"], 14), picks=(c["picks"], 2)):
                        for j in range(2):
                            for q in range(6):
                                nb = 2 if q < 5 else 1
                                w = panel(8, 2 * nb * P)
                                c["gu"].next()
                                pe.wait_ge(s["gu_taken"], c["gu"].ahead(0))
                                if q == 0:
                                    pe.wait_ge(s["moved_taken"], c["moved"].ahead(0))
                                pl = c["gu"].place(2)
                                for bank, off in ((PS[pl], 0), (PS[2 + pl], nb * P)):
                                    for b in range(nb):
                                        for k in range(8):
                                            last = mm(bank[:, b * P:(b + 1) * P], w[:, k, off + b * P:off + (b + 1) * P],
                                                      h_own[:, j, k, :], k == 0, k == 7)
                                last.then_inc(s["gu_ready"], 1)
                            gather(1 - j)
                            pe.wait_ge(s["gu_taken"], c["gu"].ahead(-2))
                            for q in range(4):
                                w = panel(KE, 256)
                                bank = moved_item()
                                for k in range(KE):
                                    last = mm(bank[:, 0:L], e_own[:, k, :], w[:, k, :], k == 0, k == KE - 1)
                                last.then_inc(s["moved_ready"], 1)
                            pe.wait_ge(s["moved_taken"], c["moved"].ahead(0))
                            for m in range(8):
                                bank = out_item()
                                nc.tensor.matmul(bank[:, 0:L], y_own[:, m * P:(m + 1) * P], back[:, j, :],
                                                 start=True, stop=True).then_inc(s["out_ready"], 1)
                for n, x in c.items():
                    x.n, x.i, x.per = at_start[n]
                with pe.Else():
                    for e in range(NE):
                        bank = PS[e // 2]
                        last = nc.tensor.matmul(bank[:, (e % 2) * L:(e % 2) * L + L], ident[0:8, e:e + 1].to_broadcast([8, P]),
                                                r_crow, start=True, stop=True)
                    last.then_inc(s["moved_ready"], 1)
                    pe.wait_ge(s["picks_ready"], 1)
                    with turns(pe, NE // 2, panels=(c["panels"], 20), gu=(c["gu"], 12), out=(c["out"], 16)):
                        for _ in range(2):
                            for q in range(6):
                                nb = 2 if q < 5 else 1
                                w = panel(8, 2 * nb * P)
                                c["gu"].next()
                                pe.wait_ge(s["gu_taken"], c["gu"].ahead(0))
                                pl = c["gu"].place(2)
                                for bank, off in ((PS[pl], 0), (PS[2 + pl], nb * P)):
                                    for b in range(nb):
                                        for k in range(8):
                                            last = mm(bank[:, b * L:(b + 1) * L], w[:, k, off + b * P:off + (b + 1) * P],
                                                      hT[:, k, 0:L], k == 0, k == 7)
                                last.then_inc(s["gu_ready"], 1)
                            pe.wait_ge(s["gu_taken"], c["gu"].ahead(-2))
                            for q in range(4):
                                w = panel(KE, 256)
                                for b in range(2):
                                    bank = out_item()
                                    for k in range(KE):
                                        last = mm(bank[:, 0:L], w[:, k, b * P:(b + 1) * P], e_act[:, k, :], k == 0, k == KE - 1)
                                    last.then_inc(s["out_ready"], 1)
            norm_sum(8, L, const("ones"))
            await_("dve_for_pe", "dve")
            for t in range(2):
                for half in range(2):
                    n = 2 * t + half
                    for b in range(4):
                        last = turn(PS[n][:, b * P:(b + 1) * P], hT[:, half * 4 + b, t * P:(t + 1) * P])
                    last.then_inc(s["x_turned"], 1)

        @block.vector
        def _(dve):
            c = {n: Count() for n in ("ada", "gu", "out", "proj", "sum", "rstd", "scaled", "dve", "act", "pe", "score", "exp",
                                      "turn", "o", "fa", "inv", "step", "st", "ot", "silu", "masked", "pair", "panels", "astep")}
            V = nc.vector

            def link(ins):
                ins.then_inc(s["dve_step"], 1)
                dve.wait_ge(s["dve_step"], c["step"].next())

            def await_(name, stream):
                dve.wait_ge(s[name], c[stream].next())

            def post(ins, name, stream):
                ins.then_inc(s[name], 1)
                dve.wait_ge(s[name], c[stream].next())

            def scale(o, i, by, plus=None, op1=ALU.add):
                if plus is None:
                    return V.tensor_scalar(o, i, by, None, ALU.mult)
                return V.tensor_scalar(o, i, by, plus, ALU.mult, op1)

            def stt(o, a, sc, b, op0=ALU.mult, op1=ALU.add):
                return V.scalar_tensor_tensor(out=o, in0=a, scalar=sc, in1=b, op0=op0, op1=op1)

            def tt(o, a, b, op=ALU.mult):
                return V.tensor_tensor(o, a, b, op)

            def ada_acc(cond, nconds, acc=acc_t):
                m = c["panels"]
                m.next()
                place = m.place(NSLOT)
                fills = (m.n - 1) // NSLOT + 1
                if m.i is not None:
                    fills = m.i * (m.per // NSLOT) + fills
                dve.wait_ge(panel_loaded[place], fills * 32)
                w = slot(place, 8, 512)
                for k in range(8):
                    for j in range(nconds):
                        cc = conds[:, cond + j, k:k + 1]
                        if k == 0:
                            last = V.tensor_scalar(acc[:, j, :], w[:, 0, :], cc, None, ALU.mult)
                        else:
                            last = stt(acc[:, j, :], w[:, k, :], cc, acc[:, j, :])
                        if k < 7:
                            last.then_inc(s["acc_step"], 1)
                            c["astep"].next()
                    if k < 7:
                        dve.wait_ge(s["acc_step"], c["astep"].ahead(0))
                last.then_inc(s["acc_ready"], 1)

            def ada(bias, par, i, nconds=2):
                n = c["ada"]
                await_("ada_ready", "ada")
                bank = PS[4 + n.place(2)][:, 0:8].rearrange("p (a b) -> p a b", a=4)
                cols = mod[:, par, bass.ds(i * 4, 4), 0:nconds] if not isinstance(i, int) else \
                    mod[:, par, i * 4:i * 4 + 4, 0:nconds]
                bc = bias[:, bass.ds(i * 4, 4)] if not isinstance(i, int) else bias[:, i * 4:i * 4 + 4]
                tt(cols, bank[:, :, 0:nconds], bc.unsqueeze(2).to_broadcast([P, 4, nconds]), ALU.add).then_inc(s["ada_taken"], 1)

            def mean(bank, width, n, where=None, add=EPS):
                where = rstd if where is None else where
                link(scale(where[:, 0:width], bank[:, 0:width], 1.0 / n, add))
                V.reciprocal(where[:, 0:width], where[:, 0:width]).then_inc(s["mean_ready"], 1)

            def norm(par, which, weight, parts, final=False):
                await_("sum_ready", "sum")
                mean(PS[3], parts * L, D)
                dve.wait_ge(s["ada_taken"], c["ada"].n)
                if not final:
                    nw = weight.unsqueeze(2).to_broadcast([P, KD, parts])
                    link(stt(gain[:, :, 0:parts], mod[:, par, 24 * which + 8:24 * which + 16, 0:parts], 1.0, nw,
                             ALU.add, ALU.mult))
                await_("rstd_ready", "rstd")
                for k in range(KD):
                    for j in range(parts):
                        t = slice(j * L, (j + 1) * L)
                        g = weight[:, k:k + 1] if final else gain[:, k, j:j + 1]
                        stt(hT[:, k, t], xT[:, k, t], g, rstd[:, t], ALU.mult, ALU.mult).then_inc(s["scaled"], 1)
                        c["scaled"].next()

            def add_out(par, which, parts, m):
                n = c["out"]
                await_("out_ready", "out")
                bank = PS[6 + n.place(2)]
                blk = lambda a, t: a[:, m, t] if isinstance(m, int) else a[:, bass.ds(m, 1), t].squeeze(1)
                for j in range(parts):
                    t = slice(j * L, (j + 1) * L)
                    if isinstance(m, int):
                        xv, gv = xT[:, m, t], mod[:, par, 24 * which + 16 + m, j:j + 1]
                    else:
                        xv = xT[:, bass.ds(m, 1), t]
                        gv = mod[:, par, bass.ds(m + (24 * which + 16), 1), j:j + 1]
                        xv, gv = xv.squeeze(1), gv.squeeze(1)
                    last = stt(xv, bank[:, t], gv, xv)
                last.then_inc(s["out_taken"], 1)

            def add_project_out(par, parts, panels):
                c["panels"].n += panels
                dve.wait_ge(s["ada_taken"], c["ada"].n)
                for m in range(8):
                    add_out(par, 0, parts, m)

            def item(bank_only=False):
                await_("proj_ready", "proj")
                return PS[c["proj"].place(4)]

            def ffn(width, par, bias, cond, nconds, norm_of):
                ada_acc(cond, nconds)
                norm_of()
                ada(bias, 1 - par, 0, nconds)
                nb = T2 // width

                def chunk(i):
                    for it in range(2 // nb):
                        await_("silu_ready", "gu")
                        pl = c["gu"].place(2)
                        f = i * 2 + it * nb
                        o = act_t[:, f:f + nb, 0:width] if isinstance(i, int) else act_t[:, bass.ds(f, nb), 0:width]
                        v = lambda t: t.rearrange("p (a b) -> p a b", a=nb)
                        tt(o, v(silu_t[:, pl, :]), v(PS[2 + pl][:, :])).then_inc(s["gu_taken"], 1)

                with turns(dve, 5, ada=(c["ada"], 2), gu=(c["gu"], 4 // nb), panels=(c["panels"], 4),
                           astep=(c["astep"], 14 * nconds)) as i:
                    for j in range(2):
                        c["panels"].next()
                        ada_acc(cond, nconds)
                        chunk(i * 2 + j)
                        ada(bias, 1 - par, i * 2 + (j + 1), nconds)
                c["panels"].next()
                ada_acc(cond, nconds)
                chunk(10)
                ada(bias, 1 - par, 11, nconds)
                c["panels"].n += 8
                with turns(dve, 2, out=(c["out"], 4)) as i:
                    for j in range(4):
                        add_out(par, 1, T2 // L if width == T2 else 1, i * 4 + j)

            for _ in range(2):
                dve.nop().then_inc(s["gu_taken"], 1)
            dve.wait_ge(s["packs_turned"], 1)
            for g, pack in enumerate(PACKS):
                n = sum(x for _, x in pack)
                V.tensor_copy(pack_cols[:, g, 0:n], PS[6][:, g * P:g * P + n]).then_inc(s["packs_copied"], 1)
            for k in range(8):
                dve.wait_ge(s["x_turned"], k + 1)
                V.tensor_copy(xT[:, k, :], PS[k % 4][:, :]).then_inc(s["x_copied"], 1)
            dve.wait_ge(s["rows_loaded"], NROW * 16)
            V.tensor_scalar(lgam[:, 1, :], lgam[:, 0, :], 256.0, None, ALU.mult).then_inc(s["dve_for_act"], 1)
            V.tensor_scalar(lgam[:, 2, :], lgam[:, 0, :], -1.0, None, ALU.mult).then_inc(s["dve_for_act"], 1)
            c["fa"].n = 2
            dve.wait_ge(s["packs_copied"], 4)
            dve.wait_ge(s["cond_ready"], 4)
            c["panels"].n = 2
            ada_acc(0, 2)
            ada_acc(0, 2, acc_t2)
            for i in range(4):
                ada(col("ada_b", 0, 48), 0, i)
            dve.wait_ge(s["x_copied"], 8)

            def rope(dst, bank, tmp):
                link(tt(tmp[:, 0, :], dst, const("cos")))
                link(tt(tmp[:, 1, :], bank[:, 0:L], const("sin")))
                return tt(dst, tmp[:, 0, :], tmp[:, 1, :], ALU.add)

            if stop >= 1:
                norm(0, 0, col("norm_w", 0, 8), 2)
                V.memset(vext[:, :, :, HD:HD + 1], 1.0)
                bank = item()
                V.tensor_scalar(graw, bank[0:32, :], rowvec[0:32, 32:33], None, ALU.add).then_inc(s["proj_taken"], 1)
                c["panels"].n += 1
                more = [4]

                def ada_next():
                    c["panels"].n += 1
                    ada_acc(0, 2)

                def ada_end():
                    ada(col("ada_b", 0, 48), 0, more[0])
                    more[0] += 1

                for b in range(8):
                    if b % 4 == 0:
                        ada_next()
                    bank = item()
                    V.tensor_copy(qk[:, b, :], bank[:, :]).then_inc(s["proj_taken"], 1)
                    if b % 4 == 3:
                        ada_end()
                dve.wait_ge(s["gates_split"], 64)
                fg, ig = gate[:, 1::2, :], gate[:, 0::2, :]
                post(stt(mrow, fg, -1.0, fg, ALU.mult, ALU.max), "dve_for_act", "fa")

                def rotate(b):
                    bank = item()
                    rope(qk[:, b, 0:L], bank, rope_tmp).then_inc(s["proj_taken"], 1)
                    dve.wait_ge(s["proj_taken"], c["proj"].n)

                ada_next()
                dve.wait_ge(s["proj_taken"], 9)
                for t in range(4):
                    bank = item()
                    V.tensor_copy(tok[:, 0, t, :], bank[:, :]).then_inc(s["proj_taken"], 1)
                    rotate(t)
                ada_end()
                await_("act_for_dve", "act")
                link(stt(fg, fg, 0.0, mrow, ALU.min, ALU.subtract))
                ends = {}
                for d in range(2):
                    prev = None
                    for t in ORDER[d]:
                        a, z = t * P, (t + 1) * P
                        v = (lambda r: r[:, a:z]) if d == 0 else (lambda r: r[:, z - 1:(a - 1 if a else None):-1])
                        e = z - 1 if d == 0 else a
                        link(V.tensor_tensor_scan(v(mrow[:, d, :]), v(gate[:, 2 * d + 1, :]), v(gate[:, 2 * d, :]),
                                                  0.0 if prev is None else mrow[:, d, prev:prev + 1], ALU.add, ALU.max))
                        V.tensor_tensor_scan(v(rrow[:, d, :]), const("ones", (0, 8)), v(gate[:, 2 * d + 1, :]),
                                             0.0, ALU.mult, ALU.add).then_inc(s["dve_step"], 1)
                        c["step"].next()
                        prev = ends[d, t] = e
                dve.wait_ge(s["dve_step"], c["step"].n)
                off = rowvec[0:8, 36:48]
                for d in range(2):
                    for ki in range(3):
                        for qi in range(ki + 1, 4):
                            a = CROSS[d, ki, qi]
                            e = ends[d, ORDER[d][qi - 1]]
                            be = rrow[:, d, e:e + 1]
                            if qi == ki + 1:
                                link(V.tensor_copy(off[:, a:a + 1], be))
                            else:
                                link(tt(off[:, a:a + 1], off[:, a - 1:a], be, ALU.add))
                link(tt(ig, ig, rrow, ALU.subtract))
                link(tt(rrow, rrow, mrow, ALU.subtract))
                for b in range(8):
                    if b % 4 == 0:
                        ada_next()
                    bank = item()
                    w = lambda j: col("mlstm_conv_w", 8 * j + b, 1)
                    x3 = bank[:, :].rearrange("p (a t) -> p a t", a=2)
                    y3 = qk[:, 8 + b, :].rearrange("p (a t) -> p a t", a=2)
                    link(V.tensor_scalar(qk[:, 8 + b, :], bank[:, :], w(1), col("mlstm_conv_b", b, 1), ALU.mult, ALU.add))
                    link(stt(y3[:, :, 1:L], x3[:, :, 0:L - 1], w(0), y3[:, :, 1:L]))
                    stt(y3[:, :, 0:L - 1], x3[:, :, 1:L], w(2), y3[:, :, 0:L - 1]).then_inc(s["proj_taken"], 1)
                    if b % 4 == 3:
                        ada_end()
                ada_next()
                for t in range(4):
                    bank = item()
                    V.tensor_copy(vext[:, t, :, 0:HD], bank[:, :].rearrange("p (h n) -> p h n", h=8)).then_inc(s["proj_taken"], 1)
                    rotate(4 + t)
                ada_end()
                for kind in (1, 2):
                    ada_next()
                    for t in range(4):
                        bank = item()
                        V.tensor_copy(tok[:, kind, t, :], bank[:, :]).then_inc(s["proj_taken"], 1)
                    ada_end()
                for (d, ki, qi), a in CROSS.items():
                    k = ORDER[d][ki]
                    last = V.tensor_scalar(arow[:, a, :], gate[:, 2 * d, k * P:(k + 1) * P], off[:, a:a + 1], None, ALU.add)
                last.then_inc(s["dve_for_pe"], 1)
                await_("pe_for_dve", "pe")
                V.tensor_copy(small[:, 0:224], PS[5][:, 0:224]).then_inc(s["dve_for_act"], 1)
                c["fa"].next()

                def retained(h):
                    dve.wait_ge(s["retain_ready"], h + 1)
                    bank = PS[5 + 2 * (h % 2)][:, 0:L].rearrange("p (t n) -> p t n", t=4)
                    gated = tok[:, 1, :, h * HD:(h + 1) * HD]
                    V.tensor_copy(tok[:, 3, :, h * HD:(h + 1) * HD], bank)
                    tt(gated, bank, gated).then_inc(s["retain_taken"], 1)

                for h in range(8):
                    await_("act_for_dve", "act")
                    strip_same, strip_from, t0, t1, t2 = strips[h % 2]
                    b0, b1, b2 = RET_BANKS[h % 2]
                    rp = rprob[h % 2]
                    link(tt(t0, t0, pconst("is_ahead")))
                    link(tt(t1, t1, pconst("is_behind")))
                    link(tt(strip_same, t0, t1, ALU.add))
                    link(tt(strip_from, strip_from, t2, ALU.add))
                    await_("score_ready", "score")
                    for t in range(2):
                        win = slice(P - P * t, P - P * t + L)
                        stt(rp[:, t * L:(t + 1) * L], PS[b0][:, t * L:(t + 1) * L], HD ** -0.5, strip_same[:, win],
                            ALU.mult, ALU.mult)
                        a = T2 + t * T2
                        bank = PS[(b1, b2)[t]]
                        stt(rp[:, a:a + L], bank[:, 0:L], HD ** -0.5, strip_from[:, win], ALU.mult, ALU.mult)
                        last = stt(rp[:, a + L:a + T2], bank[:, L:T2], HD ** -0.5, strip_same[:, win], ALU.mult, ALU.mult)
                    last.then_inc(s["weight_ready"], 1)
                    if h:
                        retained(h - 1)
                retained(7)
                dve.wait_ge(s["weight_ready"], 8)

                def rows(h, directions):
                    dve.wait_ge(s["rows_ready"], h + 1)
                    for d in directions:
                        V.tensor_copy(rowb[:, 2 * (h % 2) + d, 0, :], PS[3 + d][:, :])
                        m = const("upto" if d == 0 else "from").unsqueeze(1).to_broadcast([P, 4, P])
                        tt(rowb[:, 2 * (h % 2) + d, 1, :].rearrange("p (a t) -> p a t", a=4),
                           PS[3 + d][:, :].rearrange("p (a t) -> p a t", a=4), m, ALU.add).then_inc(s["masked_ready"], 1)

                def taken(n, h, d):
                    dve.wait_ge(s["o_ready"], n + 1)
                    bank = PS[5 + d][:, 0:4 * (HD + 1)].rearrange("p (t n) -> p t n", t=4)
                    den, f = bank[:, :, HD], fl[:, d, :, h]
                    link(stt(f, den, 1.0, f, ALU.mult, ALU.max))
                    link(stt(f, den, -1.0, f, ALU.mult, ALU.max))
                    link(V.reciprocal(f, f))
                    y = tok[:, 0, :, h * HD:(h + 1) * HD]
                    tt(y if d == 0 else y_back, bank[:, :, 0:HD], f.unsqueeze(2).to_broadcast([P, 4, HD]))\
                        .then_inc(s["o_taken"], 1)
                    if d == 1:
                        gated = tok[:, 2, :, h * HD:(h + 1) * HD]
                        dve.wait_ge(s["o_taken"], 2 * h + 2)
                        link(tt(y, y, y_back, ALU.add))
                        tt(gated, gated, y).then_inc(s["head_ready"], 1)

                fl = mcol.rearrange("p (d t h) -> p d t h", d=2, t=4)
                rows(0, (0, 1))
                c["score"].n += 1
                for h in range(8):
                    for g, (d, qi) in enumerate(GROUPS):
                        if g == 0 or (g == 4 and h):
                            await_("score_ready", "score")
                        q = ORDER[d][qi]
                        n = h * 8 + g
                        await_("exp_ready", "exp")
                        if n >= 3:
                            dve.wait_ge(s["o_ready"], n - 2)
                        for ki in range(qi + 1):
                            last = stt(prob[:, n % 3, ki, :], mlstm_scores(h, ORDER[d][ki], q), HD ** -0.5, expo[:, n % 2, ki, :],
                                       ALU.mult, ALU.mult)
                        last.then_inc(s["pair_ready"], 1)
                        if h < 7 and g in (2, 5):
                            rows(h + 1, (int(g == 5),))
                        if g >= 6:
                            taken(n if g == 7 else n - 1, h, g - 6)
                c["o"].n, c["ot"].n = 64, 16
                dve.wait_ge(s["o_taken"], 16)
                dve.wait_ge(s["dve_step"], c["step"].n)
                await_("act_for_dve", "act")
                link(scale(y_ms, y_ms, 1.0 / HD, EPS))
                post(V.reciprocal(y_ms, y_ms), "dve_for_act", "fa")
                await_("act_for_dve", "act")
                for m in range(2):
                    v = tok[:, 1 + m, :, :].rearrange("p t (h n) -> p t h n", h=8)
                    tt(v, v, y_ms[:, m, :, :].unsqueeze(3).to_broadcast([P, 4, 8, HD])).then_inc(s["dve_for_pe"], 1)
                for b in range(8):
                    bank = item()
                    w = col("ret_norm_w", b, 1) if b < 4 else col("mlstm_norm_w", b - 4, 1)
                    V.tensor_scalar(hT[:, b, :], bank[:, :], w, None, ALU.mult).then_inc(s["proj_taken"], 1)
                add_project_out(0, 2, 2)

            if stop >= 2:
                ffn(T2, 0, col("ada_b", 48, 48), 0, 2, lambda: norm(0, 1, col("norm_w", 8, 8), 2))

            mx, nmx, dsum, esink, rec = (a_mx[:, i, :] for i in range(5))

            def attention(items, keys, sink, scaled):
                N = len(items)
                ready0, turn0, o0 = c["st"].n, c["turn"].n, c["o"].n
                for step in range(N + 2):
                    if step < N:
                        h, q = items[step]
                        nk = keys(items[step])
                        await_("score_ready", "score")
                        if step >= 3:
                            dve.wait_ge(s["turn_ready"], turn0 + step - 2)
                        scaled(items[step], step)
                        link(V.reduce_max(mx[:, step:step + 1], a_prob[:, step % 3, 0:nk], X))
                        if sink is not None:
                            link(tt(mx[:, step:step + 1], mx[:, step:step + 1], sink[:, h:h + 1], ALU.max))
                        V.tensor_scalar(nmx[:, step:step + 1], mx[:, step:step + 1], -1.0, None, ALU.mult)\
                            .then_inc(s["max_ready"], 1)
                    if step - 2 >= 0:
                        n = step - 2
                        h, q = items[n]
                        await_("exp_ready", "exp")
                        if sink is not None:
                            link(tt(dsum[:, n:n + 1], dsum[:, n:n + 1], esink[:, n:n + 1], ALU.add))
                        link(V.reciprocal(rec[:, n:n + 1], dsum[:, n:n + 1]))
                        await_("o_ready", "o")
                        V.tensor_scalar(a_y[:, q, h * HD:(h + 1) * HD], PS[4 + n % 2][:, 0:HD], rec[:, n:n + 1], None, ALU.mult)\
                            .then_inc(s["o_taken"], 1)
                        c["ot"].next()
                c["turn"].n += N
                dve.wait_ge(s["o_taken"], c["ot"].n)
                dve.nop().then_inc(s["dve_for_pe"], 1)

            if stop >= 3:
                norm(1, 0, col("norm_w", 16, 8), 2)
                for b in range(8):
                    bank = item()
                    V.tensor_copy(a_q[:, b, :], bank[:, 0:L]).then_inc(s["proj_taken"], 1)
                sq2 = lambda b: a_sq[:, 8 + 2 * b:10 + 2 * b, :].rearrange("p a t -> p (a t)")

                def inverse(b0, b1):
                    V.reciprocal(a_sq[:, b0:b1, :], a_sq[:, b0:b1, :]).then_inc(s["mean_ready"], 1)

                def copy_v(t):
                    bank = item()
                    V.tensor_copy(a_v[:, t, :], bank[:, 0:L]).then_inc(s["proj_taken"], 1)

                def q_normed(b0):
                    await_("rstd_ready", "rstd")
                    for b in range(b0, b0 + 4):
                        stt(a_q[:, b, :], a_q[:, b, :], col("attn_q_norm_w"), a_sq[:, b, :], ALU.mult, ALU.mult)

                for b in range(8):
                    bank = item()
                    scale(a_sq[:, b, :], bank[:, 0:L], 1.0 / HD, EPS).then_inc(s["proj_taken"], 1)
                dve.wait_ge(s["proj_taken"], c["proj"].n)
                for b in range(2):
                    bank = item()
                    V.tensor_copy(a_k2[:, b, :], bank[:, :]).then_inc(s["proj_taken"], 1)
                    inverse(4 * b, 4 * b + 4)
                copy_v(0)
                for b in range(2):
                    bank = item()
                    scale(sq2(b), bank[:, :], 1.0 / HD, EPS).then_inc(s["proj_taken"], 1)
                dve.wait_ge(s["proj_taken"], c["proj"].n)
                for b in range(2):
                    copy_v(1 + b)
                    inverse(8 + 2 * b, 10 + 2 * b)
                    q_normed(4 * b)
                copy_v(3)
                for b in range(2):
                    await_("rstd_ready", "rstd")
                    last = stt(a_k2[:, b, :], a_k2[:, b, :], col("attn_k_norm_w"), sq2(b), ALU.mult, ALU.mult)
                last.then_inc(s["dve_for_pe"], 1)
                for b in range(10):
                    bank = item()
                    dst = a_q[:, b, :] if b < 8 else a_k2[:, b - 8, 0:L]
                    rope(dst, bank, a_rs).then_inc(s["proj_taken"], 1)
                    dve.wait_ge(s["proj_taken"], c["proj"].n)
                for kv in range(4):
                    r = (kv % 2) * HD
                    for half in range(2):
                        last = V.tensor_copy(a_kdup[half * HD:(half + 1) * HD, kv, :], a_k2[r:r + HD, kv // 2, :])
                last.then_inc(s["dve_for_pe"], 1)
                dve.wait_ge(s["phase_loaded"], 32)
                wmask = at(phase0, 2, T2)

                def scaled(it, n):
                    post(stt(a_prob[:, n % 3, :], PS[n % 2][:, :], HD ** -0.5, wmask[:, it[1], :]), "score_taken", "st")

                attention([(h, q) for h in range(16) for q in range(2)], lambda it: T2, rowvec[:, 16:32], scaled)
                for b in range(8):
                    bank = item()
                    V.tensor_copy(hT[:, b, 0:L], bank[:, 0:L]).then_inc(s["proj_taken"], 1)
                add_project_out(1, 1, 5)

            if stop >= 4:
                ffn(L, 1, col("ada_b_2", 0, 48), 2, 1, lambda: norm(1, 1, col("norm_w", 24, 8), 1))

            if stop >= 5:
                norm(0, 0, col("norm_mix_2", 0, 8), 1)
                for b in range(6):
                    bank = item()
                    V.tensor_copy(m_lat[:, b, :], bank[:, 0:L]).then_inc(s["proj_taken"], 1)
                bank = item()
                V.tensor_copy(m_kr[64:96, :], bank[64:96, 0:L]).then_inc(s["proj_taken"], 1)
                for j, n in ((0, Q_LORA), (1, KV_LORA)):
                    bank = item()
                    scale(a_rs[:, j, :], bank[:, 0:L], 1.0 / n, EPS).then_inc(s["proj_taken"], 1)
                dve.wait_ge(s["proj_taken"], c["proj"].n)
                V.reciprocal(a_rs[:, 0:2, :], a_rs[:, 0:2, :]).then_inc(s["mean_ready"], 1)
                await_("rstd_ready", "rstd")
                for b in range(6):
                    w = col("mla_q_norm_2", b, 1) if b < 4 else col("mla_kv_norm_2", b - 4, 1)
                    last = stt(m_lat[:, b, :], m_lat[:, b, :], w, a_rs[:, b // 4, :], ALU.mult, ALU.mult)
                last.then_inc(s["dve_for_pe"], 1)
                R = slice(64, 96)
                ang, kf, cosr = m_cs[R, 0, :], m_cs[R, 1, :], m_cs[R, 2, :]
                ki = m_cs[R, 3, :].bitcast(I32)
                dve.wait_ge(s["rows_loaded"], (NROW + 1) * 16)
                link(V.tensor_copy(ang, pos[R, :].bitcast(I32)))
                link(V.tensor_scalar(ang, ang, const("invf", (64, 96)), None, ALU.mult))
                link(scale(kf, ang, 1.0 / TWO_PI))
                link(V.tensor_copy(ki, kf))
                link(V.tensor_copy(kf, ki))
                for part in TWO_PI_PARTS:
                    link(stt(ang, kf, -part, ang))
                link(V.tensor_scalar(kf, ang, PI, -TWO_PI, ALU.is_gt, ALU.mult))
                link(tt(ang, ang, kf, ALU.add))
                link(V.tensor_scalar(kf, ang, -PI, TWO_PI, ALU.is_lt, ALU.mult))
                link(tt(ang, ang, kf, ALU.add))
                link(V.tensor_scalar(cosr, ang, HALF_PI, None, ALU.add))
                link(V.tensor_scalar(kf, cosr, PI, -TWO_PI, ALU.is_gt, ALU.mult))
                link(tt(cosr, cosr, kf, ALU.add))
                link(V.tensor_scalar(ang, ang, -PI, PI, ALU.max, ALU.min))
                post(V.tensor_scalar(cosr, cosr, -PI, PI, ALU.max, ALU.min), "dve_for_act", "fa")
                await_("act_for_dve", "act")
                bank = item()
                t1 = a_rs[R, 2, :]
                link(tt(t1, bank[R, 0:L], ang))
                link(tt(m_kr[R, :], m_kr[R, :], cosr))
                tt(m_kr[R, :], m_kr[R, :], t1, ALU.add).then_inc(s["proj_taken"], 1)
                dve.wait_ge(s["proj_taken"], c["proj"].n)
                V.tensor_copy(a_k[R, :, :], m_kr[R, :].unsqueeze(1).to_broadcast([32, 16, L]))

                def rotated(b):
                    bank = item()
                    q2 = a_q[R, 2 * b:2 * b + 2, :]
                    t2 = a_rs[R, 2:4, :]
                    bc = lambda v: v.unsqueeze(1).to_broadcast([32, 2, L])
                    dve.wait_ge(s["proj_taken"], c["proj"].n - 1)
                    link(tt(t2, bank[R, :].rearrange("p (a t) -> p a t", a=2), bc(ang)))
                    link(tt(q2, q2, bc(cosr)))
                    tt(q2, q2, t2, ALU.add).then_inc(s["proj_taken"], 1)

                for h in range(16):
                    bank = item()
                    V.tensor_copy(a_q[0:96, h, :], bank[0:96, 0:L]).then_inc(s["proj_taken"], 1)
                    if h % 2 and h >= 3:
                        rotated((h - 3) // 2)
                rotated(7)
                for h in range(16):
                    bank = item()
                    V.tensor_copy(a_k[0:HD, h, :], bank[0:HD, 0:L]).then_inc(s["proj_taken"], 1)
                for t in range(2):
                    for half in range(2):
                        bank = item()
                        V.tensor_copy(m_v[:, t, half * 512:(half + 1) * 512], bank[:, :]).then_inc(s["proj_taken"], 1)
                dve.wait_ge(s["proj_taken"], c["proj"].n)
                dve.nop().then_inc(s["dve_for_pe"], 1)
                SC = (64 + 32) ** -0.5

                def scaled_m(it, n):
                    if it[1]:
                        scale(a_prob[:, n % 3, 0:P], PS[n % 2][:, 0:P], SC)
                    a = it[1] * P
                    post(stt(a_prob[:, n % 3, a:a + P], PS[n % 2][:, a:a + P], SC, const("from")), "score_taken", "st")

                attention([(h, q) for h in range(16) for q in range(2)], lambda it: (it[1] + 1) * P, None, scaled_m)
                for b in range(8):
                    bank = item()
                    V.tensor_copy(hT[:, b, 0:L], bank[:, 0:L]).then_inc(s["proj_taken"], 1)
                add_project_out(0, 1, 7)

            if stop >= 6:
                ffn(L, 0, col("ada_b_2", 48, 48), 2, 1, lambda: norm(0, 1, col("norm_ffn_2", 0, 8), 1))

            if stop >= 7:
                norm(1, 0, col("norm_mix_2", 8, 8), 1)
                bank = item()
                V.tensor_copy(g_rows.rearrange("p a t -> p (a t)"), bank[0:8, :]).then_inc(s["proj_taken"], 1)
                dve.wait_ge(s["proj_taken"], c["proj"].n)
                beta_raw, a_raw = g_rows[:, 0, :], g_rows[:, 1, :]
                xx, ab, gg = (g_row2[:, i, :] for i in range(3))
                link(V.tensor_scalar(xx, a_raw, rowvec[0:8, 34:35], None, ALU.add))
                post(stt(ab, xx, -1.0, xx, ALU.mult, ALU.max), "dve_for_act", "fa")
                await_("act_for_dve", "act")
                link(stt(xx, xx, 0.0, ab, ALU.max, ALU.add))
                link(V.tensor_scalar(xx, xx, rowvec[0:8, 35:36], -1.0, ALU.mult, ALU.mult))
                for t in range(2):
                    link(V.tensor_tensor_scan(g_rows[:, 0, t * P:(t + 1) * P], const("ones", (0, 8)),
                                              xx[:, t * P:(t + 1) * P], 0.0, ALU.mult, ALU.add))
                V.tensor_copy(g_rows[:, 1, :], gg).then_inc(s["dve_for_pe"], 1)

                def tap(b):
                    bank = item()
                    await_("act_for_dve", "act")
                    acc = g_acc[:, b % 4, :]
                    w = lambda j: col("gdn_conv_w_2", 24 * j + b, 1)
                    link(stt(acc[:, 1:L], bank[:, 0:L - 1], w(2), acc[:, 1:L]))
                    link(stt(acc[:, 2:L], bank[:, 0:L - 2], w(1), acc[:, 2:L]))
                    stt(acc[:, 3:L], bank[:, 0:L - 3], w(0), acc[:, 3:L]).then_inc(s["proj_taken"], 1)

                def square_sums(b0):
                    for b in range(b0, b0 + 8):
                        bank = item()
                        V.tensor_scalar(g_sq[:, b, :], bank[:, 0:L], EPS, None, ALU.add).then_inc(s["proj_taken"], 1)
                    dve.wait_ge(s["proj_taken"], c["proj"].n)

                for b in range(16):
                    tap(b)
                square_sums(0)
                for b in range(8):
                    tap(16 + b)
                    last = V.reciprocal(g_sq[:, b, :], g_sq[:, b, :])
                last.then_inc(s["mean_ready"], 1)
                square_sums(8)
                await_("pe_for_dve", "pe")
                gcols = small[:, 0:32]
                link(V.tensor_copy(gcols, PS[7][:, 0:32]))
                post(V.tensor_scalar(small[:, 32:48], gcols[:, 0:16], -1.0, None, ALU.mult), "dve_for_act", "fa")
                for half in range(2):
                    for t in range(2):
                        bank = item()
                        V.tensor_copy(g_z[:, t, half * 512:(half + 1) * 512], bank[:, :]).then_inc(s["proj_taken"], 1)
                        k0 = 8 + 4 * half + 2 * t
                        last = V.reciprocal(g_sq[:, k0:k0 + 2, :], g_sq[:, k0:k0 + 2, :])
                    last.then_inc(s["mean_ready"], 1)
                    if half == 0:
                        await_("rstd_ready", "rstd")
                        stt(g_x[:, 0:8, :], g_x[:, 0:8, :], P ** -0.5, g_sq[:, 0:8, :], ALU.mult, ALU.mult)
                for k0 in (8, 12):
                    await_("rstd_ready", "rstd")
                    last = tt(g_x[:, k0:k0 + 4, :], g_x[:, k0:k0 + 4, :], g_sq[:, k0:k0 + 4, :])
                last.then_inc(s["dve_for_pe"], 1)
                b3 = lambda v: v.unsqueeze(1).to_broadcast([P, 2, P])
                r3 = lambda v: v.rearrange("p (a t) -> p a t", a=2)

                def gmask(h):
                    await_("score_ready", "score")
                    if h >= 2:
                        dve.wait_ge(s["pair_ready"], 64 + h - 1)
                    V.tensor_copy(g_tmp[:, h % 2, 2, P:L], PS[ROW_BANKS[h % 4]][:, P:L])
                    tt(r3(g_tmp[:, h % 2, 0, :]), r3(PS[ROW_BANKS[h % 4]][:, 0:L]), b3(const("upto")), ALU.add)\
                        .then_inc(s["masked_ready"], 1)

                gmask(0)
                for h in range(8):
                    await_("exp_ready", "exp")
                    if h < 7:
                        gmask(h + 1)
                    g = h % 2
                    et, tm = g_tmp[:, g, 1, :], g_tmp[:, g, 0, :]
                    rows_of, keys_of = PS[ROW_BANKS[h % 4]], PS[KEY_BANKS[h % 4]]
                    tt(g_att[:, h, :], keys_of[:, L:T2], et)
                    link(tt(tm, keys_of[:, 0:L], et))
                    link(tt(tm, tm, rows_of[:, L:T2]))
                    tt(r3(g_at[:, h, :]), r3(tm), b3(const("before")))
                    tt(g_qd[:, h, :], g_x[:, h, P:L], g_tmp[:, g, 2, 0:P])
                    tt(small[:, 80 + h:81 + h], rows_of[:, P - 1:P], gcols[:, h:h + 1], ALU.subtract).then_inc(s["pair_ready"], 1)
                dve.wait_ge(s["pair_ready"], c["pair"].n + 72)
                dve.wait_ge(s["phase_loaded"], 48)
                for h in range(8):
                    tm = g_tmp[:, h % 2, 0, :]
                    link(tt(r3(tm), r3(g_at[:, h, :]), b3(imask(0))))
                    stt(r3(g_tt[:, h, :]), r3(tm), -1.0, b3(ident)).then_inc(s["inv_copied"], 1)
                for h in range(8):
                    await_("inv_ready", "inv")
                    V.tensor_copy(g_t[:, h, :], PS[4 + h % 2][:, 0:L]).then_inc(s["inv_copied"], 1)
                for lev in range(6):
                    for h in range(8):
                        await_("inv_ready", "inv")
                        V.tensor_copy(g_u[:, h, :], PS[4 + h % 2][:, 0:L]).then_inc(s["inv_copied"], 1)
                    for h in range(8):
                        await_("inv_ready", "inv")
                        tt(g_t[:, h, :], g_t[:, h, :], PS[6 + h % 2][:, 0:L], ALU.subtract)
                        tt(g_tt[:, h, :], g_tt[:, h, :], PS[6 + h % 2][:, L:T2], ALU.subtract).then_inc(s["inv_copied"], 1)
                await_("act_for_dve", "act")
                link(tt(small[:, 64:80], small[:, 64:80], gcols[:, 16:32]))
                for first in range(0, 8, 2):
                    pair = (first, first + 1)
                    for h in pair:
                        await_("turn_ready", "turn")
                        g = h % 2
                        for j, (o, sc) in enumerate(((L, gcols[:, 16 + h:17 + h]), (L + P, gcols[:, 24 + h:25 + h]),
                                                     (P, small[:, 72 + h:73 + h]), (0, small[:, 80 + h:81 + h]))):
                            last = V.tensor_scalar(g_tok[:, g, j, :], PS[g][:, o:o + P], sc, None, ALU.mult)
                        last.then_inc(s["turn_copied"], 1)
                    for h in pair:
                        g = h % 2
                        await_("pe_for_dve", "pe")
                        V.tensor_copy(g_tok[:, g, 5, :], PS[2 + 3 * g][:, 0:P])
                        V.tensor_scalar(g_tok[:, g, 4, :], PS[2 + 3 * g][:, P:L], -1.0, None, ALU.mult)\
                            .then_inc(s["dve_for_pe"], 1)
                    for h in pair:
                        await_("pe_for_dve", "pe")
                        V.tensor_copy(g_s[:, h % 2, :], PS[3 + 3 * (h % 2)][:, 0:P]).then_inc(s["dve_for_pe"], 1)
                    for h in pair:
                        await_("pe_for_dve", "pe")
                        V.tensor_copy(g_tok[:, h % 2, 6, :], PS[2 + 3 * (h % 2)][:, L:L + P]).then_inc(s["dve_for_pe"], 1)
                    for h in pair:
                        await_("o_ready", "o")
                        bank, gated = r3(PS[4 + 3 * (h % 2)][:, 0:L]), g_z[:, :, h * P:(h + 1) * P]
                        V.tensor_copy(g_o[:, :, h * P:(h + 1) * P], bank)
                        tt(gated, bank, gated).then_inc(s["o_taken"], 1)
                        c["ot"].next()
                rs = small[:, 96:112]
                await_("act_for_dve", "act")
                link(scale(rs, rs, 1.0 / P, EPS))
                post(V.reciprocal(rs, rs), "dve_for_act", "fa")
                await_("act_for_dve", "act")
                z3 = g_z.rearrange("p t (h n) -> p (t h) n", n=P)
                tt(z3, z3, rs.unsqueeze(2).to_broadcast([P, 16, P])).then_inc(s["dve_for_pe"], 1)
                for b in range(8):
                    bank = item()
                    V.tensor_scalar(hT[:, b, 0:L], bank[:, 0:L], col("gdn_out_norm_2"), None, ALU.mult).then_inc(s["proj_taken"], 1)
                add_project_out(1, 1, 11)

            if stop >= 8:
                norm(1, 1, col("norm_ffn_2", 8, 8), 1)
                await_("pe_for_dve", "pe")
                lg = r_tmp[:, 0:16].rearrange("p (t e) -> p t e", t=2)
                link(V.tensor_copy(r_tmp[:, 0:16], PS[7][:, 0:16]))
                m1, sel, rank, tot = r_tmp[:, 16:18], r_tmp[:, 32:48], r_tmp[:, 48:64], r_tmp[:, 64:66]
                link(V.tensor_reduce(m1, lg, X, ALU.max))
                for t in range(2):
                    gt, eq = r_tmp[:, 128:192], r_tmp[:, 192:256]
                    v = lambda z: z.rearrange("p (a b) -> p a b", a=8)
                    other, own = lg[:, t, :].unsqueeze(1).to_broadcast([P, 8, 8]), lg[:, t, :].unsqueeze(2).to_broadcast([P, 8, 8])
                    link(tt(v(gt), other, own, ALU.is_gt))
                    link(tt(v(eq), other, own, ALU.is_equal))
                    link(tt(eq, eq, const("earlier")))
                    link(tt(gt, gt, eq, ALU.add))
                    link(V.tensor_reduce(rank[:, t * 8:t * 8 + 8], v(gt), X, ALU.add))
                link(V.tensor_scalar(sel, rank, 1.5, None, ALU.is_lt))
                post(tt(lg, lg, m1.unsqueeze(2).to_broadcast([P, 2, NE]), ALU.subtract), "dve_for_act", "fa")
                await_("act_for_dve", "act")
                link(tt(sel, sel, r_tmp[:, 0:16]))
                s3 = sel.rearrange("p (t e) -> p t e", t=2)
                link(V.tensor_reduce(tot, s3, X, ALU.add))
                link(V.reciprocal(tot, tot))
                tt(r_comb, s3, tot.unsqueeze(2).to_broadcast([P, 2, NE])).then_inc(s["dve_for_pe"], 1)
                await_("pe_for_dve", "pe")
                link(V.tensor_copy(r_crow, PS[7][0:8, 128:128 + L]))
                own, count, slot_of = (r_row[:, i, :] for i in range(3))
                link(V.tensor_scalar(own, r_crow, 0.0, None, ALU.is_gt))
                link(V.tensor_tensor_scan(count, const("ones", (0, 8))[:, 0:1].to_broadcast([8, L]), own, 0.0, ALU.mult, ALU.add))
                link(tt(slot_of, count, own))
                V.tensor_scalar(slot_of, slot_of, -1.0, None, ALU.add).then_inc(s["dve_for_pe"], 1)
                V.memset(slots, -1.0)
                V.memset(weights, 0.0).then_inc(s["dve_step"], 1)
                c["step"].next()
                await_("pe_for_dve", "pe")
                for n in range(4):
                    V.tensor_copy(h_tok[:, n // 2, (n % 2) * 512:(n % 2 + 1) * 512], PS[n][:, :])
                dve.wait_ge(s["dve_step"], c["step"].n)
                V.tensor_copy(weights[:, 0:NE, :].rearrange("p e t -> p t e"), r_comb)
                await_("pe_for_dve", "pe")
                V.tensor_copy(slots[:, 0:NE, :].rearrange("p e t -> p t e"), PS[7][:, 0:16].rearrange("p (t e) -> p t e", t=2))
                link(V.tensor_reduce(most_f[:, 0:1], PS[7][0:1, 16:24], X, ALU.max))
                V.tensor_copy(most_i, most_f[:, 0:1]).then_inc(s["most_ready"], 1)
                dve.wait_ge(s["most_ready"], 1)
                most = dve.value_load(most_i, min_val=0, max_val=L)
                at_start = {n: (x.n, x.i, x.per) for n, x in c.items()}

                def picks(e):
                    for t in range(2):
                        sl, wt = (v[:, bass.ds(e, 1), t:t + 1].squeeze(1) if not isinstance(e, int) else v[:, e, t:t + 1]
                                  for v in (slots, weights))
                        V.tensor_scalar(pick[:, t, :], imask(7), sl, None, ALU.is_equal)
                        last = V.tensor_scalar(pick[:, 2 + t, :], imask(7), sl, wt, ALU.is_equal, ALU.mult)
                    last.then_inc(s["picks_ready"], 1)

                with dve.If(most <= P):
                    picks(0)
                    with turns(dve, NE // 2, gu=(c["gu"], 12), out=(c["out"], 16)) as i:
                        for j in range(2):
                            for q in range(6):
                                nb = 2 if q < 5 else 1
                                await_("silu_ready", "gu")
                                pl = c["gu"].place(2)
                                v = lambda z: z.rearrange("p (a b) -> p a b", a=nb)
                                tt(e_own[:, 2 * q:2 * q + nb, :], v(e_silu[:, pl, 0:nb * P]), v(PS[2 + pl][:, 0:nb * P]))\
                                    .then_inc(s["gu_taken"], 1)
                                if q == 0:
                                    picks(i * 2 + (j + 1))
                            for m in range(8):
                                add_out(1, 1, 1, m)
                for n, x in c.items():
                    x.n, x.i, x.per = at_start[n]
                with dve.Else():
                    dve.wait_ge(s["moved_ready"], 1)
                    for b in range(4):
                        last = V.tensor_copy(e_row[:, 2 * b:2 * b + 2, :].rearrange("p a t -> p (a t)"), PS[b][:, :])
                    last.then_inc(s["picks_ready"], 1)
                    dve.wait_ge(s["picks_ready"], 1)
                    with turns(dve, NE // 2, gu=(c["gu"], 12), out=(c["out"], 16), astep=(c["astep"], 12)) as i:
                        for j in range(2):
                            e = i * 2 + j
                            for q in range(6):
                                nb = 2 if q < 5 else 1
                                await_("silu_ready", "gu")
                                pl = c["gu"].place(2)
                                v = lambda z: z.rearrange("p (a b) -> p a b", a=nb)
                                sv = v(e_silu[:, pl, 0:nb * L])
                                tt(sv, sv, e_row[:, bass.ds(e, 1), :].to_broadcast([P, nb, L])).then_inc(s["acc_step"], 1)
                                dve.wait_ge(s["acc_step"], c["astep"].next())
                                tt(e_act[:, 2 * q:2 * q + nb, :], sv, v(PS[2 + pl][:, 0:nb * L])).then_inc(s["gu_taken"], 1)
                            for m in range(8):
                                add_out(1, 1, 1, m)
            dve.wait_ge(s["out_taken"], c["out"].n)
            norm(0, 0, col("final_norm_2"), 1, final=True)
            dve.wait_ge(s["scaled"], c["scaled"].n)
            dve.nop().then_inc(s["dve_for_pe"], 1)
            for n in range(4):
                dve.wait_ge(s["x_turned"], 8 + n + 1)
                V.tensor_copy(work(0, 2, D)[:, n // 2, (n % 2) * 512:(n % 2 + 1) * 512], PS[n][:, :]).then_inc(s["final_copied"], 1)

        @block.scalar
        def _(act):
            c = {n: Count() for n in ("gu", "out", "proj", "mean", "scaled", "h", "fa", "exp", "max", "turn", "o", "tr", "pair", "step", "moved")}
            ac = lambda o, i, f, **k: nc.scalar.activation(o, i, f, **k)

            def await_(name, stream):
                act.wait_ge(s[name], c[stream].next())

            def link(ins):
                ins.then_inc(s["act_step"], 1)
                act.wait_ge(s["act_step"], c["step"].next())

            def squares(width, dst):
                for k in range(KD):
                    if c["out"].n:
                        act.wait_ge(s["out_taken"], c["out"].n - 7 + k)
                    else:
                        act.wait_ge(s["x_copied"], k + 1)
                    ac(dst[:, k, 0:width], xT[:, k, 0:width], ACT.Square).then_inc(s["square_ready"], 1)

            def root(v, width=None):
                await_("mean_ready", "mean")
                ac(v, v, ACT.Sqrt).then_inc(s["rstd_ready"], 1)

            def norm(par, which, parts):
                squares(parts * L, squares_t if which else hT)
                root(rstd[:, 0:parts * L])
                for k in range(KD):
                    for j in range(parts):
                        await_("scaled", "scaled")
                        v = hT[:, k, j * L:(j + 1) * L]
                        ac(v, v, ACT.Identity, bias=mod[:, par, 24 * which + k, j:j + 1]).then_inc(s["h_ready"], 1)

            def ffn(width):
                nb = T2 // width

                def chunk():
                    for _ in range(2 // nb):
                        await_("gu_ready", "gu")
                        act.wait_ge(s["gu_taken"], c["gu"].ahead(0))
                        pl = c["gu"].place(2)
                        ac(silu_t[:, pl, :], PS[pl][:, :], ACT.Silu).then_inc(s["silu_ready"], 1)

                with turns(act, 5, gu=(c["gu"], 4 // nb)):
                    chunk()
                    chunk()
                chunk()
                c["out"].n += 8

            act.dma_start(at(const0, NCONST), A["consts"]).then_inc(s["const_loaded"], 16)
            nvec = 0
            for g, r, src in vector_rows():
                act.dma_start(pack_rows[r:r + src.shape[0], g, 0:src.shape[1]] if src.shape[1] == P else
                              pack_rows[r:r + 1, g, :].rearrange("a (b n) -> a b n", b=2)[:, 0, :], src)\
                    .then_inc(s["vectors_loaded"], 16)
                if src.shape[1] != P:
                    act.dma_start(pack_rows[r:r + 1, g, HD:P], src).then_inc(s["vectors_loaded"], 16)
            act.dma_start(at(phase0, NPHASE_A), A["phase_a"]).then_inc(s["phase_loaded"], 16)
            with nc.allow_non_contiguous_dma(reason="a few small vectors"):
                act.dma_start(lgam[:, 0, :], A["ret_log_gamma"].rearrange("a d h -> a (d h)").to_broadcast([P, 16])).then_inc(s["rows_loaded"], 16)
                act.dma_start(rowvec[:, 16:32], A["attn_sink"].to_broadcast([P, 16])).then_inc(s["rows_loaded"], 16)
                act.dma_start(rowvec[0:32, 32:33], A["mlstm_gate_b"].rearrange("a k h -> (k h) a")).then_inc(s["rows_loaded"], 16)
                act.dma_start(rowvec[0:8, 33:34], A["gdn_a_log_2"].rearrange("a h -> h a")).then_inc(s["rows_loaded"], 16)
                act.dma_start(rowvec[0:8, 34:35], A["gdn_dt_bias_2"].rearrange("a h -> h a")).then_inc(s["rows_loaded"], 16)
                act.dma_start(rw, A["moe_w_router_2"][0].rearrange("(k p) n -> p k n", p=P)).then_inc(s["rows_loaded"], 16)
            act.wait_ge(s["packs_copied"], 1)
            for i, name in enumerate(("c", "c_ctx", "c_2", "c_2")):
                ac(conds[:, i, :], col(name), ACT.Silu).then_inc(s["cond_ready"], 1)

            if stop >= 1:
                norm(0, 0, 2)
                act.wait_ge(s["proj_taken"], 1)
                for k in range(4):
                    act.dma_start(gate[:, k, :], graw[8 * k:8 * k + 8, :]).then_inc(s["gates_split"], 16)
                act.wait_ge(s["dve_for_act"], 3)
                c["fa"].n = 3
                link(ac(mrow, mrow, ACT.Exp, scale=-1.0))
                ac(mrow, mrow, ACT.Ln, bias=1.0).then_inc(s["act_for_dve"], 1)
                act.wait_ge(s["proj_taken"], 25)
                for b in range(4):
                    v = qk[:, 8 + 2 * b:10 + 2 * b, :]
                    last = ac(v, v, ACT.Silu)
                last.then_inc(s["act_for_pe"], 1)
                act.wait_ge(s["proj_taken"], 41)
                for t in range(2):
                    v = tok[:, 1, 2 * t:2 * t + 2, :]
                    ac(v, v, ACT.Silu)
                for t in range(2):
                    v = tok[:, 2, 2 * t:2 * t + 2, :]
                    ac(v, v, ACT.Sigmoid)
                await_("dve_for_act", "fa")
                link(ac(mcol, mcol, ACT.Exp, scale=-1.0))
                act.wait_ge(s["phase_loaded"], 16)

                def head_squares(m, h):
                    for t in range(4):
                        v = tok[:, (3, 0)[m], t, h * HD:(h + 1) * HD]
                        last = ac(v, v, ACT.Square, accum_out=y_ms[:, m, t, h:h + 1])
                    return last

                for h in range(8):
                    if h >= 2:
                        act.wait_ge(s["weight_ready"], h - 1)
                    _, strip_from, *strip_tmp = strips[h % 2]
                    f, b = slice(h, h + 1), slice(8 + h, 9 + h)
                    ac(strip_tmp[0], pconst("ahead"), ACT.Exp, scale=lgam[:, 0, f])
                    ac(strip_tmp[1], pconst("behind"), ACT.Exp, scale=lgam[:, 0, b])
                    ac(strip_from, pconst("dist"), ACT.Exp, scale=lgam[:, 0, f], bias=lgam[:, 1, f])
                    ac(strip_tmp[2], pconst("dist"), ACT.Exp, scale=lgam[:, 2, b], bias=lgam[:, 1, b])\
                        .then_inc(s["act_for_dve"], 1)
                    if h >= 2:
                        act.wait_ge(s["retain_taken"], h - 1)
                        head_squares(0, h - 2)
                for h in (6, 7):
                    act.wait_ge(s["retain_taken"], h + 1)
                    head_squares(0, h)
                for h in range(8):
                    for g, (d, qi) in enumerate(GROUPS):
                        if g == 4 and h:
                            act.wait_ge(s["head_ready"], h)
                            head_squares(1, h - 1)
                        n = h * 8 + g
                        q = ORDER[d][qi]
                        act.wait_ge(s["masked_ready"], 2 * h + d + 1)
                        if n >= 2:
                            act.wait_ge(s["pair_ready"], n - 1)
                        for ki in range(qi + 1):
                            k = ORDER[d][ki]
                            a = 4 * d + k if ki == qi else 8 + CROSS[d, ki, qi]
                            src = rowb[:, 2 * (h % 2) + d, int(ki == qi), q * P:(q + 1) * P]
                            last = ac(expo[:, n % 2, ki, :], src, ACT.Exp, bias=acol[:, a, h:h + 1])
                        last.then_inc(s["exp_ready"], 1)
                act.wait_ge(s["head_ready"], 8)
                head_squares(1, 7).then_inc(s["act_for_dve"], 1)
                await_("dve_for_act", "fa")
                ac(y_ms, y_ms, ACT.Sqrt).then_inc(s["act_for_dve"], 1)
                c["out"].n += 8

            if stop >= 2:
                norm(0, 1, 2)
                ffn(T2)

            def attention(N, sink, width):
                turn0, o0 = c["turn"].n, c["o"].n
                for step in range(N + 1):
                    if step < N:
                        h = step // 2
                        await_("max_ready", "max")
                        v = a_prob[:, step % 3, 0:width(step)]
                        last = ac(v, v, ACT.Exp, bias=a_mx[:, 1, step:step + 1], accum_out=a_mx[:, 2, step:step + 1])
                        if sink is not None:
                            last = ac(a_mx[:, 3, step:step + 1], sink[:, h:h + 1], ACT.Exp, bias=a_mx[:, 1, step:step + 1])
                        last.then_inc(s["exp_ready"], 1)
                    if step >= 1:
                        n = step - 1
                        await_("turn_ready", "turn")
                        if n >= 3:
                            act.wait_ge(s["o_ready"], c["o"].n + n - 2)
                        w = width(n) // P
                        ac(a_turn[:, n % 3, 0:w, :].rearrange("p a b -> p (a b)"), PS[2 + n % 2][:, 0:width(n)], ACT.Copy)\
                            .then_inc(s["turn_copied"], 1)
                c["o"].n += N

            c["o"].n = 64
            if stop >= 3:
                norm(1, 0, 2)
                act.dma_start(at(phase0, NPHASE_B), A["phase_b"]).then_inc(s["phase_loaded"], 16)
                c["proj"].n = 49
                for b in range(8):
                    act.wait_ge(s["proj_taken"], 49 + b + 1)
                    ac(a_sq[:, b, :], a_q[:, b, :], ACT.Square).then_inc(s["square_ready"], 1)
                for b in range(2):
                    act.wait_ge(s["proj_taken"], 49 + 16 + b + 1)
                    ac(a_sq[:, 8 + 2 * b:10 + 2 * b, :].rearrange("p a t -> p (a t)"), a_k2[:, b, :], ACT.Square)\
                        .then_inc(s["square_ready"], 1)
                for b0, b1 in ((0, 4), (4, 8), (8, 10), (10, 12)):
                    root(a_sq[:, b0:b1, :])
                attention(32, rowvec[:, 16:32], lambda n: T2)
                c["out"].n += 8

            if stop >= 4:
                norm(1, 1, 1)
                ffn(L)

            if stop >= 5:
                norm(0, 0, 1)
                act.dma_start(pos[64:96, :].bitcast(I32), A["positions_2"].to_broadcast([32, L])).then_inc(s["rows_loaded"], 16)
                for b in range(6):
                    act.wait_ge(s["proj_taken"], 91 + b + 1)
                    ac(a_sq[:, b, :], m_lat[:, b, :], ACT.Square).then_inc(s["square_ready"], 1)
                root(a_rs[:, 0:2, :])
                await_("dve_for_act", "fa")
                for j in (0, 2):
                    v = m_cs[64:96, j, :]
                    last = ac(v, v, ACT.Sin)
                last.then_inc(s["act_for_dve"], 1)
                attention(32, None, lambda n: (n % 2 + 1) * P)
                c["out"].n += 8

            if stop >= 6:
                norm(0, 1, 1)
                ffn(L)

            if stop >= 7:
                norm(1, 0, 1)
                act.dma_start(at(phase0, NPHASE_G), A["phase_g"]).then_inc(s["phase_loaded"], 16)
                await_("dve_for_act", "fa")
                ab = g_row2[:, 1, :]
                ac(g_row2[:, 2, :], g_rows[:, 0, :], ACT.Sigmoid)
                ac(rowvec[0:8, 35:36], rowvec[0:8, 33:34], ACT.Exp)
                link(ac(ab, ab, ACT.Exp, scale=-1.0))
                ac(ab, ab, ACT.Ln, bias=1.0).then_inc(s["act_for_dve"], 1)
                p0 = NPROJ["gdn"] + 1

                def tap_silu(b):
                    act.wait_ge(s["proj_taken"], p0 + b + 1 + (8 if b >= 16 else 0))
                    ac(g_x[:, b, :], g_acc[:, b % 4, :], ACT.Silu).then_inc(s["act_step"], 1)
                    c["step"].next()

                for b in range(24 + 2):
                    if b < 24:
                        act.wait_ge(s["proj_ready"], p0 + b + 1 + (8 if b >= 16 else 0))
                        if b >= 4:
                            act.wait_ge(s["act_step"], c["step"].n - 1)
                        ac(g_acc[:, b % 4, :], PS[(p0 + b) % 4][:, 0:L], ACT.Identity, scale=col("gdn_conv_w_2", 72 + b, 1))\
                            .then_inc(s["act_for_dve"], 1)
                    if b >= 2:
                        tap_silu(b - 2)
                    if 3 <= b < 19:
                        act.wait_ge(s["act_step"], c["step"].n - 1)
                        ac(g_sq[:, b - 3, :], g_x[:, b - 3, :], ACT.Square).then_inc(s["square_ready"], 1)
                root(g_sq[:, 0:8, :])
                root(g_sq[:, 8:12, :])
                root(g_sq[:, 12:16, :])
                act.wait_ge(s["proj_taken"], p0 + 44)
                for t in range(2):
                    ac(g_z[:, t, :], g_z[:, t, :], ACT.Silu)
                await_("dve_for_act", "fa")
                for h in range(8):
                    act.wait_ge(s["masked_ready"], 16 + h + 1)
                    if h >= 2:
                        act.wait_ge(s["pair_ready"], 64 + h - 1)
                    g = h % 2
                    for t in range(2):
                        ac(g_tmp[:, g, 1, t * P:(t + 1) * P], g_tmp[:, g, 0, t * P:(t + 1) * P], ACT.Exp,
                           bias=small[:, 32 + 8 * t + h:33 + 8 * t + h])
                    ac(g_tmp[:, g, 2, 0:P], g_tmp[:, g, 2, P:L], ACT.Exp).then_inc(s["exp_ready"], 1)
                ac(small[:, 64:80], small[:, 0:16], ACT.Exp)
                act.wait_ge(s["pair_ready"], 64 + 8)
                ac(small[:, 80:88], small[:, 80:88], ACT.Exp).then_inc(s["act_for_dve"], 1)
                for h in range(8):
                    act.wait_ge(s["o_taken"], 80 + h + 1)
                    for t in range(2):
                        v = g_o[:, t, h * P:(h + 1) * P]
                        last = ac(v, v, ACT.Square, accum_out=small[:, 96 + 8 * t + h:97 + 8 * t + h])
                last.then_inc(s["act_for_dve"], 1)
                await_("dve_for_act", "fa")
                ac(small[:, 96:112], small[:, 96:112], ACT.Sqrt).then_inc(s["act_for_dve"], 1)
                c["out"].n += 8

            if stop >= 8:
                norm(1, 1, 1)
                await_("dve_for_act", "fa")
                ac(r_tmp[:, 0:16], r_tmp[:, 0:16], ACT.Exp).then_inc(s["act_for_dve"], 1)
                act.wait_ge(s["most_ready"], 1)
                most = act.value_load(most_i, min_val=0, max_val=L)
                at_start = {n: (x.n, x.i, x.per) for n, x in c.items()}

                def moved(o, width):
                    await_("moved_ready", "moved")
                    ac(o, PS[4 + c["moved"].place(2)][:, 0:width], ACT.Copy).then_inc(s["moved_taken"], 1)

                def gathered(j):
                    for half in range(2):
                        moved(h_own[:, j, half * 4:half * 4 + 4, :].rearrange("p a b -> p (a b)"), 512)
                    moved(back[:, j, :], L)

                with act.If(most <= P):
                    gathered(0)
                    with turns(act, NE // 2, gu=(c["gu"], 12), moved=(c["moved"], 14)):
                        for j in range(2):
                            for q in range(6):
                                nb = 2 if q < 5 else 1
                                await_("gu_ready", "gu")
                                act.wait_ge(s["gu_taken"], c["gu"].ahead(0))
                                pl = c["gu"].place(2)
                                ac(e_silu[:, pl, 0:nb * P], PS[pl][:, 0:nb * P], ACT.Silu).then_inc(s["silu_ready"], 1)
                            gathered(1 - j)
                            for q in range(4):
                                moved(y_own[:, q * L:(q + 1) * L], L)
                for n, x in c.items():
                    x.n, x.i, x.per = at_start[n]
                with act.Else():
                    with turns(act, NE // 2, gu=(c["gu"], 12)):
                        for _ in range(2):
                            for q in range(6):
                                nb = 2 if q < 5 else 1
                                await_("gu_ready", "gu")
                                act.wait_ge(s["gu_taken"], c["gu"].ahead(0))
                                pl = c["gu"].place(2)
                                ac(e_silu[:, pl, 0:nb * L], PS[pl][:, 0:nb * L], ACT.Silu).then_inc(s["silu_ready"], 1)
                c["out"].n += 64
            squares(L, hT)
            root(rstd[:, 0:L])

        @block.gpsimd
        def _(pool):
            if stop >= 7:
                b3 = lambda v: v.unsqueeze(1).to_broadcast([P, 2, P])
                r3 = lambda v: v.rearrange("p (a t) -> p a t", a=2)
                pool.wait_ge(s["phase_loaded"], 48)
                pool.wait_ge(s["pair_ready"], 64 + 8)
                for lev in range(6):
                    for h in range(8):
                        n = lev * 8 + h
                        if n >= 2:
                            m = n - 2
                            pool.wait_ge(s["inv_ready"], 8 + (m // 8) * 16 + m % 8 + 1)
                        nc.gpsimd.tensor_tensor(r3(g_mask[:, n % 2, :]), r3(g_at[:, h, :]), b3(imask(lev + 1)), ALU.mult)\
                            .then_inc(s["blocks_masked"], 1)


def host_constants():
    import numpy as np

    p, f = np.arange(P)[:, None], np.arange(P)[None, :]
    c = np.zeros((P, NCONST), np.float32)

    def put(name, v):
        a, w = CONST[name]
        c[:, a:a + w] = v

    put("ident", p == f)
    put("ones", 1.0)
    put("halves", p // 64 == f // 64)
    rot = np.zeros((P, P))
    for head in range(2):
        for d in range(32):
            rot[head * 64 + d + 32, head * 64 + d] = -1.0
            rot[head * 64 + d, head * 64 + d + 32] = 1.0
    put("rot", rot)
    put("upto", np.where(p <= f, 0.0, NEG))
    put("from", np.where(p >= f, 0.0, NEG))
    put("before", p < f)
    n = HD // 4
    inv = (np.float32(10000.0) ** (-np.arange(n, dtype=np.float32) / np.float32(n))).astype(np.float32)
    t = np.arange(L, dtype=np.float32)
    ang = np.concatenate([np.floor(t / 64)[:, None] * inv, (t % 64)[:, None] * inv], axis=-1).astype(np.float32)
    put("cos", np.tile(np.cos(ang).T, (4, 1)))
    put("sin", np.tile(np.sin(ang).T, (4, 1)))
    r32 = np.zeros((P, 32))
    for d in range(16):
        r32[64 + d + 16, d] = -1.0
        r32[64 + d, d + 16] = 1.0
    put("rot32", r32)
    inv16 = (np.float32(10000.0) ** (-np.arange(16, dtype=np.float32) / np.float32(16))).astype(np.float32)
    put("invf", np.tile(inv16, 8)[:, None])
    e = np.arange(64)
    put("earlier", (e % 8 < e // 8)[None, :])
    a = np.zeros((P, NPHASE_A), np.float32)
    dist = np.arange(STRIP)[None, :] - P - p
    for name, v in (("dist", dist), ("ahead", np.maximum(dist, 0)), ("behind", np.maximum(-dist, 0)),
                    ("is_ahead", dist >= 0), ("is_behind", dist <= 0)):
        o, w = PHASE_A[name]
        a[:, o:o + w] = v
    b = np.zeros((P, 2, T2), np.float32)
    for q in range(2):
        far = np.abs(q * P + p - np.arange(L)[None, :]) > 128
        b[:, q, 0:L] = np.where(far, NEG, 0.0)
    g = np.zeros((P, 8, P), np.float32)
    g[:, 7, :] = f
    for lev in range(7):
        w = 1 << lev
        g[:, lev, :] = (p // (2 * w) == f // (2 * w)) & (p % (2 * w) < w) & (f % (2 * w) >= w)
    return {"consts": c, "phase_a": a, "phase_b": b.reshape(P, 2 * T2), "phase_g": g.reshape(P, 8 * P)}


def kernel(**inputs):
    import numpy as np
    import concourse.bacc as bacc
    from concourse import mybir as mb
    from concourse.bass_utils import run_bass_kernel_spmd

    nc = bacc.Bacc("TRN2", target_bir_lowering=False, num_devices=1)
    arrays, A = {}, {}
    for name, value in {**inputs, **host_constants()}.items():
        a = np.ascontiguousarray(value)
        arrays[f"in_{name}"] = a
        A[name] = nc.dram_tensor(f"in_{name}", a.shape, mb.dt.from_np(a.dtype), kind="ExternalInput").ap()
    out = nc.dram_tensor("out_x", (1, L, D), F32, kind="ExternalOutput").ap()
    build(nc, A, out)
    return run_bass_kernel_spmd(nc, [arrays], core_ids=[0]).results[0]["out_x"]
```
